# Optimizing a Trainium2 kernel written in Bass

```python
import math
import jax
import jax.numpy as jnp
from jax import lax
import numpy as np

D_MODEL = 1024
BATCH = 1
SEQ = 256
DEPTH = 2

CHUNK = 64
EPS = 1e-6
SGU_BLOCK = 128
SGU_GROUPS = 8
SGU_WIDTH = D_MODEL // 2
SGU_GDIM = SGU_WIDTH // SGU_GROUPS
GDN_HEADS = 4
GDN_DK = 128
GDN_DV = 128
GDN_CONV = 4
GDN_QK = GDN_HEADS * GDN_DK
GDN_V = GDN_HEADS * GDN_DV
CONV_CH = 2 * GDN_QK + GDN_V
IN_EVEN = 2 * SGU_WIDTH + CONV_CH + GDN_V + 2 * GDN_HEADS
SPLITS_EVEN = (SGU_WIDTH, 2 * SGU_WIDTH, 2 * SGU_WIDTH + CONV_CH,
               2 * SGU_WIDTH + CONV_CH + GDN_V, 2 * SGU_WIDTH + CONV_CH + GDN_V + GDN_HEADS)
MIX_EVEN = SGU_WIDTH + GDN_V
SB_HEADS = 16
SB_DIM = D_MODEL // SB_HEADS
SB_BLOCK = 128
D_FF = 2816
N_EXPERTS = 8
TOP_K = 2
N_EVEN = (DEPTH + 1) // 2
N_ODD = DEPTH // 2

kernel_name = 'hybrid_sgu_gdn_stickbreak_moe_trunk'

def rmsnorm(x, g):
    xf = x.astype(jnp.float32)
    y = xf * lax.rsqrt(jnp.mean(xf * xf, axis=-1, keepdims=True) + EPS)
    return (y * g.astype(jnp.float32)).astype(x.dtype)

def layernorm(x, g, b):
    xf = x.astype(jnp.float32)
    mu = jnp.mean(xf, axis=-1, keepdims=True)
    var = jnp.mean(jnp.square(xf - mu), axis=-1, keepdims=True)
    y = (xf - mu) * lax.rsqrt(var + EPS)
    return (y * g.astype(jnp.float32) + b.astype(jnp.float32)).astype(x.dtype)

def l2norm(x):
    xf = x.astype(jnp.float32)
    return xf * lax.rsqrt(jnp.sum(xf * xf, axis=-1, keepdims=True) + EPS)

def swiglu(x, w1, w3, w2):
    return (jax.nn.silu(x @ w1) * (x @ w3)) @ w2

def causal_conv(x, w):
    K = w.shape[0]
    S = x.shape[1]
    xp = jnp.pad(x, ((0, 0), (K - 1, 0), (0, 0)))
    return sum(xp[:, i:i + S] * w[i] for i in range(K))

def spatial_gating(u_pre, v_pre, ln_g, ln_b, w_s, b_s):
    B, S, _ = u_pre.shape
    u = jax.nn.gelu(u_pre)
    v = layernorm(jax.nn.gelu(v_pre), ln_g, ln_b)
    nb = S // SGU_BLOCK
    v = v.reshape(B, nb, SGU_BLOCK, SGU_GROUPS, SGU_GDIM)
    pos_chunk = jnp.arange(SGU_BLOCK) // CHUNK
    mask = pos_chunk[None, :] <= pos_chunk[:, None]
    w = jnp.where(mask[None], w_s, 0.0).astype(v.dtype)
    mixed = jnp.einsum('gts,bnsgc->bntgc', w, v) + b_s.T[None, None, :, :, None].astype(v.dtype)
    return u * mixed.reshape(B, S, SGU_WIDTH)

def chunk_gated_delta(q, k, v, beta, g):
    B, S, H, dk = q.shape
    dv = v.shape[-1]
    N, C = S // CHUNK, CHUNK

    def blk(t):
        return jnp.moveaxis(t.reshape((B, N, C, H) + t.shape[3:]), 3, 1)

    q, k, v, beta, g = blk(q), blk(k), blk(v), blk(beta), blk(g)
    gc = jnp.cumsum(g, axis=-1)
    idx = jnp.arange(C)
    causal = idx[:, None] >= idx[None, :]
    strict = idx[:, None] > idx[None, :]
    gamma = jnp.exp(jnp.where(causal, gc[..., :, None] - gc[..., None, :], -jnp.inf))
    kb = k * beta[..., None]
    L = jnp.where(strict, jnp.einsum('bhnid,bhnjd->bhnij', kb, k) * gamma, 0.0)
    rhs = jnp.concatenate([v * beta[..., None], kb * jnp.exp(gc)[..., None]], axis=-1)
    sol = lax.linalg.triangular_solve(jnp.eye(C, dtype=L.dtype) + L, rhs,
                                      left_side=True, lower=True, unit_diagonal=True)
    U, W = sol[..., :dv], sol[..., dv:]
    attn = jnp.einsum('bhnid,bhnjd->bhnij', q, k) * gamma
    q_dec = q * jnp.exp(gc)[..., None]
    g_last = gc[..., -1]
    k_dec = k * jnp.exp(g_last[..., None] - gc)[..., None]

    def step(state, xs):
        qd, kd, u, w, a, gl = xs
        v_new = u - jnp.einsum('bhcd,bhde->bhce', w, state)
        o = jnp.einsum('bhcd,bhde->bhce', qd, state) + jnp.einsum('bhij,bhje->bhie', a, v_new)
        state = state * jnp.exp(gl)[..., None, None] + jnp.einsum('bhcd,bhce->bhde', kd, v_new)
        return state, o

    xs = tuple(jnp.moveaxis(t, 2, 0) for t in (q_dec, k_dec, U, W, attn, g_last))
    state0 = jnp.zeros((B, H, dk, dv), jnp.float32)
    _, o = lax.scan(step, state0, xs)
    o = jnp.moveaxis(o, 0, 2)
    return o.transpose(0, 2, 3, 1, 4).reshape(B, S, H, dv)

def gated_deltanet(qkv_pre, gate_pre, b_pre, a_pre, conv_w, a_log, dt_bias, o_norm):
    B, S, _ = qkv_pre.shape
    qkv = jax.nn.silu(causal_conv(qkv_pre, conv_w))
    q, k, v = jnp.split(qkv, [GDN_QK, 2 * GDN_QK], axis=-1)
    q = l2norm(q.reshape(B, S, GDN_HEADS, GDN_DK)) * (GDN_DK ** -0.5)
    k = l2norm(k.reshape(B, S, GDN_HEADS, GDN_DK))
    v = v.reshape(B, S, GDN_HEADS, GDN_DV).astype(jnp.float32)
    beta = jax.nn.sigmoid(b_pre.astype(jnp.float32))
    g = -jnp.exp(a_log.astype(jnp.float32)) * jax.nn.softplus(a_pre.astype(jnp.float32) + dt_bias.astype(jnp.float32))
    o = chunk_gated_delta(q, k, v, beta, g)
    o = rmsnorm(o, o_norm) * jax.nn.silu(gate_pre.astype(jnp.float32).reshape(B, S, GDN_HEADS, GDN_DV))
    return o.reshape(B, S, GDN_V).astype(qkv_pre.dtype)

def even_mixer(xn, w_in, sgu_ln_g, sgu_ln_b, sgu_w, sgu_b, conv_w, a_log, dt_bias, o_norm, w_out):
    z = xn @ w_in
    u_pre, v_pre, qkv_pre, gate_pre, b_pre, a_pre = jnp.split(z, SPLITS_EVEN, axis=-1)
    y_a = spatial_gating(u_pre, v_pre, sgu_ln_g, sgu_ln_b, sgu_w, sgu_b)
    y_b = gated_deltanet(qkv_pre, gate_pre, b_pre, a_pre, conv_w, a_log, dt_bias, o_norm)
    return jnp.concatenate([y_a, y_b], axis=-1) @ w_out

def stick_breaking_mixer(xn, w_qkv, w_out):
    B, S, _ = xn.shape
    q, k, v = jnp.split(xn @ w_qkv, 3, axis=-1)

    def heads(t):
        return t.reshape(B, S, SB_HEADS, SB_DIM).transpose(0, 2, 1, 3)

    q, k, v = heads(q), heads(k), heads(v)
    scale = SB_DIM ** -0.5
    outs = []
    for qb in range(S // SB_BLOCK):
        kn = (qb + 1) * SB_BLOCK
        qi = q[:, :, qb * SB_BLOCK:kn]
        z = jnp.einsum('bhtd,bhsd->bhts', qi, k[:, :, :kn]).astype(jnp.float32) * scale
        t_pos = qb * SB_BLOCK + jnp.arange(SB_BLOCK)
        s_pos = jnp.arange(kn)
        mask = s_pos[None, :] < t_pos[:, None]
        log_keep = jnp.where(mask, jax.nn.log_sigmoid(-z), 0.0)
        after = lax.cumsum(log_keep, axis=3, reverse=True) - log_keep
        att = jnp.where(mask, jnp.exp(jax.nn.log_sigmoid(z) + after), 0.0)
        outs.append(jnp.einsum('bhts,bhsd->bhtd', att.astype(v.dtype), v[:, :, :kn]))
    o = jnp.concatenate(outs, axis=2).transpose(0, 2, 1, 3).reshape(B, S, D_MODEL)
    return o @ w_out

def moe_swiglu(xn, w_router, w1, w3, w2):
    B, S, D = xn.shape
    xf = xn.reshape(-1, D)
    logits = (xf @ w_router).astype(jnp.float32)
    vals, idx = lax.top_k(logits, TOP_K)
    gates = jax.nn.softmax(vals, axis=-1)
    combine = jnp.sum(jax.nn.one_hot(idx, N_EXPERTS, dtype=jnp.float32) * gates[..., None], axis=1)
    y = jnp.zeros_like(xf)
    for e in range(N_EXPERTS):
        y = y + combine[:, e:e + 1].astype(xf.dtype) * swiglu(xf, w1[e], w3[e], w2[e])
    return y.reshape(B, S, D)

def setup_inputs(seed: int = 0) -> dict:
    key = jax.random.key(seed)
    ks = iter(jax.random.split(key, 32))
    D = D_MODEL

    def nrm(shape, scale):
        return scale * jax.random.normal(next(ks), shape, jnp.float32)

    def gain(shape):
        return 1.0 + 0.05 * jax.random.normal(next(ks), shape, jnp.float32)

    x = nrm((BATCH, SEQ, D), 1.0)
    e_norm1 = gain((N_EVEN, D))
    e_w_in = nrm((N_EVEN, D, IN_EVEN), D ** -0.5)
    e_sgu_ln_g = gain((N_EVEN, SGU_WIDTH))
    e_sgu_ln_b = nrm((N_EVEN, SGU_WIDTH), 0.02)
    e_sgu_w = nrm((N_EVEN, SGU_GROUPS, SGU_BLOCK, SGU_BLOCK), SGU_BLOCK ** -0.5)
    e_sgu_b = gain((N_EVEN, SGU_GROUPS, SGU_BLOCK))
    e_conv_w = nrm((N_EVEN, GDN_CONV, CONV_CH), GDN_CONV ** -0.5)
    e_a_log = jnp.log(jax.random.uniform(next(ks), (N_EVEN, GDN_HEADS), jnp.float32, 1.0, 16.0))
    dt = jnp.exp(jax.random.uniform(next(ks), (N_EVEN, GDN_HEADS), jnp.float32,
                                    math.log(1e-3), math.log(1e-1)))
    e_dt_bias = dt + jnp.log(-jnp.expm1(-dt))
    e_o_norm = gain((N_EVEN, GDN_DV))
    e_w_out = nrm((N_EVEN, MIX_EVEN, D), MIX_EVEN ** -0.5)
    e_norm2 = gain((N_EVEN, D))
    e_ffn_w1 = nrm((N_EVEN, D, D_FF), D ** -0.5)
    e_ffn_w3 = nrm((N_EVEN, D, D_FF), D ** -0.5)
    e_ffn_w2 = nrm((N_EVEN, D_FF, D), D_FF ** -0.5)
    o_norm1 = gain((N_ODD, D))
    o_w_qkv = nrm((N_ODD, D, 3 * D), D ** -0.5)
    o_w_out = nrm((N_ODD, D, D), D ** -0.5)
    o_norm2 = gain((N_ODD, D))
    o_router = nrm((N_ODD, D, N_EXPERTS), D ** -0.5)
    o_moe_w1 = nrm((N_ODD, N_EXPERTS, D, D_FF), D ** -0.5)
    o_moe_w3 = nrm((N_ODD, N_EXPERTS, D, D_FF), D ** -0.5)
    o_moe_w2 = nrm((N_ODD, N_EXPERTS, D_FF, D), D_FF ** -0.5)
    final_norm = gain((D,))
    return {'x': x, 'e_norm1': e_norm1, 'e_w_in': e_w_in, 'e_sgu_ln_g': e_sgu_ln_g,
            'e_sgu_ln_b': e_sgu_ln_b, 'e_sgu_w': e_sgu_w, 'e_sgu_b': e_sgu_b, 'e_conv_w': e_conv_w,
            'e_a_log': e_a_log, 'e_dt_bias': e_dt_bias, 'e_o_norm': e_o_norm, 'e_w_out': e_w_out,
            'e_norm2': e_norm2, 'e_ffn_w1': e_ffn_w1, 'e_ffn_w3': e_ffn_w3, 'e_ffn_w2': e_ffn_w2,
            'o_norm1': o_norm1, 'o_w_qkv': o_w_qkv, 'o_w_out': o_w_out, 'o_norm2': o_norm2,
            'o_router': o_router, 'o_moe_w1': o_moe_w1, 'o_moe_w3': o_moe_w3, 'o_moe_w2': o_moe_w2,
            'final_norm': final_norm}

def reference(x, e_norm1, e_w_in, e_sgu_ln_g, e_sgu_ln_b, e_sgu_w, e_sgu_b, e_conv_w, e_a_log,
              e_dt_bias, e_o_norm, e_w_out, e_norm2, e_ffn_w1, e_ffn_w3, e_ffn_w2, o_norm1, o_w_qkv,
              o_w_out, o_norm2, o_router, o_moe_w1, o_moe_w3, o_moe_w2, final_norm):
    h = x
    for layer in range(DEPTH):
        i = layer // 2
        if layer % 2 == 0:
            h = h + even_mixer(rmsnorm(h, e_norm1[i]), e_w_in[i], e_sgu_ln_g[i], e_sgu_ln_b[i],
                               e_sgu_w[i], e_sgu_b[i], e_conv_w[i], e_a_log[i], e_dt_bias[i],
                               e_o_norm[i], e_w_out[i])
            h = h + swiglu(rmsnorm(h, e_norm2[i]), e_ffn_w1[i], e_ffn_w3[i], e_ffn_w2[i])
        else:
            h = h + stick_breaking_mixer(rmsnorm(h, o_norm1[i]), o_w_qkv[i], o_w_out[i])
            h = h + moe_swiglu(rmsnorm(h, o_norm2[i]), o_router[i], o_moe_w1[i], o_moe_w3[i], o_moe_w2[i])
    return rmsnorm(h, final_norm)


_drawn_inputs = setup_inputs


def setup_inputs(seed=0):
    import zlib

    import numpy as np

    out = dict(_drawn_inputs(seed))
    spreads = {}
    factors = {'e_sgu_ln_b': 4.815}
    for name, (base, spread) in spreads.items():
        noise = np.random.default_rng([zlib.crc32(name.encode()), seed]).standard_normal(out[name].shape)
        drawn = base * np.exp(spread * noise) if base else spread * noise
        out[name] = jnp.asarray(drawn.astype(out[name].dtype))
    for name, factor in factors.items():
        out[name] = (out[name] * factor).astype(out[name].dtype)
    return out
```

```python
import math
from contextlib import ExitStack

import concourse.bass as bass
from concourse import mybir

F32 = mybir.dt.float32
I32 = mybir.dt.int32
ALU = mybir.AluOpType
ACT = mybir.ActivationFunctionType
AX = mybir.AxisListType

P = 128
EPS = 1e-6
EXP_LN = "natural_log_exp_and_others"


def trunk(nc, x, e_norm1, e_w_in, e_sgu_ln_g, e_sgu_ln_b, e_sgu_w, e_sgu_b, e_conv_w, e_a_log,
          e_dt_bias, e_o_norm, e_w_out, e_norm2, e_ffn_w1, e_ffn_w3, e_ffn_w2, o_norm1, o_w_qkv,
          o_w_out, o_norm2, o_router, o_moe_w1, o_moe_w3, o_moe_w2, final_norm, out):
    SEQ, D = x.shape[1], x.shape[2]
    TILES, DC = SEQ // P, D // P
    SGU_W = e_sgu_ln_g.shape[1]
    G = e_sgu_w.shape[1]
    GD = SGU_W // G
    H = e_a_log.shape[1]
    DK = e_o_norm.shape[1]
    KCONV = e_conv_w.shape[1]
    CONV_C = e_conv_w.shape[2] // P
    CH = 64
    NCH = SEQ // CH
    U = H * TILES
    SB_H, SB_D = 16, 64
    FF = e_ffn_w1.shape[2]
    FC = FF // P
    NE = o_router.shape[2]
    CW = 256
    SLOTS = 96
    NB = 3
    NK = NB * NE
    assert TILES == 2 and DC == 8 and DK == P and U == 8 and SLOTS * NB >= SEQ and FC == 22
    LEVELS = 6
    assert 2 ** LEVELS == CH
    QKV0, GATE0, BA0 = 2 * SGU_W, 2 * SGU_W + CONV_C * P, e_w_in.shape[2] - 2 * H

    RA = 11
    RB = 11
    PER_FFN = 2 * FC // 2

    def cols(w, c0):
        return w[:, c0:c0 + CW].rearrange("(c p) n -> p c n", p=P)

    w_in_cols = [QKV0 + CW * i for i in range(6)] + [GATE0, GATE0 + CW] + [0, CW] + [SGU_W, SGU_W + CW]
    N_IN, N_OUT, N_QKV = 12, D // CW, 3 * D // CW
    A_OUT, A_FFN = N_IN, N_IN + N_OUT
    A_QKV = A_FFN + PER_FFN
    A_WO = A_QKV + N_QKV
    A_MOE = A_WO + N_OUT
    assert PER_FFN % RA == 0 and FC % RB == 0

    def a_piece(i):
        if i < A_OUT:
            return cols(e_w_in[0], w_in_cols[i])
        if i < A_FFN:
            return cols(e_w_out[0], CW * (i - A_OUT))
        if i < A_QKV:
            w = (e_ffn_w1, e_ffn_w3)[(i - A_FFN) % 2]
            return cols(w[0], CW * ((i - A_FFN) // 2))
        if i < A_WO:
            return cols(o_w_qkv[0], CW * (i - A_QKV))
        return cols(o_w_out[0], CW * (i - A_WO))

    with ExitStack() as ctx:
        def sb(name, shape, dt=F32, stack=ctx):
            return stack.enter_context(nc.sbuf_tensor(name, shape, dt))

        def sem(name):
            return ctx.enter_context(nc.semaphore(name))

        ring_a = sb("ring_a", [P, RA, DC, CW])
        h = sb("h", [P, TILES, D])
        xn = sb("xn", [P, TILES, D])
        xT = sb("xT", [P, DC, SEQ])
        gain = sb("gain", [P, 2, D])
        ident = sb("ident", [P, P])
        ones = sb("ones", [P, P])
        neg_ones = sb("neg_ones", [P, P])
        tri_blk = sb("tri_blk", [P, P])
        blk_ones = sb("blk_ones", [P, P])
        before = sb("before", [P, P])
        neg_after = sb("neg_after", [P, P])
        level = sb("level", [P, LEVELS, P])
        iota = sb("iota", [P, P])
        colt = sb("colt", [P, P])
        stat = sb("stat", [P, 5, 6])
        small = sb("small", [P, 16, TILES, H])
        ba = sb("ba", [P, TILES, 2 * H])
        w_ba = sb("w_ba", [P, DC, 2 * H])
        const = sb("const", [P, 4])
        eps_col, one_col, qscale_col = const[:, 0:1], const[:, 1:2], const[:, 2:3]
        bn = sb("bn", [P, TILES, 6])
        mv = sb("mv", [P, TILES, 2])
        stat_ln = sb("stat_ln", [P, 2, TILES])
        r_small = sb("r_small", [P, 6, TILES])

        even = ExitStack()
        conv_in = sb("conv_in", [P, CONV_C, KCONV - 1 + SEQ], stack=even)
        qkvT = sb("qkvT", [P, CONV_C, SEQ], stack=even)
        yT = sb("yT", [P, DC, SEQ], stack=even)
        v_nat = sb("v_nat", [P, TILES, SGU_W], stack=even)
        wsT = sb("wsT", [P, G, P], stack=even)
        sgu_bias = sb("sgu_bias", [P, G // 2, P], stack=even)
        exp_row = sb("exp_row", [P, H, TILES, P], stack=even)
        kbT = sb("kbT", [P, H, SEQ], stack=even)
        gam = sb("gam", [P, U, P], stack=even)
        attnT = sb("attnT", [P, U, P], stack=even)
        kd = sb("kd", [P, U, P], stack=even)
        rn = sb("rn", [P, 2 * H, SEQ], stack=even)
        state = sb("state", [P, H, P], stack=even)
        even.close()
        ws_raw = gam
        rows_raw = kd[:, 0, :]
        inv = conv_in[:, :, :].rearrange("p a b -> p (a b)")[:, 0:3 * U * P].rearrange(
            "p (k u n) -> p k u n", k=3, u=U)
        inv_x, inv_xt, inv_t = inv[:, 0], inv[:, 1], inv[:, 2]
        vb = xn[:, 0, :].rearrange("p (u n) -> p u n", u=U)
        kbe = xn[:, 1, :].rearrange("p (u n) -> p u n", u=U)
        u_sol = rn[:, 0:H, :].rearrange("p h (t n) -> p (h t) n", t=TILES)
        w_solT = rn[:, H:2 * H, :].rearrange("p h (t n) -> p (h t) n", t=TILES)
        v_new = kbT[:, :, :].rearrange("p a b -> p (a b)").rearrange("p (t n) -> p t n", t=TILES)
        oT = qkvT[:, 2 * H:3 * H, :]
        ln_g, ln_b = gain[:, 1, 0:SGU_W], gain[:, 1, SGU_W:2 * SGU_W]

        ring_b = sb("ring_b", [P, RB, D])
        silu_s = sb("silu_s", [P, 2, SEQ])
        hT = sb("hT", [P, 2, SEQ])
        w_router = sb("w_router", [P, DC, NE])
        odd = ExitStack()
        qT = sb("qT", [P, DC, SEQ], stack=odd)
        kT = sb("kT", [P, DC, SEQ], stack=odd)
        NZ = 384
        lg = sb("lg", [P, 2, NZ], stack=odd)
        sp_m = sb("sp_m", [P, 2, NZ], stack=odd)
        w_log = sb("w_log", [P, 3, NZ], stack=odd)
        att = sb("att", [P, 2, NZ], stack=odd)
        odd.close()
        v_att = xn
        o_attT = xT
        sel_p = sb("sel_p", [P, TILES, SLOTS])
        sel_w = sb("sel_w", [P, TILES, SLOTS])
        back = sb("back", [SLOTS, TILES, P])
        xgT = sb("xgT", [P, DC, SLOTS])
        y_exp = sb("y_exp", [SLOTS, D])
        logits = sb("logits", [P, TILES, NE])
        rt = sb("rt", [P, 6, TILES * NE, NE])
        r2 = sb("r2", [P, 12, TILES, NE])
        table = sb("table", [P, 3, TILES, NK])
        col6 = sb("col6", [P, 3, TILES, 1])
        li = sb("li", [1, 6, 16])
        li3 = sb("li3", [1, 2, 8, 16])
        item_f = sb("item_f", [1, 3, 8])
        item_i = sb("item_i", [1, 3, 8], I32)

        ps = ctx.enter_context(nc.psum_tensor("ps", [P, 8, 512], F32))

        def two(b):
            return ps[:, b:b + 2, :].rearrange("p b n -> p (b n)")

        ld_x, ld_ba, ld_small, ld_rows, ld_ws, ld_lng, ld_bias, ld_wr = (
            sem(n) for n in ("ld_x", "ld_ba", "ld_small", "ld_rows", "ld_ws", "ld_lng", "ld_bias", "ld_wr"))
        ld_gain = [sem("ld_gain0"), sem("ld_gain1")]
        a_in = [sem(f"a_in{i}") for i in range(RA)]
        b_in = [sem(f"b_in{i}") for i in range(RB)]
        pool_own, act_own, vec_own = sem("pool_own"), sem("act_own"), sem("vec_own")
        consts_ready, pads_ready, ws_zero = sem("consts_ready"), sem("pads_ready"), sem("ws_zero")
        h_ready, rinv_ready, xn_ready, xnT_done = sem("h_ready"), sem("rinv_ready"), sem("xn_ready"), sem("xnT_done")
        xT_act, xT_vec = sem("xT_act"), sem("xT_vec")
        proj_done, act_evac, vec_evac = sem("proj_done"), sem("act_evac"), sem("vec_evac")
        rows_done, colt_ready, ba_done = sem("rows_done"), sem("colt_ready"), sem("ba_done")
        wsT_done, wsT_ready = sem("wsT_done"), sem("wsT_ready")
        ba_sb, gb_act, gb_vec, g_ready = sem("ba_sb"), sem("gb_act"), sem("gb_vec"), sem("g_ready")
        conv_done, silu_even = sem("conv_done"), sem("silu_even")
        gc_done, gc_sb, row_done, exp_row_ready = sem("gc_done"), sem("gc_sb"), sem("row_done"), sem("exp_row_ready")
        gcols_act, kbe_scale = sem("gcols_act"), sem("kbe_scale")
        sq_ready, l2_done, rn_ready, qk_ready = sem("sq_ready"), sem("l2_done"), sem("rn_ready"), sem("qk_ready")
        kb_ready, gam_arg, gam_exp, kk_done, attn_ready, lt_ready = (
            sem(n) for n in ("kb_ready", "gam_arg", "gam_exp", "kk_done", "attn_ready", "lt_ready"))
        qd_ready, turn_done, vb_ready, kbe_ready, kd_ready = (
            sem(n) for n in ("qd_ready", "turn_done", "vb_ready", "kbe_ready", "kd_ready"))
        t_done, t_ready, x_done, x_ready, xt_done, xt_ready = (
            sem(n) for n in ("t_done", "t_ready", "x_done", "x_ready", "xt_done", "xt_ready"))
        sol_done, sol_u, sol_w = sem("sol_done"), sem("sol_u"), sem("sol_w")
        ws_done, vnew_ready, o_done, o_sb, st_done, st_ready = (
            sem(n) for n in ("ws_done", "vnew_ready", "o_done", "o_sb", "st_done", "st_ready"))
        osq_ready, on_done, on_ready, yb_ready = sem("osq_ready"), sem("on_done"), sem("on_ready"), sem("yb_ready")
        gelu_v, ln_var, ln_rstd, v_ready, mix_done, ya_ready = (
            sem(n) for n in ("gelu_v", "ln_var", "ln_rstd", "v_ready", "mix_done", "ya_ready"))
        up_done, silu_done, hT_ready, down_done = sem("up_done"), sem("silu_done"), sem("hT_ready"), sem("down_done")
        z_done, log_ready, sp_ready, w_ready, spm_ready = (
            sem(n) for n in ("z_done", "log_ready", "sp_ready", "w_ready", "spm_ready"))
        after_done, la_ready, att_exp, att_ready, oh_done, oh_ready = (
            sem(n) for n in ("after_done", "la_ready", "att_exp", "att_ready", "oh_done", "oh_ready"))
        lgt_done, r_exp, r_d, sel_ready, pos_done, table_ready, items_ready = (
            sem(n) for n in ("lgt_done", "r_exp", "r_d", "sel_ready", "pos_done", "table_ready", "items_ready"))
        prep_col, prep_done, gather_done, xg_act, xg_vec, back_act, back_vec = (
            sem(n) for n in ("prep_col", "prep_done", "gather_done", "xg_act", "xg_vec", "back_act", "back_vec"))
        y_act, y_vec, scat_done, scat_added = sem("y_act"), sem("y_vec"), sem("scat_done"), sem("scat_added")
        out_ready, out_sem = sem("out_ready"), sem("out_sem")

        block = ctx.enter_context(nc.Block())

        def a_slot(i):
            return ring_a[:, i % RA]

        def a_arrived(eng, i):
            eng.wait_ge(a_in[i % RA], 16 * (i // RA + 1))

        @block.sync
        def _(sp):
            sp.dma_start(h[:, :, :], x[0].rearrange("(t p) d -> p t d", p=P)).then_inc(ld_x, 16)

            def load_a(i):
                if i >= RA and (i - RA < A_FFN or i - RA >= A_QKV):
                    sp.wait_ge(proj_done, i - RA + 1 - (PER_FFN if i - RA >= A_QKV else 0))
                elif i >= RA:
                    sp.wait_ge(up_done, 2 * ((i - RA - A_FFN) // 2) + 2)
                sp.dma_start(a_slot(i), a_piece(i)).then_inc(a_in[i % RA], 16)

            for i in range(A_FFN):
                load_a(i)
            for g in range(FC // 2):
                load_a(A_FFN + 2 * g)
                load_a(A_FFN + 2 * g + 1)
                for j in (2 * g, 2 * g + 1):
                    if g == 0 and j == 0:
                        sp.wait_ge(proj_done, A_FFN)
                    if j >= RB:
                        sp.wait_ge(down_done, j - RB + 1)
                    sp.dma_start(ring_b[:, j % RB, :], e_ffn_w2[0, j * P:(j + 1) * P, :]).then_inc(b_in[j % RB], 16)
            for i in range(A_QKV, A_MOE):
                load_a(i)

            def load_item(n, e, first):
                for g in range(FC // 2):
                    for m, w in enumerate((o_moe_w1, o_moe_w3)):
                        p = 2 * g + m
                        src = w[0][bass.ds(e, 1), :, g * CW:(g + 1) * CW].rearrange("e (c p) n -> p (e c) n", p=P)
                        q = p - RA
                        need = sp.snap(n * FC + (2 * (q // 2) + 2 + FC))
                        if q < 0 and first:
                            sp.wait_ge(proj_done, A_MOE + q + 1 - PER_FFN)
                        sp.wait_ge(up_done, need)
                        sp.dma_start(a_slot(A_MOE + p), src).then_inc(a_in[(A_MOE + p) % RA], 16)
                    for j in (2 * g, 2 * g + 1):
                        src = o_moe_w2[0][bass.ds(e, 1), j * P:(j + 1) * P, :].rearrange("e p d -> p (e d)")
                        need = sp.snap(n * FC + (FC + j - RB + 1))
                        sp.wait_ge(down_done, need)
                        sp.dma_start(ring_b[:, j % RB, :], src).then_inc(b_in[j % RB], 16)

            with sp.Fori(0, NE) as e:
                load_item(e, e, True)
            sp.wait_ge(items_ready, 1)
            n_more = sp.value_load(item_i[0:1, 0, 0:1], min_val=0, max_val=7)
            with sp.If(n_more > 0):
                with sp.Fori(0, n_more) as it:
                    e = sp.value_load(item_i[0:1, 2, bass.ds(it, 1)], min_val=0, max_val=NE - 1)
                    load_item(it + NE, e, False)
            for t in range(TILES):
                sp.wait_ge(out_ready, t + 1)
                sp.dma_start(out[0, t * P:(t + 1) * P, :], xn[:, t, :]).then_inc(out_sem, 16)
            sp.wait_ge(out_sem, 16 * TILES)

        @block.gpsimd
        def _(pool):
            own = [0]

            def after(ins):
                own[0] += 1
                ins.then_inc(pool_own, 1)
                pool.wait_ge(pool_own, own[0])

            def keep(t, pattern, base, cm, op=ALU.is_ge, fill=0.0):
                after(pool.affine_select(out=t, in_=t, pattern=pattern, compare_op=op, fill=fill, base=base,
                                         channel_multiplier=cm))

            def gain_load(k, g):
                if k >= 2:
                    pool.wait_ge(xn_ready, TILES * (k - 1))
                if k == 1:
                    pool.wait_ge(v_ready, TILES)
                pool.dma_start(gain[:, k % 2, :], g.partition_broadcast(P)).then_inc(ld_gain[k % 2], 16)

            gain_load(0, e_norm1[0])
            pool.dma_start(w_ba[:, :, :], e_w_in[0][:, BA0:BA0 + 2 * H].rearrange("(c p) n -> p c n", p=P)).then_inc(ld_ba, 16)
            pool.dma_start(rows_raw[0:KCONV * CONV_C, :], e_conv_w[0].rearrange("k (c p) -> (k c) p", p=P)).then_inc(ld_rows, 16)
            pool.dma_start(rows_raw[KCONV * CONV_C:KCONV * CONV_C + 1, :], e_o_norm).then_inc(ld_rows, 16)
            pool.dma_start(small[:, 0, 0, :], e_dt_bias[0].partition_broadcast(P)).then_inc(ld_small, 16)
            pool.dma_start(small[:, 0, 1, :], e_a_log[0].partition_broadcast(P)).then_inc(ld_small, 16)
            after(pool.memset(ident[:, :], 0.0))
            keep(ident[:, :], [[-1, P]], 0, 1, ALU.not_equal, 1.0)
            pool.memset(conv_in[:, :, 0:KCONV - 1], 0.0).then_inc(pads_ready, 1)
            pool.memset(ones[:, :], 1.0)
            pool.memset(neg_ones[:, :], -1.0)
            after(pool.memset(before[:, :], 1.0))
            keep(before[:, :], [[1, P]], -1, -1)
            after(pool.memset(neg_after[:, :], -1.0))
            keep(neg_after[:, :], [[-1, P]], -1, 1)
            after(pool.memset(blk_ones[:, :], 1.0))
            halves = blk_ones[:, :].rearrange("p (a n) -> p a n", n=CH)
            keep(halves, [[-CH, P // CH], [0, CH]], 0, 1)
            keep(halves, [[CH, P // CH], [0, CH]], CH - 1, -1)
            after(pool.affine_select(out=tri_blk[:, :], in_=blk_ones[:, :], pattern=[[1, P]], compare_op=ALU.is_ge,
                                     fill=0.0, base=0, channel_multiplier=-1))
            after(pool.memset(level[:, :, :], 0.0))
            for k in range(LEVELS):
                b = 2 ** k
                v = level[:, k, :].rearrange("p (a n) -> p a n", n=2 * b)[:, :, 0:b]
                after(pool.memset(v, 1.0))
                keep(v, [[-2 * b, P // (2 * b)], [0, b]], -b, 1)
                keep(v, [[2 * b, P // (2 * b)], [0, b]], 2 * b - 1, -1)
            pool.iota(iota[:, :], [[1, P]], base=0, channel_multiplier=0,
                      allow_small_or_imprecise_dtypes=True).then_inc(pool_own, 1)
            own[0] += 1
            after(pool.memset(ws_raw[0:CH, :, CH:P], 0.0))
            pool.drain().then_inc(consts_ready, 1)
            w = e_sgu_w[0].rearrange("g t s -> t g s")
            pool.dma_start(ws_raw[0:CH, :, 0:CH], w[0:CH, :, 0:CH]).then_inc(ld_ws, 16)
            pool.dma_start(ws_raw[CH:P, :, :], w[CH:P]).then_inc(ld_ws, 16)
            pool.dma_start(ln_g, e_sgu_ln_g[0].partition_broadcast(P)).then_inc(ld_lng, 16)
            pool.dma_start(ln_b, e_sgu_ln_b[0].partition_broadcast(P)).then_inc(ld_lng, 16)
            for m in range(2):
                b = e_sgu_b[0].rearrange("(c m) t -> m c t", m=2)[m].partition_broadcast(CH)
                pool.dma_start(sgu_bias[m * CH:(m + 1) * CH, :, :], b).then_inc(ld_bias, 16)
            gain_load(1, e_norm2[0])
            gain_load(2, o_norm1[0])
            gain_load(3, o_norm2[0])
            pool.wait_ge(proj_done, A_FFN)
            pool.dma_start(w_router[:, :, :], o_router[0].rearrange("(c p) e -> p c e", p=P)).then_inc(ld_wr, 16)
            mask2 = before[:, :].unsqueeze(1).to_broadcast([P, 2, P])

            def diag(t):
                return t[:, 0:2 * P].rearrange("p (a n) -> p a n", a=2)

            def mask_sp(i):
                pool.wait_ge(sp_ready, i + 1)
                pool.tensor_tensor(diag(sp_m[:, i % 2]), diag(sp_m[:, i % 2]), mask2, ALU.mult).then_inc(spm_ready, 1)

            def mask_att(i):
                pool.wait_ge(att_exp, i + 1)
                pool.tensor_tensor(diag(att[:, i % 2]), diag(att[:, i % 2]), mask2, ALU.mult).then_inc(att_ready, 1)

            for i in range(SB_H + 1):
                if i < SB_H:
                    mask_sp(i)
                if i >= 1:
                    mask_att(i - 1)
            gain_load(4, final_norm)

        @block.scalar
        def _(act):
            own = [0]

            def after(ins):
                own[0] += 1
                ins.then_inc(act_own, 1)
                act.wait_ge(act_own, own[0])

            def norm(k, transposed=True):
                for t in range(TILES):
                    if k:
                        act.wait_ge(h_ready, k)
                    else:
                        act.wait_ge(ld_x, 16)
                    after(act.activation(xn[:, t, :], h[:, t, :], ACT.Square, accum_out=stat[:, k, t:t + 1]))
                after(act.activation(stat[:, k, 2:4], stat[:, k, 0:2], ACT.Ln, scale=1.0 / D, bias=eps_col))
                act.activation(stat[:, k, 4:6], stat[:, k, 2:4], ACT.Exp, scale=-0.5).then_inc(rinv_ready, 1)
                if transposed:
                    for b in (1, 3):
                        act.wait_ge(xnT_done, 4 * k + b + 1)
                        act.activation(xT[:, 2 * b:2 * b + 2, :], ps[:, b, :].rearrange("p (c n) -> p c n", c=2),
                                       ACT.Copy).then_inc(xT_act, 1)

            act.wait_ge(vec_own, 1)
            act.preload_act_table_set(EXP_LN)
            norm(0)
            act.wait_ge(ba_sb, 1)
            act.activation(small[:, 1], ba[:, :, 0:H], ACT.Exp, scale=-1.0).then_inc(gb_act, 1)
            act.wait_ge(ld_small, 32)
            act.activation(small[:, 2, 0, :], small[:, 0, 1, :], ACT.Exp).then_inc(gb_act, 1)
            act.wait_ge(gb_vec, 1)
            after(act.activation(small[:, 5], small[:, 4], ACT.Exp, scale=-1.0))
            act.activation(small[:, 6], small[:, 5], ACT.Ln, bias=one_col).then_inc(gb_act, 1)

            act.preload_act_table(ACT.Silu)
            def copy_conv(i):
                act.wait_ge(proj_done, i + 1)
                if i == 0:
                    act.wait_ge(pads_ready, 1)
                act.activation(conv_in[:, 2 * i:2 * i + 2, KCONV - 1:], ps[:, i % 4, :].rearrange("p (c n) -> p c n", c=2),
                               ACT.Copy).then_inc(act_evac, 1)

            def silu_conv(i):
                act.wait_ge(conv_done, i + 1)
                act.activation(qkvT[:, 2 * i:2 * i + 2, :], qkvT[:, 2 * i:2 * i + 2, :], ACT.Silu).then_inc(silu_even, 1)

            for i in range(6):
                copy_conv(i)
                if i >= 1:
                    silu_conv(i - 1)
            silu_conv(5)
            for i in (6, 7):
                act.wait_ge(proj_done, i + 1)
                act.activation(yT[:, 4 + 2 * (i - 6):6 + 2 * (i - 6), :], ps[:, i % 4, :].rearrange("p (c n) -> p c n", c=2),
                               ACT.Silu).then_inc(act_evac, 1)

            act.preload_act_table_set(EXP_LN)
            act.wait_ge(silu_even, 4)
            act.activation(rn[:, :, :], qkvT[:, 0:2 * H, :], ACT.Square).then_inc(sq_ready, 1)
            act.wait_ge(gc_sb, 1)
            act.wait_ge(row_done, 1)
            act.activation(exp_row[:, :, :, :].rearrange("p h t n -> p (h t n)"), two(4), ACT.Exp).then_inc(exp_row_ready, 1)
            act.activation(small[:, 10], small[:, 8], ACT.Exp).then_inc(gcols_act, 1)
            act.activation(small[:, 12], small[:, 11], ACT.Exp).then_inc(gcols_act, 1)
            act.wait_ge(l2_done, 1)
            flat = rn[:, :, :].rearrange("p a b -> p (a b)")
            after(act.activation(flat, ps[:, 0:4, :].rearrange("p b n -> p (b n)"), ACT.Ln, bias=eps_col))
            half = H * SEQ
            act.activation(flat[:, 0:half], flat[:, 0:half], ACT.Exp, scale=-0.5, bias=qscale_col).then_inc(rn_ready, 1)
            act.activation(flat[:, half:], flat[:, half:], ACT.Exp, scale=-0.5).then_inc(rn_ready, 1)
            act.wait_ge(gam_arg, U)
            act.activation(gam[:, :, :], gam[:, :, :], ACT.Exp).then_inc(gam_exp, 1)

            act.preload_act_table(ACT.Gelu_apprx_tanh)
            for i in (8, 9):
                act.wait_ge(proj_done, i + 1)
                act.activation(yT[:, 2 * (i - 8):2 + 2 * (i - 8), :], ps[:, i % 4, :].rearrange("p (c n) -> p c n", c=2),
                               ACT.Gelu_apprx_tanh).then_inc(act_evac, 1)
            for i in (10, 11):
                act.wait_ge(proj_done, i + 1)
                act.activation(v_nat[:, :, (i - 10) * CW:(i - 9) * CW], ps[:, i % 4, :].rearrange("p (t n) -> p t n", t=TILES),
                               ACT.Gelu_apprx_tanh).then_inc(act_evac, 1)
            act.preload_act_table_set(EXP_LN)
            act.wait_ge(ln_var, 1)
            after(act.activation(stat_ln[:, 0, :], mv[:, :, 1], ACT.Ln, bias=eps_col))
            act.activation(stat_ln[:, 1, :], stat_ln[:, 0, :], ACT.Exp, scale=-0.5).then_inc(ln_rstd, 1)
            act.wait_ge(turn_done, 1)
            act.wait_ge(gcols_act, 2)
            for u in range(U):
                hd, t = u // TILES, u % TILES
                act.activation(kd[:, u, :], two(0)[:, u * P:(u + 1) * P], ACT.Copy,
                               scale=small[:, 12, t, hd:hd + 1]).then_inc(kd_ready, 1)
            act.wait_ge(kbe_scale, 1)
            for u in range(U):
                hd, t = u // TILES, u % TILES
                act.activation(kbe[:, u, :], two(0)[:, u * P:(u + 1) * P], ACT.Copy,
                               scale=small[:, 13, t, hd:hd + 1]).then_inc(kbe_ready, 1)
            act.wait_ge(sol_done, 1)
            act.activation(w_solT.rearrange("p u n -> p (u n)"), two(4), ACT.Copy).then_inc(sol_w, 1)
            for c in range(NCH):
                act.wait_ge(o_done, c + 1)
                act.activation(oT[:, :, c * CH:(c + 1) * CH], ps[:, (7, 3)[c % 2], 0:H * CH].rearrange("p (h n) -> p h n", h=H),
                               ACT.Copy).then_inc(o_sb, 1)
            act.wait_ge(o_sb, NCH)
            act.activation(rn[:, 0:H, :], oT, ACT.Square).then_inc(osq_ready, 1)
            act.wait_ge(on_done, 1)
            after(act.activation(rn[:, H:2 * H, :].rearrange("p a b -> p (a b)"), two(0), ACT.Ln, scale=1.0 / DK, bias=eps_col))
            act.activation(rn[:, H:2 * H, :], rn[:, H:2 * H, :], ACT.Exp, scale=-0.5).then_inc(on_ready, 1)

            norm(1)

            def ffn_silu(item, n, j):
                act.wait_ge(up_done, item * FC + (j + 1))
                act.activation(silu_s[:, j % 2, 0:n], ps[:, 4 + j % 2, 0:n], ACT.Silu).then_inc(silu_done, 1)

            act.preload_act_table(ACT.Silu)
            for j in range(FC):
                ffn_silu(0, SEQ, j)

            act.preload_act_table_set(EXP_LN)
            norm(2)
            for i in range(N_QKV):
                act.wait_ge(proj_done, A_FFN + i + 1)
                src = ps[:, i % 4, :].rearrange("p (c n) -> p c n", c=2)
                if i < 4:
                    ins = act.activation(qT[:, 2 * i:2 * i + 2, :], src, ACT.Copy, scale=float(SB_D) ** -0.5)
                elif i < 8:
                    ins = act.activation(kT[:, 2 * i - 8:2 * i - 6, :], src, ACT.Copy)
                else:
                    ins = act.activation(v_att[:, :, (i - 8) * CW:(i - 7) * CW], src, ACT.Copy)
                ins.then_inc(act_evac, 1)

            def log_part(i):
                act.wait_ge(z_done, i + 1)
                if i >= 2:
                    act.wait_ge(w_ready, i - 1)
                after(act.activation(lg[:, i % 2], ps[:, i % 3, 0:NZ], ACT.Abs))
                after(act.activation(lg[:, i % 2], lg[:, i % 2], ACT.Exp, scale=-1.0))
                act.activation(lg[:, i % 2], lg[:, i % 2], ACT.Ln, bias=one_col).then_inc(log_ready, 1)

            def att_part(i):
                act.wait_ge(la_ready, i + 1)
                if i >= 2:
                    act.wait_ge(oh_done, i - 1)
                act.activation(att[:, i % 2], w_log[:, i % 3], ACT.Exp).then_inc(att_exp, 1)

            for i in range(SB_H + 1):
                if i < SB_H:
                    log_part(i)
                if i >= 1:
                    att_part(i - 1)

            norm(3)
            act.wait_ge(r_d, 1)
            act.activation(r_small[:, 1], r_small[:, 0], ACT.Exp).then_inc(r_exp, 1)
            act.preload_act_table(ACT.Silu)

            def evac_y(n):
                act.wait_ge(down_done, (n + 2) * FC)
                act.activation(y_exp[:, 512:D], ps[0:SLOTS, 1, :], ACT.Copy).then_inc(y_act, 1)

            def evac_xg(n):
                act.wait_ge(gather_done, n + 1)
                act.activation(xgT[:, 4:8, :], ps[:, 7, 0:4 * SLOTS].rearrange("p (c n) -> p c n", c=4),
                               ACT.Copy).then_inc(xg_act, 1)

            def evac_back():
                act.activation(back[:, 1, :], ps[0:SLOTS, 7, 4 * SLOTS:4 * SLOTS + P], ACT.Copy).then_inc(back_act, 1)

            evac_xg(0)
            evac_back()
            with act.Fori(0, NE) as n:
                for j in range(FC):
                    ffn_silu(n + 1, SLOTS, j)
                evac_y(n)
                evac_xg(n + 1)
                act.wait_ge(scat_done, n * 4 + 4)
                evac_back()
            act.wait_ge(items_ready, 1)
            n_more = act.value_load(item_i[0:1, 0, 0:1], min_val=0, max_val=7)
            with act.If(n_more > 0):
                with act.Fori(0, n_more) as it:
                    evac_xg(it + NE + 1)
                    evac_back()
                    for j in range(FC):
                        ffn_silu(it + NE + 1, SLOTS, j)
                    evac_y(it + NE)
            act.preload_act_table_set(EXP_LN)
            norm(4, False)

        @block.tensor
        def _(pe):
            mm = pe.matmul

            def norm_turn(k):
                pe.wait_ge(xn_ready, TILES * (k + 1))
                if k == 0:
                    pe.wait_ge(consts_ready, 1)
                for b in range(4):
                    for c in (2 * b, 2 * b + 1):
                        for t in range(TILES):
                            at = (c % 2) * SEQ + t * P
                            last = pe.transpose(ps[:, b, at:at + P], xn[:, t, c * P:(c + 1) * P], ident[:, :])
                    last.then_inc(xnT_done, 1)

            def x_columns(k):
                pe.wait_ge(xT_act, 2 * (k + 1))
                pe.wait_ge(xT_vec, 2 * (k + 1))

            def project_T(i, bank):
                a_arrived(pe, i)
                for m in range(2):
                    for c in range(DC):
                        last = mm(ps[:, bank, m * SEQ:(m + 1) * SEQ], a_slot(i)[:, c, m * P:(m + 1) * P], xT[:, c, :],
                                  start=(c == 0), stop=(c == DC - 1))
                last.then_inc(proj_done, 1)

            def project_N(i, bank, src):
                a_arrived(pe, i)
                for t in range(TILES):
                    for c in range(DC):
                        last = mm(ps[:, bank, t * CW:(t + 1) * CW], src[:, c, t * P:(t + 1) * P], a_slot(i)[:, c, :],
                                  start=(c == 0), stop=(c == DC - 1))
                last.then_inc(proj_done, 1)

            pe.wait_ge(consts_ready, 1)
            pe.wait_ge(ld_rows, 32)
            n_rows = KCONV * CONV_C + 1
            pe.transpose(ps[:, 6, 0:n_rows], rows_raw[0:n_rows, :], ident[0:n_rows, 0:n_rows]).then_inc(rows_done, 1)
            norm_turn(0)
            pe.wait_ge(ld_ba, 16)
            x_columns(0)
            for t in range(TILES):
                for c in range(DC):
                    last = mm(ps[:, 7, t * 2 * H:(t + 1) * 2 * H], xT[:, c, t * P:(t + 1) * P], w_ba[:, c, :],
                              start=(c == 0), stop=(c == DC - 1))
            last.then_inc(ba_done, 1)
            pe.wait_ge(ld_ws, 32)
            for g in range(G):
                last = pe.transpose(two(4)[:, g * P:(g + 1) * P], ws_raw[:, g, :], ident[:, :])
            last.then_inc(wsT_done, 1)

            def decay_rows():
                pe.wait_ge(g_ready, 1)
                pe.wait_ge(wsT_ready, 1)
                g = small[:, 7].rearrange("p t h -> p (t h)")
                mm(ps[:, 6, 0:U], tri_blk[:, :], g, start=True, stop=True)
                mm(ps[:, 6, U:2 * U], blk_ones[:, :], g, start=True, stop=True).then_inc(gc_done, 1)
                for u in range(U):
                    last = mm(two(4)[:, u * P:(u + 1) * P], small[:, 7, u % TILES, u // TILES:u // TILES + 1].to_broadcast([P, P]),
                              tri_blk[:, :], start=True, stop=True)
                last.then_inc(row_done, 1)
                pe.wait_ge(gc_sb, 1)
                for u in range(U):
                    last = mm(two(6)[:, u * P:(u + 1) * P], small[:, 3, u % TILES, u // TILES:u // TILES + 1].to_broadcast([P, P]),
                              ident[:, :], start=True, stop=True)
                last.then_inc(row_done, 1)

            for i in range(8):
                if i >= 4:
                    pe.wait_ge(act_evac, i - 3)
                project_T(i, i % 4)
                if i == 2:
                    decay_rows()
            pe.wait_ge(sq_ready, 1)
            pe.wait_ge(act_evac, 8)
            for b in range(4):
                last = mm(ps[:, b, :], ones[:, :], rn[:, 2 * b:2 * b + 2, :].rearrange("p a b -> p (a b)"), start=True, stop=True)
            last.then_inc(l2_done, 1)
            pe.wait_ge(rn_ready, 1)
            for i in (8, 9):
                project_T(i, i % 4)
            for i in (10, 11):
                project_N(i, i % 4, xT)
            pe.wait_ge(kb_ready, 2)
            pe.wait_ge(gam_arg, U)
            pe.wait_ge(exp_row_ready, 1)
            for m, src in enumerate((kbT, qkvT)):
                for u in range(U):
                    hd, t = u // TILES, u % TILES
                    last = mm(two(4 + 2 * m)[:, u * P:(u + 1) * P], qkvT[:, H + hd, t * P:(t + 1) * P],
                              src[:, hd, t * P:(t + 1) * P], start=True, stop=True)
                last.then_inc(kk_done, 1)
            pe.wait_ge(act_evac, 12)
            for m in range(2):
                for u in range(U):
                    hd, t = u // TILES, u % TILES
                    last = pe.transpose(two(2 * m)[:, u * P:(u + 1) * P], qkvT[:, (1 + m) * H + hd, t * P:(t + 1) * P],
                                        ident[:, :])
                last.then_inc(turn_done, 1)

            def gate_mix():
                pe.wait_ge(v_ready, TILES)
                pe.wait_ge(kd_ready, U)
                pe.wait_ge(kbe_ready, U)
                for t in range(TILES):
                    for g in range(G):
                        at = (g // 2) * SEQ + t * P
                        last = mm(two(0)[(g % 2) * GD:(g % 2 + 1) * GD, at:at + P], v_nat[:, t, g * GD:(g + 1) * GD],
                                  wsT[:, g, :], start=True, stop=True)
                last.then_inc(mix_done, 1)

            pe.wait_ge(lt_ready, 1)
            pe.wait_ge(attn_ready, 1)
            pe.wait_ge(vb_ready, U)
            for k in range(LEVELS):
                for hf in range(2):
                    if k:
                        pe.wait_ge(x_ready, 2 * k + hf - 1)
                    for m in range(4):
                        u = 4 * hf + m
                        last = mm(ps[:, 4 + hf, m * P:(m + 1) * P], gam[:, u, :], inv_x[:, u, :] if k else ident[:, :],
                                  start=True, stop=True)
                    last.then_inc(t_done, 1)
                for hf in range(2):
                    pe.wait_ge(t_ready, 2 * k + hf + 1)
                    if k:
                        pe.wait_ge(xt_ready, 2 * k + hf - 1)
                    if k < LEVELS - 1:
                        for m in range(4):
                            u = 4 * hf + m
                            last = mm(ps[:, 6 + hf, m * P:(m + 1) * P], inv_xt[:, u, :] if k else ident[:, :],
                                      inv_t[:, u, :], start=True, stop=True)
                        last.then_inc(x_done, 1)
                    for m in range(4):
                        u = 4 * hf + m
                        last = mm(ps[:, 2 + hf, m * P:(m + 1) * P], inv_t[:, u, :], inv_xt[:, u, :] if k else ident[:, :],
                                  start=True, stop=True)
                    last.then_inc(xt_done, 1)
                if k == 2:
                    gate_mix()
            pe.wait_ge(xt_ready, 2 * LEVELS)
            pe.wait_ge(ya_ready, 1)
            for u in range(U):
                last = mm(two(4)[:, u * P:(u + 1) * P], kbe[:, u, :], inv_xt[:, u, :], start=True, stop=True)
            last.then_inc(sol_done, 1)
            for u in range(U):
                last = mm(two(0)[:, u * P:(u + 1) * P], inv_xt[:, u, :], vb[:, u, :], start=True, stop=True)
            last.then_inc(sol_done, 1)
            pe.wait_ge(sol_w, 1)
            pe.wait_ge(qd_ready, 1)
            for c in range(NCH):
                t, p0 = c // 2, (c % 2) * CH
                rows, tok = slice(p0, p0 + CH), slice(c * CH, (c + 1) * CH)
                if c:
                    pe.wait_ge(st_ready, c)
                    for hd in range(H):
                        last = mm(ps[rows, 6, hd * P:(hd + 1) * P], w_solT[:, hd * TILES + t, rows], state[:, hd, :],
                                  start=True, stop=True)
                    last.then_inc(ws_done, 1)
                pe.wait_ge(vnew_ready, c + 1)
                if c < NCH - 1:
                    for hd in range(H):
                        last = mm(ps[:, 2, hd * P:(hd + 1) * P], kd[rows, hd * TILES + t, :],
                                  v_new[rows, t, hd * P:(hd + 1) * P], start=True, stop=True)
                    last.then_inc(st_done, 1)
                if c >= 2:
                    pe.wait_ge(o_sb, c - 1)
                for hd in range(H):
                    o = ps[:, (7, 3)[c % 2], hd * CH:(hd + 1) * CH]
                    if c:
                        mm(o, state[:, hd, :], qkvT[:, hd, tok], start=True, stop=False)
                    last = mm(o, v_new[rows, t, hd * P:(hd + 1) * P], attnT[rows, hd * TILES + t, rows],
                              start=(c == 0), stop=True)
                last.then_inc(o_done, 1)
            pe.wait_ge(osq_ready, 1)
            for b in range(2):
                last = mm(ps[:, b, :], ones[:, :], rn[:, 2 * b:2 * b + 2, :].rearrange("p a b -> p (a b)"), start=True, stop=True)
            last.then_inc(on_done, 1)
            pe.wait_ge(yb_ready, 1)
            for i in range(A_OUT, A_FFN):
                project_N(i, i % 4, yT)

            def up(item, n, j, x_src, first, arrived):
                g, m = j // 2, j % 2
                if m == 0:
                    arrived(2 * g)
                    arrived(2 * g + 1)
                if j >= 2 or not isinstance(item, int):
                    pe.wait_ge(hT_ready, item * FC + (j - 1))
                for w in range(2):
                    slot = a_slot(first + 2 * g + w)
                    for c in range(DC):
                        last = mm(ps[:, 4 + j % 2, w * n:(w + 1) * n], slot[:, c, m * P:(m + 1) * P], x_src[:, c, 0:n],
                                  start=(c == 0), stop=(c == DC - 1))
                    if w == 1:
                        last.then_inc(up_done, 1)

            def down(item, n, j, arrived):
                arrived(j)
                pe.wait_ge(hT_ready, item * FC + (j + 1))
                for t in range((n + P - 1) // P):
                    rows = min(n, P)
                    for hf in range(2):
                        last = mm(ps[0:rows, 2 * t + hf, :], hT[:, j % 2, t * P:t * P + rows], ring_b[:, j % RB, hf * 512:(hf + 1) * 512],
                                  start=(j == 0), stop=(j == FC - 1))
                last.then_inc(down_done, 1)

            def ffn(item, n, x_src, first, a_arr, b_arr):
                up(item, n, 0, x_src, first, a_arr)
                for j in range(1, FC):
                    up(item, n, j, x_src, first, a_arr)
                    down(item, n, j - 1, b_arr)
                down(item, n, FC - 1, b_arr)

            norm_turn(1)
            x_columns(1)
            ffn(0, SEQ, xT, A_FFN, lambda p: a_arrived(pe, A_FFN + p), lambda j: pe.wait_ge(b_in[j % RB], 16 * (j // RB + 1)))
            norm_turn(2)
            x_columns(2)
            for i in range(N_QKV):
                if i >= 4:
                    pe.wait_ge(act_evac, 12 + i - 3)
                (project_T(A_QKV + i, i % 4) if i < 8 else project_N(A_QKV + i, i % 4, xT))
            pe.wait_ge(act_evac, 12 + N_QKV)

            def scores(i):
                rows = slice((i % 2) * SB_D, (i % 2 + 1) * SB_D)
                if i >= 3:
                    pe.wait_ge(w_ready, i - 2)
                for b, (s, t) in enumerate(((0, 0), (1, 1), (0, 1))):
                    last = mm(ps[:, i % 3, b * P:(b + 1) * P], kT[rows, i // 2, s * P:(s + 1) * P],
                              qT[rows, i // 2, t * P:(t + 1) * P], start=True, stop=True)
                last.then_inc(z_done, 1)

            def sums_after(i):
                pe.wait_ge(spm_ready, i + 1)
                if i >= 3:
                    pe.wait_ge(la_ready, i - 2)
                o = ps[:, 3 + i % 3]
                mm(o[:, 0:2 * P], neg_after[:, :], sp_m[:, i % 2, 0:2 * P], start=True, stop=True)
                mm(o[:, 2 * P:NZ], neg_after[:, :], sp_m[:, i % 2, 2 * P:NZ], start=True, stop=False)
                mm(o[:, 2 * P:NZ], neg_ones[:, :], sp_m[:, i % 2, P:2 * P], start=False, stop=True).then_inc(after_done, 1)

            def head_o(i):
                pe.wait_ge(att_ready, i + 1)
                pr = i // 2
                if pr >= 2:
                    pe.wait_ge(oh_ready, pr - 1)
                o = ps[(i % 2) * SB_D:(i % 2 + 1) * SB_D, 6 + pr % 2]
                mm(o[:, 0:P], v_att[:, 0, i * SB_D:(i + 1) * SB_D], att[:, i % 2, 0:P], start=True, stop=True)
                mm(o[:, P:2 * P], v_att[:, 0, i * SB_D:(i + 1) * SB_D], att[:, i % 2, 2 * P:NZ], start=True, stop=False)
                mm(o[:, P:2 * P], v_att[:, 1, i * SB_D:(i + 1) * SB_D], att[:, i % 2, P:2 * P], start=False, stop=True)\
                    .then_inc(oh_done, 1)

            scores(0)
            scores(1)
            for i in range(SB_H + 1):
                if i + 2 < SB_H:
                    scores(i + 2)
                if i < SB_H:
                    sums_after(i)
                if i >= 1:
                    head_o(i - 1)
            pe.wait_ge(oh_ready, SB_H // 2)
            for i in range(A_WO, A_MOE):
                project_N(i, (i - A_WO) % 4, o_attT)
            norm_turn(3)
            x_columns(3)
            pe.wait_ge(ld_wr, 16)
            for t in range(TILES):
                for c in range(DC):
                    last = mm(ps[:, 6, t * NE:(t + 1) * NE], xT[:, c, t * P:(t + 1) * P], w_router[:, c, :],
                              start=(c == 0), stop=(c == DC - 1))
            last.then_inc(lgt_done, 1)
            pe.wait_ge(sel_ready, 1)
            o = ps[:, 7]
            mm(o[:, 0:NE], before[:, :], r2[:, 3, 0, :], start=True, stop=True)
            mm(o[:, NE:2 * NE], before[:, :], r2[:, 3, 1, :], start=True, stop=False)
            mm(o[:, NE:2 * NE], ones[:, :], r2[:, 3, 0, :], start=False, stop=True)
            mm(o[:, 2 * NE:3 * NE], ones[:, :], r2[:, 3, 0, :], start=True, stop=False)
            mm(o[:, 2 * NE:3 * NE], ones[:, :], r2[:, 3, 1, :], start=False, stop=True).then_inc(pos_done, 1)

            def gather(n):
                if not isinstance(n, int):
                    pe.wait_ge(xg_act, n)
                    pe.wait_ge(xg_vec, n)
                    pe.wait_ge(back_act, n)
                    pe.wait_ge(back_vec, n)
                pe.wait_ge(prep_done, n * 4 + 4)
                for c in range(DC):
                    for t in range(TILES):
                        at = (c % 4) * SLOTS
                        mm(ps[:, 6 + c // 4, at:at + SLOTS], xn[:, t, c * P:(c + 1) * P], sel_p[:, t, :],
                           start=(t == 0), stop=(t == TILES - 1))
                for t in range(TILES):
                    last = pe.transpose(ps[0:SLOTS, 6 + t, 4 * SLOTS:4 * SLOTS + P], sel_w[:, t, :], ident[:, :])
                last.then_inc(gather_done, 1)

            def expert(n, g):
                pe.wait_ge(xg_act, g + 1)
                pe.wait_ge(xg_vec, g + 1)
                a_arr = lambda p: pe.wait_ge(a_in[(A_MOE + p) % RA], n * (16 * PER_FFN // RA) + 16 * ((A_MOE + p) // RA + 1))
                b_arr = lambda j: pe.wait_ge(b_in[j % RB], n * (16 * FC // RB) + 16 * ((FC + j) // RB + 1))
                ffn(n + 1, SLOTS, xgT, A_MOE, a_arr, b_arr)

            def scatter(n, g):
                pe.wait_ge(back_act, g + 1)
                pe.wait_ge(back_vec, g + 1)
                pe.wait_ge(y_act, n + 1)
                pe.wait_ge(y_vec, n + 1)
                for m in range(4):
                    t, hf = m // 2, m % 2
                    if m >= 2:
                        pe.wait_ge(scat_added, n * 4 + (m - 1))
                    mm(ps[:, 2 + m % 2, :], back[:, t, :], y_exp[:, hf * 512:(hf + 1) * 512], start=True, stop=True)\
                        .then_inc(scat_done, 1)

            gather(0)
            with pe.Fori(0, NE) as n:
                expert(n, n)
                gather(n + 1)
                scatter(n, n)
            pe.wait_ge(items_ready, 1)
            n_more = pe.value_load(item_i[0:1, 0, 0:1], min_val=0, max_val=7)
            with pe.If(n_more > 0):
                with pe.Fori(0, n_more) as it:
                    gather(it + NE + 1)
                    expert(it + NE, it + NE + 1)
                    scatter(it + NE, it + NE + 1)

        @block.vector
        def _(vec):
            own = [0]

            def after(ins):
                own[0] += 1
                ins.then_inc(vec_own, 1)
                vec.wait_ge(vec_own, own[0])

            tt, ts, stt = vec.tensor_tensor, vec.tensor_scalar, vec.scalar_tensor_tensor
            vec.memset(eps_col, EPS)
            vec.memset(one_col, 1.0)
            after(vec.memset(qscale_col, -0.5 * math.log(DK)))

            def norm(k, last=False):
                vec.wait_ge(rinv_ready, k + 1)
                vec.wait_ge(ld_gain[k % 2], 16 * (k // 2 + 1))
                for t in range(TILES):
                    stt(xn[:, t, :], h[:, t, :], stat[:, k, 4 + t:5 + t], gain[:, k % 2, :], ALU.mult, ALU.mult)\
                        .then_inc(out_ready if last else xn_ready, 1)
                if not last:
                    for b in (0, 2):
                        vec.wait_ge(xnT_done, 4 * k + b + 1)
                        vec.tensor_copy(xT[:, 2 * b:2 * b + 2, :], ps[:, b, :].rearrange("p (c n) -> p c n", c=2)).then_inc(xT_vec, 1)

            vec.wait_ge(ld_x, 16)
            vec.wait_ge(consts_ready, 1)
            norm(0)
            vec.wait_ge(rows_done, 1)
            vec.tensor_copy(colt[:, 0:KCONV * CONV_C + 1], ps[:, 6, 0:KCONV * CONV_C + 1]).then_inc(colt_ready, 1)
            vec.wait_ge(ba_done, 1)
            vec.tensor_copy(ba[:, :, :], ps[:, 7, 0:2 * U].rearrange("p (t n) -> p t n", t=TILES)).then_inc(ba_sb, 1)
            vec.wait_ge(ba_sb, 1)
            vec.wait_ge(ld_small, 32)
            after(tt(small[:, 14], ba[:, :, H:2 * H], small[:, 0, 0, :].unsqueeze(1).to_broadcast([P, TILES, H]), ALU.add))
            stt(small[:, 4], small[:, 14], -1.0, small[:, 14], ALU.mult, ALU.max).then_inc(gb_vec, 1)
            vec.wait_ge(gb_act, 1)
            after(ts(small[:, 1], small[:, 1], 1.0, None, ALU.add))
            after(vec.reciprocal(small[:, 3], small[:, 1]))
            vec.wait_ge(gb_act, 3)
            after(stt(small[:, 15], small[:, 14], 0.0, small[:, 6], ALU.max, ALU.add))
            stt(small[:, 7], small[:, 15], -1.0, small[:, 2, 0, :].unsqueeze(1).to_broadcast([P, TILES, H]),
                ALU.mult, ALU.mult).then_inc(g_ready, 1)
            vec.wait_ge(wsT_done, 1)
            vec.tensor_copy(wsT[:, :, :].rearrange("p g n -> p (g n)"), two(4)).then_inc(wsT_ready, 1)

            conv_steps = [0]

            def conv(i):
                vec.wait_ge(act_evac, i + 1)
                for k in range(KCONV):
                    for c in (2 * i, 2 * i + 1):
                        w = colt[:, k * CONV_C + c:k * CONV_C + c + 1]
                        src = conv_in[:, c, k:k + SEQ]
                        if k == 0:
                            ins = ts(qkvT[:, c, :], src, w, None, ALU.mult)
                        else:
                            ins = stt(qkvT[:, c, :], src, w, qkvT[:, c, :], ALU.mult, ALU.add)
                        if k < KCONV - 1:
                            last = ins
                    if k < KCONV - 1:
                        after(last)
                ins.then_inc(conv_done, 1)

            vec.wait_ge(colt_ready, 1)
            for i in range(3):
                conv(i)
            vec.wait_ge(gc_done, 1)
            after(vec.tensor_copy(small[:, 8:10].rearrange("p a t h -> p (a t h)"), ps[:, 6, 0:2 * U]))
            tt(small[:, 11], small[:, 9], small[:, 8], ALU.subtract).then_inc(gc_sb, 1)
            for i in range(3, 6):
                conv(i)
            vec.wait_ge(exp_row_ready, 1)
            for u in range(U):
                hd, t = u // TILES, u % TILES
                ts(gam[:, u, :], two(4)[:, u * P:(u + 1) * P], small[:, 8, t, hd:hd + 1], 0.0,
                   ALU.subtract, ALU.min).then_inc(gam_arg, 1)
            vec.wait_ge(gcols_act, 1)
            tt(small[:, 13], small[:, 3], small[:, 10], ALU.mult).then_inc(kbe_scale, 1)
            vec.wait_ge(rn_ready, 2)
            after(tt(qkvT[:, H:2 * H, :], qkvT[:, H:2 * H, :], rn[:, H:2 * H, :], ALU.mult))
            vec.wait_ge(row_done, 2)
            tt(kbT[:, :, :].rearrange("p a b -> p (a b)"), qkvT[:, H:2 * H, :].rearrange("p a b -> p (a b)"), two(6),
               ALU.mult).then_inc(kb_ready, 1)
            tt(qkvT[:, 0:H, :], qkvT[:, 0:H, :], rn[:, 0:H, :], ALU.mult).then_inc(kb_ready, 1)
            vec.wait_ge(gam_exp, 1)
            after(tt(gam[:, :, :], gam[:, :, :], tri_blk[:, :].unsqueeze(1).to_broadcast([P, U, P]), ALU.mult))
            vec.wait_ge(kk_done, 2)
            flat_g = gam[:, :, :].rearrange("p u n -> p (u n)")
            tt(attnT[:, :, :].rearrange("p u n -> p (u n)"), two(6), flat_g, ALU.mult).then_inc(attn_ready, 1)
            vec.wait_ge(attn_ready, 1)
            tt(flat_g, two(4), flat_g, ALU.mult).then_inc(lt_ready, 1)
            tt(qkvT[:, 0:H, :].rearrange("p a b -> p (a b)"), qkvT[:, 0:H, :].rearrange("p a b -> p (a b)"),
               exp_row[:, :, :, :].rearrange("p h t n -> p (h t n)"), ALU.mult).then_inc(qd_ready, 1)
            vec.wait_ge(turn_done, 2)
            for u in range(U):
                hd, t = u // TILES, u % TILES
                ts(vb[:, u, :], two(2)[:, u * P:(u + 1) * P], small[:, 3, t, hd:hd + 1], None, ALU.mult).then_inc(vb_ready, 1)
            vec.wait_ge(act_evac, 12)
            for t in range(TILES):
                after(vec.bn_stats(bn[:, t, :], v_nat[:, t, :]))
            vec.bn_aggr(mv[:, 0, :], bn[:, 0, :])
            vec.bn_aggr(mv[:, 1, :], bn[:, 1, :]).then_inc(ln_var, 1)

            def layernorm():
                vec.wait_ge(ln_rstd, 1)
                vec.wait_ge(ld_lng, 32)
                for t in range(TILES):
                    after(ts(v_nat[:, t, :], v_nat[:, t, :], mv[:, t, 0:1], stat_ln[:, 1, t:t + 1], ALU.subtract, ALU.mult))
                    after(tt(v_nat[:, t, :], v_nat[:, t, :], ln_g, ALU.mult))
                    tt(v_nat[:, t, :], v_nat[:, t, :], ln_b, ALU.add).then_inc(v_ready, 1)

            def gate_out():
                vec.wait_ge(mix_done, 1)
                vec.wait_ge(ld_bias, 32)
                tmp = wsT[:, :, :].rearrange("p g n -> p (g n)")
                after(tt(tmp.rearrange("p (c t n) -> p c t n", c=G // 2, t=TILES),
                         two(0).rearrange("p (c t n) -> p c t n", c=G // 2, t=TILES),
                         sgu_bias[:, :, :].unsqueeze(2).to_broadcast([P, G // 2, TILES, P]), ALU.add))
                y = yT[:, 0:4, :].rearrange("p a b -> p (a b)")
                tt(y, tmp, y, ALU.mult).then_inc(ya_ready, 1)

            def units4(t):
                return t.unsqueeze(1).to_broadcast([P, 4, P])

            for k in range(LEVELS):
                for hf in range(2):
                    us = slice(4 * hf, 4 * hf + 4)
                    vec.wait_ge(t_done, 2 * k + hf + 1)
                    tt(inv_t[:, us, :], ps[:, 4 + hf, :].rearrange("p (u n) -> p u n", u=4), units4(level[:, k, :]),
                       ALU.mult).then_inc(t_ready, 1)
                for hf in range(2):
                    us = slice(4 * hf, 4 * hf + 4)
                    if k < LEVELS - 1:
                        vec.wait_ge(x_done, 2 * k + hf + 1)
                        tt(inv_x[:, us, :], inv_x[:, us, :] if k else units4(ident[:, :]),
                           ps[:, 6 + hf, :].rearrange("p (u n) -> p u n", u=4), ALU.subtract).then_inc(x_ready, 1)
                    vec.wait_ge(xt_done, 2 * k + hf + 1)
                    tt(inv_xt[:, us, :], inv_xt[:, us, :] if k else units4(ident[:, :]),
                       ps[:, 2 + hf, :].rearrange("p (u n) -> p u n", u=4), ALU.subtract).then_inc(xt_ready, 1)
                if k == 0:
                    layernorm()
                if k == 3:
                    gate_out()
            vec.wait_ge(sol_done, 2)
            vec.tensor_copy(u_sol.rearrange("p u n -> p (u n)"), two(0)).then_inc(sol_u, 1)
            vec.wait_ge(sol_u, 1)
            for c in range(NCH):
                t, p0 = c // 2, (c % 2) * CH
                rows = slice(p0, p0 + CH)
                u4 = u_sol.rearrange("p (h t) n -> p t h n", t=TILES)[rows, t]
                vn = v_new[rows, t, :].rearrange("p (h n) -> p h n", h=H)
                if c == 0:
                    vec.tensor_copy(vn, u4).then_inc(vnew_ready, 1)
                else:
                    vec.wait_ge(ws_done, c)
                    tt(vn, u4, ps[rows, 6, :].rearrange("p (h n) -> p h n", h=H), ALU.subtract).then_inc(vnew_ready, 1)
                if c < NCH - 1:
                    vec.wait_ge(st_done, c + 1)
                    if c == 0:
                        vec.tensor_copy(state[:, :, :].rearrange("p h n -> p (h n)"), ps[:, 2, :]).then_inc(st_ready, 1)
                    else:
                        vec.wait_ge(o_done, c + 1)
                        for hd in range(H):
                            ins = stt(state[:, hd, :], state[:, hd, :], exp_row[:, hd, t, p0 + CH - 1:p0 + CH],
                                      ps[:, 2, hd * P:(hd + 1) * P], ALU.mult, ALU.add)
                        ins.then_inc(st_ready, 1)
            vec.wait_ge(on_ready, 1)
            fo = oT.rearrange("p a b -> p (a b)")
            after(stt(fo, fo, colt[:, KCONV * CONV_C:KCONV * CONV_C + 1], rn[:, H:2 * H, :].rearrange("p a b -> p (a b)"),
                      ALU.mult, ALU.mult))
            yb = yT[:, 4:8, :].rearrange("p a b -> p (a b)")
            tt(yb, fo, yb, ALU.mult).then_inc(yb_ready, 1)

            def add_project(i, base, last_inc):
                vec.wait_ge(proj_done, base + i + 1)
                ins = tt(h[:, :, i * CW:(i + 1) * CW], h[:, :, i * CW:(i + 1) * CW],
                         ps[:, i % 4, :].rearrange("p (t n) -> p t n", t=TILES), ALU.add)
                if last_inc:
                    ins.then_inc(h_ready, 1)

            for i in range(N_OUT):
                add_project(i, A_OUT, i == N_OUT - 1)
            norm(1)

            def ffn_mul(item, n, j):
                vec.wait_ge(silu_done, item * FC + (j + 1))
                if j >= 2 or not isinstance(item, int):
                    vec.wait_ge(down_done, item * FC + (j - 1))
                tt(hT[:, j % 2, 0:n], silu_s[:, j % 2, 0:n], ps[:, 4 + j % 2, n:2 * n], ALU.mult).then_inc(hT_ready, 1)

            for j in range(FC):
                ffn_mul(0, SEQ, j)
            vec.wait_ge(down_done, FC)
            for m in range(4):
                t, hf = m // 2, m % 2
                cs = slice(hf * 512, (hf + 1) * 512)
                ins = tt(h[:, t, cs], h[:, t, cs], ps[:, m, :], ALU.add)
            ins.then_inc(h_ready, 1)
            norm(2)

            def softplus(i):
                vec.wait_ge(log_ready, i + 1)
                if i >= 2:
                    vec.wait_ge(after_done, i - 1)
                if i >= 3:
                    vec.wait_ge(att_exp, i - 2)
                stt(sp_m[:, i % 2], ps[:, i % 3, 0:NZ], 0.0, lg[:, i % 2], ALU.max, ALU.add).then_inc(sp_ready, 1)
                stt(w_log[:, i % 3], ps[:, i % 3, 0:NZ], 0.0, lg[:, i % 2], ALU.min, ALU.subtract).then_inc(w_ready, 1)

            def log_att(i):
                vec.wait_ge(after_done, i + 1)
                vec.wait_ge(w_ready, i + 1)
                tt(w_log[:, i % 3], w_log[:, i % 3], ps[:, 3 + i % 3, 0:NZ], ALU.add).then_inc(la_ready, 1)

            def head_out(pr):
                vec.wait_ge(oh_done, 2 * pr + 2)
                vec.tensor_copy(o_attT[:, pr, :], ps[:, 6 + pr % 2, 0:SEQ]).then_inc(oh_ready, 1)

            for i in range(SB_H + 1):
                if i < SB_H:
                    softplus(i)
                if i >= 1:
                    log_att(i - 1)
                if i >= 4 and i % 2 == 0:
                    head_out(i // 2 - 2)
            head_out(SB_H // 2 - 1)
            for i in range(N_OUT):
                add_project(i, A_FFN + N_QKV, i == N_OUT - 1)
            norm(3)

            vec.wait_ge(lgt_done, 1)
            after(vec.tensor_copy(logits[:, :, :].rearrange("p t e -> p (t e)"), ps[:, 6, 0:TILES * NE]))
            TE = TILES * NE
            lgf = logits[:, :, :]
            other = lgf.unsqueeze(2).to_broadcast([P, TILES, NE, NE])
            mine = lgf.rearrange("p t e -> p (t e)").unsqueeze(2).to_broadcast([P, TE, NE])

            def four(a):
                return a.rearrange("p (t e) f -> p t e f", t=TILES)

            mine4 = lgf.unsqueeze(3).to_broadcast([P, TILES, NE, NE])
            tt(four(rt[:, 0]), other, mine4, ALU.is_gt)
            after(tt(four(rt[:, 1]), other, mine4, ALU.is_equal))
            e_of = iota[:, 0:NE].unsqueeze(2).to_broadcast([P, NE, NE])
            f_of = iota[:, 0:NE].unsqueeze(1).to_broadcast([P, NE, NE])
            tt(rt[:, 2, 0:NE, :], f_of, e_of, ALU.is_lt)
            after(tt(rt[:, 2, NE:TE, :], f_of, e_of, ALU.is_lt))
            after(tt(rt[:, 1], rt[:, 1], rt[:, 2], ALU.mult))
            after(tt(rt[:, 0], rt[:, 0], rt[:, 1], ALU.add))
            after(vec.tensor_reduce(r2[:, 0].rearrange("p t e -> p (t e)"), rt[:, 0], AX.X, ALU.add))
            ts(r2[:, 1], r2[:, 0], 0.0, None, ALU.is_equal)
            after(ts(r2[:, 2], r2[:, 0], 1.0, None, ALU.is_equal))
            tt(r2[:, 3], r2[:, 1], r2[:, 2], ALU.add).then_inc(sel_ready, 1)
            tt(r2[:, 4], r2[:, 1], lgf, ALU.mult)
            after(tt(r2[:, 5], r2[:, 2], lgf, ALU.mult))
            after(tt(r2[:, 4], r2[:, 5], r2[:, 4], ALU.subtract))
            vec.tensor_reduce(r_small[:, 0], r2[:, 4], AX.X, ALU.add).then_inc(r_d, 1)
            vec.wait_ge(r_exp, 1)
            after(ts(r_small[:, 2], r_small[:, 1], 1.0, None, ALU.add))
            after(vec.reciprocal(r_small[:, 3], r_small[:, 2]))
            after(tt(r_small[:, 4], r_small[:, 3], r_small[:, 1], ALU.mult))
            for t in range(TILES):
                after(ts(r2[:, 6, t], r2[:, 1, t], r_small[:, 3, t:t + 1], None, ALU.mult))
                after(stt(r2[:, 7, t], r2[:, 2, t], r_small[:, 4, t:t + 1], r2[:, 6, t], ALU.mult, ALU.add))
            vec.wait_ge(sel_ready, 1)
            vec.wait_ge(pos_done, 1)
            place = ps[:, 7, 0:2 * NE].rearrange("p (t e) -> p t e", t=TILES)
            for b in range(NB):
                ks = slice(b * NE, (b + 1) * NE)
                ts(table[:, 0, :, ks], place, float(-SLOTS * b), None, ALU.add)
                vec.tensor_copy(table[:, 1, :, ks], r2[:, 3])
                after(vec.tensor_copy(table[:, 2, :, ks], r2[:, 7]))
            for b in range(1, NB):
                after(ts(li[0:1, 0, (b - 1) * NE:b * NE], ps[0:1, 7, 2 * NE:3 * NE], float(SLOTS * b), None, ALU.is_gt))
            after(vec.tensor_tensor_scan(li[0:1, 1, :], ones[0:1, 0:16], li[0:1, 0, :], 0.0, ALU.mult, ALU.add))
            after(tt(li[0:1, 2, :], li[0:1, 0, :], iota[0:1, NE:NE + 16], ALU.mult))
            after(tt(li3[0:1, 0], li[0:1, 1, :].unsqueeze(1).to_broadcast([1, 8, 16]),
                     iota[0:1, 1:9].unsqueeze(2).to_broadcast([1, 8, 16]), ALU.is_equal))
            after(tt(li3[0:1, 0], li3[0:1, 0], li[0:1, 2, :].unsqueeze(1).to_broadcast([1, 8, 16]), ALU.mult))
            after(vec.tensor_reduce(item_f[0:1, 1, :], li3[0:1, 0], AX.X, ALU.add))
            after(ts(li[0:1, 3, 0:8], item_f[0:1, 1, :], float(2 * NE), -float(NE), ALU.is_ge, ALU.mult))
            after(tt(li[0:1, 4, 0:8], item_f[0:1, 1, :], li[0:1, 3, 0:8], ALU.add))
            after(ts(item_f[0:1, 2, :], li[0:1, 4, 0:8], -float(NE), 0.0, ALU.add, ALU.max))
            after(vec.tensor_copy(item_f[0:1, 0, :], li[0:1, 1, 15:16].to_broadcast([1, 8])))
            vec.tensor_copy(item_i[:, :, :], item_f[:, :, :]).then_inc(items_ready, 1)

            def prep(n, k):
                vec.tensor_copy(col6[:, :, :, :], table[:, :, :, bass.ds(k, 1)]).then_inc(prep_col, 1)
                vec.wait_ge(prep_col, n + 1)
                if not isinstance(n, int):
                    vec.wait_ge(gather_done, n)
                for t in range(TILES):
                    ts(sel_p[:, t, :], iota[:, 0:SLOTS], col6[:, 0, t], col6[:, 1, t], ALU.is_equal, ALU.mult).then_inc(prep_done, 1)
                    ts(sel_w[:, t, :], iota[:, 0:SLOTS], col6[:, 0, t], col6[:, 2, t], ALU.is_equal, ALU.mult).then_inc(prep_done, 1)

            def evac_y(n):
                vec.wait_ge(down_done, (n + 2) * FC)
                vec.tensor_copy(y_exp[:, 0:512], ps[0:SLOTS, 0, :]).then_inc(y_vec, 1)

            def evac_xg(n):
                vec.wait_ge(gather_done, n + 1)
                vec.tensor_copy(xgT[:, 0:4, :], ps[:, 6, 0:4 * SLOTS].rearrange("p (c n) -> p c n", c=4)).then_inc(xg_vec, 1)

            def evac_back():
                vec.tensor_copy(back[:, 0, :], ps[0:SLOTS, 6, 4 * SLOTS:4 * SLOTS + P]).then_inc(back_vec, 1)

            def add_scatter(n):
                for m in range(4):
                    t, hf = m // 2, m % 2
                    cs = slice(hf * 512, (hf + 1) * 512)
                    vec.wait_ge(scat_done, n * 4 + (m + 1))
                    tt(h[:, t, cs], h[:, t, cs], ps[:, 2 + m % 2, :], ALU.add).then_inc(scat_added, 1)

            prep(0, 0)
            evac_xg(0)
            evac_back()
            with vec.Fori(0, NE) as n:
                for j in range(FC):
                    ffn_mul(n + 1, SLOTS, j)
                    if j == 4:
                        prep(n + 1, n + 1)
                evac_y(n)
                evac_xg(n + 1)
                add_scatter(n)
                evac_back()
            vec.wait_ge(items_ready, 1)
            n_more = vec.value_load(item_i[0:1, 0, 0:1], min_val=0, max_val=7)
            with vec.If(n_more > 0):
                with vec.Fori(0, n_more) as it:
                    k = vec.value_load(item_i[0:1, 1, bass.ds(it, 1)], min_val=0, max_val=NK - 1)
                    prep(it + NE + 1, k)
                    evac_xg(it + NE + 1)
                    evac_back()
                    for j in range(FC):
                        ffn_mul(it + NE + 1, SLOTS, j)
                    evac_y(it + NE)
                    add_scatter(it + NE)
            vec.wait_ge(items_ready, 1)
            vec.drain().then_inc(h_ready, 1)
            norm(4, True)


_INS = ['x', 'e_norm1', 'e_w_in', 'e_sgu_ln_g', 'e_sgu_ln_b', 'e_sgu_w', 'e_sgu_b', 'e_conv_w', 'e_a_log',
        'e_dt_bias', 'e_o_norm', 'e_w_out', 'e_norm2', 'e_ffn_w1', 'e_ffn_w3', 'e_ffn_w2', 'o_norm1', 'o_w_qkv',
        'o_w_out', 'o_norm2', 'o_router', 'o_moe_w1', 'o_moe_w3', 'o_moe_w2', 'final_norm']
_OUTS = [((1, 256, 1024), 'float32')]


def kernel(**inputs):
    import numpy as _np
    import concourse.bacc as _bacc
    from concourse import mybir as _mybir
    from concourse.bass_utils import run_bass_kernel_spmd as _run

    nc = _bacc.Bacc("TRN2", target_bir_lowering=False, num_devices=1)
    arrays, args = {}, []
    for name in _INS:
        a = _np.ascontiguousarray(inputs[name])
        arrays[f"in_{name}_dram"] = a
        args.append(nc.dram_tensor(f"in_{name}_dram", a.shape, _mybir.dt.from_np(a.dtype), kind="ExternalInput").ap())
    for i, (shape, dtype) in enumerate(_OUTS):
        dt = _mybir.dt.from_np(_np.dtype(dtype))
        args.append(nc.dram_tensor(f"out_{i}_dram", shape, dt, kind="ExternalOutput").ap())
    trunk(nc, *args)
    r = _run(nc, [arrays], core_ids=[0])
    got = tuple(r.results[0][f"out_{i}_dram"] for i in range(len(_OUTS)))
    return got[0]
```

```python
import math
from contextlib import ExitStack

import concourse.bass as bass
from concourse import mybir

F32 = mybir.dt.float32
F32R = mybir.dt.float32r
I32 = mybir.dt.int32
ALU = mybir.AluOpType
ACT = mybir.ActivationFunctionType
AX = mybir.AxisListType

P = 128
EPS = 1e-6
EXP_LN = "natural_log_exp_and_others"


def trunk(nc, x, e_norm1, e_w_in, e_sgu_ln_g, e_sgu_ln_b, e_sgu_w, e_sgu_b, e_conv_w, e_a_log,
          e_dt_bias, e_o_norm, e_w_out, e_norm2, e_ffn_w1, e_ffn_w3, e_ffn_w2, o_norm1, o_w_qkv,
          o_w_out, o_norm2, o_router, o_moe_w1, o_moe_w3, o_moe_w2, final_norm, out):
    SEQ, D = x.shape[1], x.shape[2]
    TILES, DC = SEQ // P, D // P
    SGU_W = e_sgu_ln_g.shape[1]
    G = e_sgu_w.shape[1]
    GD = SGU_W // G
    H = e_a_log.shape[1]
    DK = e_o_norm.shape[1]
    KCONV = e_conv_w.shape[1]
    CONV_C = e_conv_w.shape[2] // P
    CH = 64
    NCH = SEQ // CH
    U = H * TILES
    SB_H, SB_D = 16, 64
    FF = e_ffn_w1.shape[2]
    FC = FF // P
    NE = o_router.shape[2]
    CW = 256
    SLOTS = P
    NB = SEQ // SLOTS
    NK = NB * NE
    assert TILES == 2 and DC == 8 and DK == P and U == 8 and FC == 22
    LEVELS = 6
    assert 2 ** LEVELS == CH
    QKV0, GATE0, BA0 = 2 * SGU_W, 2 * SGU_W + CONV_C * P, e_w_in.shape[2] - 2 * H

    R_EVEN, RING, SPLITS = 5, 11, 3
    N_IN, N_OUT, N_QKV = 12, D // CW, 3 * D // CW
    N_QK = 2 * D // CW
    FG = FF // CW
    PER = 3 * FG
    A_OUT, A_FFN = N_IN, N_IN + N_OUT
    A_QKV = A_FFN + PER
    A_WO = A_QKV + N_QKV
    A_MOE = A_WO + N_OUT
    assert PER % RING == 0 and PER % SPLITS == 0 and FG == 11
    HC = DC // 2

    def at_up(g, half):
        return (3 * g - 1 if g else 0) + half

    def at_down(g):
        return 3 * g + 4 if g < FG - 1 else PER - 1

    ITEM = {at_up(g, half): ("up", g, half) for g in range(FG) for half in range(2)}
    ITEM.update({at_down(g): ("down", g, 0) for g in range(FG)})
    assert sorted(ITEM) == list(range(PER))

    ALL_PARTS, HEAD, REST = range(PER), range(2), range(2, PER)
    SCAT_BANKS = (6, 7, 2, 6)

    def slot_of(i):
        return i % R_EVEN if i < A_FFN else (i - A_FFN) % RING

    slots = [slot_of(i) for i in range(A_MOE + PER + SPLITS)]

    def before_it(i):
        same = [m for m in range(i) if slots[m] == slots[i]]
        return same[-1] if same else None

    def arrivals(i):
        return 32 * sum(slots[m] == slots[i] for m in range(i + 1))

    PER_SLOT = 32 * PER // RING

    w_in_cols = [QKV0 + CW * i for i in range(6)] + [GATE0, GATE0 + CW] + [0, CW] + [SGU_W, SGU_W + CW]

    def projection(i):
        if i < A_OUT:
            return e_w_in[0], w_in_cols[i]
        if i < A_FFN:
            return e_w_out[0], CW * (i - A_OUT)
        if i < A_WO:
            return o_w_qkv[0], CW * (i - A_QKV)
        return o_w_out[0], CW * (i - A_WO)

    with ExitStack() as ctx:
        def sb(name, shape, dt=F32, stack=ctx):
            return stack.enter_context(nc.sbuf_tensor(name, shape, dt))

        def sem(name):
            return ctx.enter_context(nc.semaphore(name))

        PIECE = DC * CW
        ring = [sb(f"ring{i}", [P, PIECE]) for i in range(R_EVEN)]
        h = sb("h", [P, TILES, D])
        xn = sb("xn", [P, TILES, D])
        x_hi = sb("x_hi", [P, DC, SEQ], F32R)
        x_lo = sb("x_lo", [P, DC, SEQ], F32R)
        gain = sb("gain", [P, 2, D])
        ident = sb("ident", [P, P])
        ones = sb("ones", [P, P])
        neg_ones = sb("neg_ones", [P, P])
        tri_blk = sb("tri_blk", [P, P])
        blk_ones = sb("blk_ones", [P, P])
        before = sb("before", [P, P])
        neg_after = sb("neg_after", [P, P])
        level = sb("level", [P, LEVELS, P])
        iota = sb("iota", [P, P])
        colt = sb("colt", [P, KCONV * CONV_C + 1])
        stat = sb("stat", [P, 5, 6])
        small = sb("small", [P, 16, TILES, H])
        ba = sb("ba", [P, TILES, 2 * H])
        w_ba = sb("w_ba", [P, DC, 2 * H])
        ba_hi = sb("ba_hi", [P, DC, 2 * H], F32R)
        ba_lo = sb("ba_lo", [P, DC, 2 * H], F32R)
        w_hi = [sb(f"w_hi{i}", [P, PIECE], F32R) for i in range(SPLITS)]
        w_lo = [sb(f"w_lo{i}", [P, PIECE], F32R) for i in range(SPLITS)]
        const = sb("const", [P, 4])
        eps_col, one_col, qscale_col = const[:, 0:1], const[:, 1:2], const[:, 2:3]
        bn = sb("bn", [P, TILES, 6])
        mv = sb("mv", [P, TILES, 2])
        stat_ln = sb("stat_ln", [P, 2, TILES])
        r_small = sb("r_small", [P, 6, TILES])

        even = ExitStack()
        conv_in = sb("conv_in", [P, CONV_C, KCONV - 1 + SEQ], stack=even)
        qkvT = sb("qkvT", [P, CONV_C, SEQ], stack=even)
        yT = sb("yT", [P, DC, SEQ], stack=even)
        v_nat = sb("v_nat", [P, TILES, SGU_W], stack=even)
        wsT = sb("wsT", [P, G, P], stack=even)
        sgu_bias = sb("sgu_bias", [P, G // 2, P], stack=even)
        exp_row = sb("exp_row", [P, H, TILES, P], stack=even)
        kbT = sb("kbT", [P, H, SEQ], stack=even)
        gam = sb("gam", [P, U, P], stack=even)
        attnT = sb("attnT", [P, U, P], stack=even)
        kd = sb("kd", [P, U, P], stack=even)
        rn = sb("rn", [P, 2 * H, SEQ], stack=even)
        even.close()
        state = wsT[:, 0:H, :]
        ws_raw = gam
        rows_raw = kd[:, 0, :]
        inv = conv_in[:, :, :].rearrange("p a b -> p (a b)")[:, 0:3 * U * P].rearrange(
            "p (k u n) -> p k u n", k=3, u=U)
        inv_x, inv_xt, inv_t = inv[:, 0], inv[:, 1], inv[:, 2]
        vb = xn[:, 0, :].rearrange("p (u n) -> p u n", u=U)
        kbe = xn[:, 1, :].rearrange("p (u n) -> p u n", u=U)
        u_sol = rn[:, 0:H, :].rearrange("p h (t n) -> p (h t) n", t=TILES)
        w_solT = rn[:, H:2 * H, :].rearrange("p h (t n) -> p (h t) n", t=TILES)
        v_new = kbT[:, :, :].rearrange("p a b -> p (a b)").rearrange("p (t n) -> p t n", t=TILES)
        oT = qkvT[:, 2 * H:3 * H, :]
        ln_g, ln_b = gain[:, 1, 0:SGU_W], gain[:, 1, SGU_W:2 * SGU_W]

        ring += [sb(f"ring{i}", [P, PIECE]) for i in range(R_EVEN, RING)]
        w_router = sb("w_router", [P, DC, NE])
        wr_hi = sb("wr_hi", [P, DC, NE], F32R)
        wr_lo = sb("wr_lo", [P, DC, NE], F32R)
        odd = ExitStack()
        NZ = 384
        qT = sb("qT", [P, DC, SEQ], stack=odd)
        kT = sb("kT", [P, DC, SEQ], stack=odd)
        sp_m = sb("sp_m", [P, 2, NZ], stack=odd)
        att = sb("att", [P, 2, NZ], stack=odd)
        odd.close()
        lg = level[:, :, :].rearrange("p a b -> p (a b)").rearrange("p (a n) -> p a n", a=2)
        w_log = gain[:, 0, 0:2 * NZ].rearrange("p (a n) -> p a n", a=2)
        v_att = xn
        silu_s = sb("silu_s", [P, TILES, CW])
        h_act = sb("h_act", [P, 2, TILES, CW])
        hT_hi = sb("hT_hi", [P, 2, 2, SEQ], F32R)
        hT_lo = sb("hT_lo", [P, 2, 2, SEQ], F32R)
        sel_p = sb("sel_p", [P, TILES, SLOTS])
        sel_w = sb("sel_w", [P, TILES, SLOTS])
        back = sb("back", [SLOTS, TILES, P])
        y_exp = sb("y_exp", [SLOTS, D])
        logits = sb("logits", [P, TILES, NE])
        rt = y_exp[:, 0:3 * TILES * NE * NE].rearrange("p (k a b) -> p k a b", k=3, a=TILES * NE)
        r2 = sb("r2", [P, 8, TILES, NE])
        table = sb("table", [P, 3, TILES, NK])
        col6 = sb("col6", [P, 3, TILES, 1])
        router_end = 3 * TILES * NE * NE
        li = y_exp[0:1, router_end:router_end + 5 * NE].rearrange("p (a b) -> p a b", a=5)
        li3 = y_exp[0:1, router_end + 5 * NE:router_end + 13 * NE].rearrange("p (a b) -> p a b", a=8)
        item_f = y_exp[0:1, router_end + 13 * NE:router_end + 16 * NE].rearrange("p (a b) -> p a b", a=3)
        item_i = sb("item_i", [1, 3, 8], I32)

        ps = ctx.enter_context(nc.psum_tensor("ps", [P, 8, 512], F32))

        def two(b):
            return ps[:, b:b + 2, :].rearrange("p b n -> p (b n)")

        ld_ba, ld_small, ld_rows, ld_ws, ld_lng, ld_bias, ld_wr = (
            sem(n) for n in ("ld_ba", "ld_small", "ld_rows", "ld_ws", "ld_lng", "ld_bias", "ld_wr"))
        ld_x = [sem("ld_x0"), sem("ld_x1")]
        ld_gain = [sem("ld_gain0"), sem("ld_gain1")]
        ring_in = [sem(f"ring_in{i}") for i in range(RING)]
        hi_done, lo_done, piece_used = sem("hi_done"), sem("lo_done"), sem("piece_used")
        pool_own, act_own, vec_own = sem("pool_own"), sem("act_own"), sem("vec_own")
        consts_ready, pads_ready, ident_ready = sem("consts_ready"), sem("pads_ready"), sem("ident_ready")
        h_ready, rinv_ready, xn_ready, xnT_done = sem("h_ready"), sem("rinv_ready"), sem("xn_ready"), sem("xnT_done")
        xh_ready, xl_ready, yh_ready, yl_ready = sem("xh_ready"), sem("xl_ready"), sem("yh_ready"), sem("yl_ready")
        bah_ready, bal_ready, wrh_ready, wrl_ready = (
            sem(n) for n in ("bah_ready", "bal_ready", "wrh_ready", "wrl_ready"))
        act_evac, oh_hi = sem("act_evac"), sem("oh_hi")
        rows_done, colt_ready, ba_done = sem("rows_done"), sem("colt_ready"), sem("ba_done")
        wsT_done, wsT_ready = sem("wsT_done"), sem("wsT_ready")
        ba_sb, gb_act, gb_vec, g_ready = sem("ba_sb"), sem("gb_act"), sem("gb_vec"), sem("g_ready")
        conv_done, silu_even = sem("conv_done"), sem("silu_even")
        gc_done, gc_sb, row_done, exp_row_ready = sem("gc_done"), sem("gc_sb"), sem("row_done"), sem("exp_row_ready")
        gcols_act, kbe_scale = sem("gcols_act"), sem("kbe_scale")
        sq_ready, l2_done, rn_ready, qk_ready = sem("sq_ready"), sem("l2_done"), sem("rn_ready"), sem("qk_ready")
        kb_ready, gam_arg, gam_exp, kk_done, attn_ready, lt_ready = (
            sem(n) for n in ("kb_ready", "gam_arg", "gam_exp", "kk_done", "attn_ready", "lt_ready"))
        qd_ready, turn_done, vb_ready, kbe_ready, kd_ready = (
            sem(n) for n in ("qd_ready", "turn_done", "vb_ready", "kbe_ready", "kd_ready"))
        t_done, t_ready, x_done, x_ready, xt_done, xt_ready = (
            sem(n) for n in ("t_done", "t_ready", "x_done", "x_ready", "xt_done", "xt_ready"))
        sol_done, sol_u, sol_w = sem("sol_done"), sem("sol_u"), sem("sol_w")
        ws_done, vnew_ready, o_done, o_sb, st_done, st_ready = (
            sem(n) for n in ("ws_done", "vnew_ready", "o_done", "o_sb", "st_done", "st_ready"))
        osq_ready, on_done, on_ready, yb_ready = sem("osq_ready"), sem("on_done"), sem("on_ready"), sem("yb_ready")
        gelu_v, ln_var, ln_rstd, v_ready, mix_done, ya_ready = (
            sem(n) for n in ("gelu_v", "ln_var", "ln_rstd", "v_ready", "mix_done", "ya_ready"))
        silu_done, act_ready, hT_done, hTh_ready, hTl_ready = (
            sem(n) for n in ("silu_done", "act_ready", "hT_done", "hTh_ready", "hTl_ready"))
        z_done, log_ready, sp_ready, w_ready, spm_ready = (
            sem(n) for n in ("z_done", "log_ready", "sp_ready", "w_ready", "spm_ready"))
        after_done, la_ready, att_exp, att_ready, oh_done, oh_ready = (
            sem(n) for n in ("after_done", "la_ready", "att_exp", "att_ready", "oh_done", "oh_ready"))
        lgt_done, r_exp, r_d, sel_ready, pos_done, table_ready, items_ready = (
            sem(n) for n in ("lgt_done", "r_exp", "r_d", "sel_ready", "pos_done", "table_ready", "items_ready"))
        prep_col, prep_done, gather_done, back_done, xgh_ready, xgl_ready, back_ready = (
            sem(n) for n in ("prep_col", "prep_done", "gather_done", "back_done", "xgh_ready", "xgl_ready", "back_ready"))
        y_act, y_vec, scat_done, scat_added = sem("y_act"), sem("y_vec"), sem("scat_done"), sem("scat_added")
        out_ready, out_sem = sem("out_ready"), sem("out_sem")

        block = ctx.enter_context(nc.Block())

        def used(eng, i, n=None):
            eng.wait_ge(piece_used, i + 1 if n is None else n * PER + (i + 1))

        def count(n, per, c):
            return c if n is None else n * per + c

        def product(pe, o, a_hi, a_lo, b_hi, b_lo, first, last):
            pe.matmul(o, a_hi, b_hi, start=first, stop=False)
            pe.matmul(o, a_hi, b_lo, start=False, stop=False)
            return pe.matmul(o, a_lo, b_hi, start=False, stop=last)

        @block.sync
        def _(sp):
            for t in range(TILES):
                sp.dma_start(h[:, t, :], x[0, t * P:(t + 1) * P, :]).then_inc(ld_x[t], 16)

            def load_projection(i):
                w, c0 = projection(i)
                dst = ring[slots[i]][:, :].rearrange("p (c n) -> p c n", c=DC)
                for m in range(2):
                    src = w[m * HC * P:(m + 1) * HC * P, c0:c0 + CW].rearrange("(c p) n -> p c n", p=P)
                    sp.dma_start(dst[:, m * HC:(m + 1) * HC, :], src).then_inc(ring_in[slots[i]], 16)

            def item_sources(p, w1, w3, w2):
                kind, g, half = ITEM[p]
                if kind == "up":
                    rows, cs = slice(half * HC * P, (half + 1) * HC * P), slice(g * CW, (g + 1) * CW)
                    return [(m, w, rows, cs) for m, w in enumerate((w1, w3))]
                return [(m, w2, slice((2 * g + m) * P, (2 * g + m + 1) * P), slice(0, D)) for m in range(2)]

            def destination(i, p, m):
                t = ring[slots[i]]
                if ITEM[p][0] == "up":
                    return t[:, :].rearrange("p (c w n) -> p c w n", c=HC, w=2)[:, :, m, :]
                return t[:, m * D:(m + 1) * D]

            for i in range(A_MOE):
                last = before_it(i)
                if last is not None:
                    sp.wait_ge(lo_done, last + 1)
                elif i >= A_FFN:
                    used(sp, A_FFN - 1)
                if A_FFN <= i < A_QKV:
                    for m, w, rows, cs in item_sources(i - A_FFN, e_ffn_w1, e_ffn_w3, e_ffn_w2):
                        src = w[0, rows, cs]
                        if ITEM[i - A_FFN][0] == "up":
                            src = src.rearrange("(c p) n -> p c n", p=P)
                        sp.dma_start(destination(i, i - A_FFN, m), src).then_inc(ring_in[slots[i]], 16)
                else:
                    load_projection(i)

            def load_item(n, e):
                for p in range(PER):
                    i = A_MOE + p
                    need = before_it(i) + 1 if isinstance(n, int) and n == 0 else sp.snap(n * PER + (A_MOE + p - RING + 1))
                    sp.wait_ge(lo_done, need)
                    for m, w, rows, cs in item_sources(p, o_moe_w1, o_moe_w3, o_moe_w2):
                        src = w[0][bass.ds(e, 1), rows, cs]
                        if ITEM[p][0] == "up":
                            src = src.rearrange("e (c p) n -> p (e c) n", p=P)
                        else:
                            src = src.rearrange("e p d -> p (e d)")
                        sp.dma_start(destination(i, p, m), src).then_inc(ring_in[slots[i]], 16)

            with sp.Fori(0, NE) as e:
                load_item(e, e)
            sp.wait_ge(items_ready, 1)
            n_more = sp.value_load(item_i[0:1, 0, 0:1], min_val=0, max_val=7)
            with sp.If(n_more > 0):
                with sp.Fori(0, n_more) as it:
                    e = sp.value_load(item_i[0:1, 2, bass.ds(it, 1)], min_val=0, max_val=NE - 1)
                    load_item(it + NE, e)
            for t in range(TILES):
                sp.wait_ge(out_ready, t + 1)
                sp.dma_start(out[0, t * P:(t + 1) * P, :], xn[:, t, :]).then_inc(out_sem, 16)
            sp.wait_ge(out_sem, 16 * TILES)

        @block.gpsimd
        def _(pool):
            own = [0]

            def after(ins):
                own[0] += 1
                ins.then_inc(pool_own, 1)
                pool.wait_ge(pool_own, own[0])

            def keep(t, pattern, base, cm, op=ALU.is_ge, fill=0.0):
                after(pool.affine_select(out=t, in_=t, pattern=pattern, compare_op=op, fill=fill, base=base,
                                         channel_multiplier=cm))

            def gain_load(k, g):
                if k >= 2:
                    pool.wait_ge(xn_ready, TILES * (k - 1))
                if k == 1:
                    pool.wait_ge(v_ready, TILES)
                pool.dma_start(gain[:, k % 2, :], g.partition_broadcast(P)).then_inc(ld_gain[k % 2], 16)

            gain_load(0, e_norm1[0])
            after(pool.memset(ident[:, :], 0.0))
            pool.affine_select(out=ident[:, :], in_=ident[:, :], pattern=[[-1, P]], compare_op=ALU.not_equal, fill=1.0,
                               base=0, channel_multiplier=1).then_inc(ident_ready, 1)
            pool.dma_start(w_ba[:, :, :], e_w_in[0][:, BA0:BA0 + 2 * H].rearrange("(c p) n -> p c n", p=P)).then_inc(ld_ba, 16)
            pool.dma_start(rows_raw[0:KCONV * CONV_C, :], e_conv_w[0].rearrange("k (c p) -> (k c) p", p=P)).then_inc(ld_rows, 16)
            pool.dma_start(rows_raw[KCONV * CONV_C:KCONV * CONV_C + 1, :], e_o_norm).then_inc(ld_rows, 16)
            pool.dma_start(small[:, 0, 0, :], e_dt_bias[0].partition_broadcast(P)).then_inc(ld_small, 16)
            pool.dma_start(small[:, 0, 1, :], e_a_log[0].partition_broadcast(P)).then_inc(ld_small, 16)
            pool.memset(conv_in[:, :, 0:KCONV - 1], 0.0).then_inc(pads_ready, 1)
            pool.memset(ones[:, :], 1.0)
            pool.memset(neg_ones[:, :], -1.0)
            after(pool.memset(before[:, :], 1.0))
            keep(before[:, :], [[1, P]], -1, -1)
            after(pool.memset(neg_after[:, :], -1.0))
            keep(neg_after[:, :], [[-1, P]], -1, 1)
            after(pool.memset(blk_ones[:, :], 1.0))
            halves = blk_ones[:, :].rearrange("p (a n) -> p a n", n=CH)
            keep(halves, [[-CH, P // CH], [0, CH]], 0, 1)
            keep(halves, [[CH, P // CH], [0, CH]], CH - 1, -1)
            after(pool.affine_select(out=tri_blk[:, :], in_=blk_ones[:, :], pattern=[[1, P]], compare_op=ALU.is_ge,
                                     fill=0.0, base=0, channel_multiplier=-1))
            after(pool.memset(level[:, :, :], 0.0))
            for k in range(LEVELS):
                b = 2 ** k
                v = level[:, k, :].rearrange("p (a n) -> p a n", n=2 * b)[:, :, 0:b]
                after(pool.memset(v, 1.0))
                keep(v, [[-2 * b, P // (2 * b)], [0, b]], -b, 1)
                keep(v, [[2 * b, P // (2 * b)], [0, b]], 2 * b - 1, -1)
            pool.iota(iota[:, :], [[1, P]], base=0, channel_multiplier=0,
                      allow_small_or_imprecise_dtypes=True).then_inc(pool_own, 1)
            own[0] += 1
            after(pool.memset(ws_raw[0:CH, :, CH:P], 0.0))
            pool.drain().then_inc(consts_ready, 1)
            w = e_sgu_w[0].rearrange("g t s -> t g s")
            pool.dma_start(ws_raw[0:CH, :, 0:CH], w[0:CH, :, 0:CH]).then_inc(ld_ws, 16)
            pool.dma_start(ws_raw[CH:P, :, :], w[CH:P]).then_inc(ld_ws, 16)
            pool.dma_start(ln_g, e_sgu_ln_g[0].partition_broadcast(P)).then_inc(ld_lng, 16)
            pool.dma_start(ln_b, e_sgu_ln_b[0].partition_broadcast(P)).then_inc(ld_lng, 16)
            for m in range(2):
                b = e_sgu_b[0].rearrange("(c m) t -> m c t", m=2)[m].partition_broadcast(CH)
                pool.dma_start(sgu_bias[m * CH:(m + 1) * CH, :, :], b).then_inc(ld_bias, 16)
            gain_load(1, e_norm2[0])
            gain_load(2, o_norm1[0])
            gain_load(3, o_norm2[0])
            used(pool, A_FFN - 1)
            pool.dma_start(w_router[:, :, :], o_router[0].rearrange("(c p) e -> p c e", p=P)).then_inc(ld_wr, 16)
            mask2 = before[:, :].unsqueeze(1).to_broadcast([P, 2, P])

            def diag(t):
                return t[:, 0:2 * P].rearrange("p (a n) -> p a n", a=2)

            def mask_sp(i):
                pool.wait_ge(sp_ready, i + 1)
                pool.tensor_tensor(diag(sp_m[:, i % 2]), diag(sp_m[:, i % 2]), mask2, ALU.mult).then_inc(spm_ready, 1)

            def mask_att(i):
                pool.wait_ge(att_exp, i + 1)
                pool.tensor_tensor(diag(att[:, i % 2]), diag(att[:, i % 2]), mask2, ALU.mult).then_inc(att_ready, 1)

            for i in range(SB_H + 1):
                if i < SB_H:
                    mask_sp(i)
                if i >= 1:
                    mask_att(i - 1)
            pool.wait_ge(att_exp, SB_H)
            gain_load(4, final_norm)

        @block.scalar
        def _(act):
            own = [0]

            def after(ins):
                own[0] += 1
                ins.then_inc(act_own, 1)
                act.wait_ge(act_own, own[0])

            def norm(k, transposed=True, between=None):
                for t in range(TILES):
                    if k:
                        act.wait_ge(h_ready, TILES * (k - 1) + t + 1)
                    else:
                        act.wait_ge(ld_x[t], 16)
                    after(act.activation(xn[:, t, :], h[:, t, :], ACT.Square, accum_out=stat[:, k, t:t + 1]))
                    after(act.activation(stat[:, k, 2 + t:3 + t], stat[:, k, t:t + 1], ACT.Ln, scale=1.0 / D, bias=eps_col))
                    act.activation(stat[:, k, 4 + t:5 + t], stat[:, k, 2 + t:3 + t], ACT.Exp, scale=-0.5).then_inc(rinv_ready, 1)
                if between is not None:
                    between()
                if transposed:
                    for b in range(4):
                        act.wait_ge(xnT_done, 4 * k + b + 1)
                        act.activation(x_hi[:, 2 * b:2 * b + 2, :], ps[:, b, :].rearrange("p (c n) -> p c n", c=2),
                                       ACT.Copy).then_inc(xh_ready, 1)

            def split_hi(i, n=None):
                if n is None:
                    act.wait_ge(ring_in[slots[i]], arrivals(i))
                    if i >= SPLITS:
                        used(act, i - SPLITS)
                else:
                    act.wait_ge(ring_in[slots[i]], n * PER_SLOT + arrivals(i))
                    used(act, i - SPLITS, n)
                act.activation(w_hi[i % SPLITS][:, :], ring[slots[i]][:, :], ACT.Copy).then_inc(hi_done, 1)

            act.wait_ge(vec_own, 1)
            act.preload_act_table_set(EXP_LN)
            norm(0)
            act.wait_ge(ld_ba, 16)
            act.activation(ba_hi[:, :, :], w_ba[:, :, :], ACT.Copy).then_inc(bah_ready, 1)
            for i in range(SPLITS):
                split_hi(i)
            act.wait_ge(ba_sb, 1)
            act.activation(small[:, 1], ba[:, :, 0:H], ACT.Exp, scale=-1.0).then_inc(gb_act, 1)
            act.wait_ge(ld_small, 32)
            act.activation(small[:, 2, 0, :], small[:, 0, 1, :], ACT.Exp).then_inc(gb_act, 1)
            act.wait_ge(gb_vec, 1)
            after(act.activation(small[:, 5], small[:, 4], ACT.Exp, scale=-1.0))
            act.activation(small[:, 6], small[:, 5], ACT.Ln, bias=one_col).then_inc(gb_act, 1)

            act.preload_act_table(ACT.Silu)
            def copy_conv(i):
                used(act, i)
                if i == 0:
                    act.wait_ge(pads_ready, 1)
                act.activation(conv_in[:, 2 * i:2 * i + 2, KCONV - 1:], ps[:, i % 4, :].rearrange("p (c n) -> p c n", c=2),
                               ACT.Copy).then_inc(act_evac, 1)

            def silu_conv(i):
                act.wait_ge(conv_done, i + 1)
                act.activation(qkvT[:, 2 * i:2 * i + 2, :], qkvT[:, 2 * i:2 * i + 2, :], ACT.Silu).then_inc(silu_even, 1)

            for i in range(6):
                copy_conv(i)
                split_hi(i + SPLITS)
                if i >= 1:
                    silu_conv(i - 1)
            silu_conv(5)
            for i in (6, 7):
                used(act, i)
                act.activation(yT[:, 4 + 2 * (i - 6):6 + 2 * (i - 6), :], ps[:, i % 4, :].rearrange("p (c n) -> p c n", c=2),
                               ACT.Silu).then_inc(act_evac, 1)
                split_hi(i + SPLITS)

            act.preload_act_table_set(EXP_LN)
            act.wait_ge(silu_even, 4)
            act.activation(rn[:, :, :], qkvT[:, 0:2 * H, :], ACT.Square).then_inc(sq_ready, 1)
            act.wait_ge(gc_sb, 1)
            act.wait_ge(row_done, 1)
            act.activation(exp_row[:, :, :, :].rearrange("p h t n -> p (h t n)"), two(4), ACT.Exp).then_inc(exp_row_ready, 1)
            act.activation(small[:, 10], small[:, 8], ACT.Exp).then_inc(gcols_act, 1)
            act.activation(small[:, 12], small[:, 11], ACT.Exp).then_inc(gcols_act, 1)
            act.wait_ge(l2_done, 1)
            flat = rn[:, :, :].rearrange("p a b -> p (a b)")
            after(act.activation(flat, ps[:, 0:4, :].rearrange("p b n -> p (b n)"), ACT.Ln, bias=eps_col))
            half = H * SEQ
            act.activation(flat[:, 0:half], flat[:, 0:half], ACT.Exp, scale=-0.5, bias=qscale_col).then_inc(rn_ready, 1)
            act.activation(flat[:, half:], flat[:, half:], ACT.Exp, scale=-0.5).then_inc(rn_ready, 1)
            act.wait_ge(gam_arg, U)
            act.activation(gam[:, :, :], gam[:, :, :], ACT.Exp).then_inc(gam_exp, 1)
            split_hi(11)

            act.preload_act_table(ACT.Gelu_apprx_tanh)
            for i in (8, 9):
                used(act, i)
                act.activation(yT[:, 2 * (i - 8):2 + 2 * (i - 8), :], ps[:, i % 4, :].rearrange("p (c n) -> p c n", c=2),
                               ACT.Gelu_apprx_tanh).then_inc(act_evac, 1)
            for i in (10, 11):
                used(act, i)
                act.activation(v_nat[:, :, (i - 10) * CW:(i - 9) * CW], ps[:, i % 4, :].rearrange("p (t n) -> p t n", t=TILES),
                               ACT.Gelu_apprx_tanh).then_inc(act_evac, 1)
            for i in (12, 13, 14):
                split_hi(i)
            act.preload_act_table_set(EXP_LN)
            act.wait_ge(ln_var, 1)
            after(act.activation(stat_ln[:, 0, :], mv[:, :, 1], ACT.Ln, bias=eps_col))
            act.activation(stat_ln[:, 1, :], stat_ln[:, 0, :], ACT.Exp, scale=-0.5).then_inc(ln_rstd, 1)
            act.wait_ge(turn_done, 1)
            act.wait_ge(gcols_act, 2)
            for u in range(U):
                hd, t = u // TILES, u % TILES
                act.activation(kd[:, u, :], two(0)[:, u * P:(u + 1) * P], ACT.Copy,
                               scale=small[:, 12, t, hd:hd + 1]).then_inc(kd_ready, 1)
            act.wait_ge(kbe_scale, 1)
            for u in range(U):
                hd, t = u // TILES, u % TILES
                act.activation(kbe[:, u, :], two(0)[:, u * P:(u + 1) * P], ACT.Copy,
                               scale=small[:, 13, t, hd:hd + 1]).then_inc(kbe_ready, 1)
            act.wait_ge(sol_done, 1)
            act.activation(w_solT.rearrange("p u n -> p (u n)"), two(4), ACT.Copy).then_inc(sol_w, 1)
            act.wait_ge(ya_ready, 1)
            act.activation(x_hi[:, 0:4, :], yT[:, 0:4, :], ACT.Copy).then_inc(yh_ready, 1)
            for c in range(NCH):
                act.wait_ge(o_done, c + 1)
                act.activation(oT[:, :, c * CH:(c + 1) * CH], ps[:, (7, 3)[c % 2], 0:H * CH].rearrange("p (h n) -> p h n", h=H),
                               ACT.Copy).then_inc(o_sb, 1)
            act.wait_ge(o_sb, NCH)
            act.activation(rn[:, 0:H, :], oT, ACT.Square).then_inc(osq_ready, 1)
            act.wait_ge(on_done, 1)
            after(act.activation(rn[:, H:2 * H, :].rearrange("p a b -> p (a b)"), two(0), ACT.Ln, scale=1.0 / DK, bias=eps_col))
            act.activation(rn[:, H:2 * H, :], rn[:, H:2 * H, :], ACT.Exp, scale=-0.5).then_inc(on_ready, 1)

            act.wait_ge(yb_ready, 1)
            act.activation(x_hi[:, 4:8, :], yT[:, 4:8, :], ACT.Copy).then_inc(yh_ready, 1)
            for i in (15, 16, 17):
                split_hi(i)
            norm(1)
            split_hi(18)

            def ffn(tiles, first, unit0, group0, ahead, n=None, parts=ALL_PARTS, extra={}):
                def silu(g):
                    used(act, first + at_up(g, 1), n)
                    for t in range(tiles):
                        bank = 4 + (tiles * g + t) % (tiles + 1)
                        if tiles * g + t >= 1 or n is not None:
                            act.wait_ge(act_ready, count(n, FG, unit0 + tiles * (g - 1) + t + 1))
                        act.activation(silu_s[:, t, :], ps[:, bank, 0:CW], ACT.Silu).then_inc(silu_done, 1)

                def turned(g):
                    act.wait_ge(hT_done, count(n, FG, group0 + g + 1))
                    if g >= 2:
                        used(act, first + at_down(g - 2), n)
                    act.activation(hT_hi[:, g % 2, :, 0:tiles * P], ps[:, 7 if tiles == 2 else 3, 0:2 * tiles * P].rearrange(
                        "p (j n) -> p j n", j=2), ACT.Copy).then_inc(hTh_ready, 1)

                for p in parts:
                    kind, g, half = ITEM[p]
                    if kind == "up" and half == 1:
                        silu(g)
                    if kind == "up" and half == 0 and g >= 1:
                        turned(g - 1)
                    if p in extra:
                        extra[p]()
                    if p + SPLITS < PER + ahead:
                        split_hi(first + p + SPLITS, n)
                    if p == PER - 2:
                        turned(FG - 1)

            act.preload_act_table(ACT.Silu)
            ffn(TILES, A_FFN, 0, 0, SPLITS - 1)

            act.preload_act_table_set(EXP_LN)
            norm(2, between=lambda: split_hi(A_QKV + SPLITS - 1))
            for i in range(N_QK):
                used(act, A_QKV + i)
                src = ps[:, i % 4, :].rearrange("p (c n) -> p c n", c=2)
                if i < 4:
                    ins = act.activation(qT[:, 2 * i:2 * i + 2, :], src, ACT.Copy, scale=float(SB_D) ** -0.5)
                else:
                    ins = act.activation(kT[:, 2 * i - 8:2 * i - 6, :], src, ACT.Copy)
                ins.then_inc(act_evac, 1)
                split_hi(A_QKV + i + SPLITS)
            def log_part(i):
                act.wait_ge(z_done, i + 1)
                if i >= 2:
                    act.wait_ge(w_ready, i - 1)
                after(act.activation(lg[:, i % 2], ps[:, i % 2, 0:NZ], ACT.Abs))
                after(act.activation(lg[:, i % 2], lg[:, i % 2], ACT.Exp, scale=-1.0))
                act.activation(lg[:, i % 2], lg[:, i % 2], ACT.Ln, bias=one_col).then_inc(log_ready, 1)

            def att_part(i):
                act.wait_ge(la_ready, i + 1)
                if i >= 2:
                    act.wait_ge(oh_done, i - 1)
                act.activation(att[:, i % 2], w_log[:, i % 2], ACT.Exp).then_inc(att_exp, 1)

            def evac_v(j):
                used(act, A_QKV + N_QK + j)
                act.activation(v_att[:, :, j * CW:(j + 1) * CW], ps[:, 2, :].rearrange("p (t n) -> p t n", t=TILES),
                               ACT.Copy).then_inc(act_evac, 1)
                split_hi(A_QKV + N_QK + j + SPLITS)

            def head_hi(pr):
                act.wait_ge(oh_done, 2 * pr + 2)
                if pr == 0:
                    used(act, A_WO - 1)
                act.activation(x_hi[:, pr, :], ps[:, 6 + pr % 2, 0:SEQ], ACT.Copy).then_inc(oh_hi, 1)

            for i in range(SB_H + 2):
                if i < SB_H:
                    log_part(i)
                if i >= 2:
                    att_part(i - 2)
                if 1 <= i <= N_QKV - N_QK:
                    evac_v(i - 1)
                if i >= 5 and i % 2 == 1:
                    head_hi((i - 5) // 2)
            head_hi(SB_H // 2 - 1)
            act.wait_ge(ld_wr, 16)
            act.activation(wr_hi[:, :, :], w_router[:, :, :], ACT.Copy).then_inc(wrh_ready, 1)
            for i in range(A_MOE - 1, A_MOE + 2):
                split_hi(i)
            norm(3)
            split_hi(A_MOE + 2)
            act.wait_ge(r_d, 1)
            act.activation(r_small[:, 1], r_small[:, 0], ACT.Exp).then_inc(r_exp, 1)
            act.preload_act_table(ACT.Silu)

            def evac_y(n):
                used(act, A_MOE + PER - 1, n)
                act.activation(y_exp[:, 512:D], ps[0:SLOTS, 1, :], ACT.Copy).then_inc(y_act, 1)

            def evac_xg(k):
                act.wait_ge(gather_done, k + 1)
                for b in range(2):
                    act.activation(x_hi[:, 4 * b:4 * b + 4, 0:SLOTS], ps[:, 6 + b, :].rearrange("p (c n) -> p c n", c=4),
                                   ACT.Copy).then_inc(xgh_ready, 1)

            def expert(n, ahead, parts):
                def before_end():
                    if ahead:
                        evac_xg(n + 1)
                    evac_y(n)
                ffn(1, A_MOE, TILES * FG, FG, ahead, n, parts, {PER - 1: before_end})

            evac_xg(0)
            expert(0, SPLITS, HEAD)
            with act.Fori(0, NE - 1) as n:
                expert(n, SPLITS, REST)
                expert(n + 1, SPLITS, HEAD)
            expert(NE - 1, 0, REST)
            act.wait_ge(items_ready, 1)
            n_more = act.value_load(item_i[0:1, 0, 0:1], min_val=0, max_val=7)
            with act.If(n_more > 0):
                with act.Fori(0, n_more) as it:
                    for p in range(SPLITS):
                        split_hi(A_MOE + p, it + NE)
                    evac_xg(it + NE)
                    expert(it + NE, 0, ALL_PARTS)
            act.preload_act_table_set(EXP_LN)
            norm(4, False)

        @block.tensor
        def _(pe):
            mm = pe.matmul

            def norm_turn(k):
                if k == 0:
                    pe.wait_ge(ident_ready, 1)
                for t in range(TILES):
                    pe.wait_ge(xn_ready, TILES * k + t + 1)
                    for b in range(4):
                        for c in (2 * b, 2 * b + 1):
                            at = (c % 2) * SEQ + t * P
                            last = pe.transpose(ps[:, b, at:at + P], xn[:, t, c * P:(c + 1) * P], ident[:, :])
                        if t == TILES - 1:
                            last.then_inc(xnT_done, 1)

            def x_columns(k):
                pe.wait_ge(xl_ready, 4 * (k + 1))

            def piece(i, **dims):
                pe.wait_ge(lo_done, i + 1)
                return [w[i % SPLITS][:, :].rearrange("p (c n) -> p c n", c=DC) for w in (w_hi, w_lo)]

            def project_T(i, bank):
                hi, lo = piece(i)
                for m in range(2):
                    ms = slice(m * P, (m + 1) * P)
                    for c in range(DC):
                        last = product(pe, ps[:, bank, m * SEQ:(m + 1) * SEQ], hi[:, c, ms], lo[:, c, ms], x_hi[:, c, :],
                                       x_lo[:, c, :], c == 0, c == DC - 1)
                last.then_inc(piece_used, 1)

            def project_N(i, bank):
                hi, lo = piece(i)
                for t in range(TILES):
                    tok = slice(t * P, (t + 1) * P)
                    for c in range(DC):
                        last = product(pe, ps[:, bank, t * CW:(t + 1) * CW], x_hi[:, c, tok], x_lo[:, c, tok], hi[:, c, :],
                                       lo[:, c, :], c == 0, c == DC - 1)
                last.then_inc(piece_used, 1)

            def narrow(o, hi, lo):
                n = hi.shape[2]
                for t in range(TILES):
                    tok = slice(t * P, (t + 1) * P)
                    for c in range(DC):
                        last = product(pe, o[:, t * n:(t + 1) * n], x_hi[:, c, tok], x_lo[:, c, tok], hi[:, c, :],
                                       lo[:, c, :], c == 0, c == DC - 1)
                return last

            norm_turn(0)
            n_rows = KCONV * CONV_C + 1
            pe.wait_ge(ld_rows, 32)
            pe.transpose(ps[:, 6, 0:n_rows], rows_raw[0:n_rows, :], ident[0:n_rows, 0:n_rows]).then_inc(rows_done, 1)
            pe.wait_ge(bal_ready, 1)
            x_columns(0)
            narrow(ps[:, 7], ba_hi, ba_lo).then_inc(ba_done, 1)
            pe.wait_ge(ld_ws, 32)
            for g in range(G):
                last = pe.transpose(two(4)[:, g * P:(g + 1) * P], ws_raw[:, g, :], ident[:, :])
            last.then_inc(wsT_done, 1)

            def decay_rows():
                pe.wait_ge(consts_ready, 1)
                pe.wait_ge(g_ready, 1)
                pe.wait_ge(wsT_ready, 1)
                g = small[:, 7].rearrange("p t h -> p (t h)")
                mm(ps[:, 6, 0:U], tri_blk[:, :], g, start=True, stop=True)
                mm(ps[:, 6, U:2 * U], blk_ones[:, :], g, start=True, stop=True).then_inc(gc_done, 1)
                for u in range(U):
                    last = mm(two(4)[:, u * P:(u + 1) * P], small[:, 7, u % TILES, u // TILES:u // TILES + 1].to_broadcast([P, P]),
                              tri_blk[:, :], start=True, stop=True)
                last.then_inc(row_done, 1)
                pe.wait_ge(gc_sb, 1)
                for u in range(U):
                    last = mm(two(6)[:, u * P:(u + 1) * P], small[:, 3, u % TILES, u // TILES:u // TILES + 1].to_broadcast([P, P]),
                              ident[:, :], start=True, stop=True)
                last.then_inc(row_done, 1)

            for i in range(8):
                if i >= 4:
                    pe.wait_ge(act_evac, i - 3)
                project_T(i, i % 4)
                if i == 2:
                    decay_rows()
            pe.wait_ge(sq_ready, 1)
            pe.wait_ge(act_evac, 8)
            for b in range(4):
                last = mm(ps[:, b, :], ones[:, :], rn[:, 2 * b:2 * b + 2, :].rearrange("p a b -> p (a b)"), start=True, stop=True)
            last.then_inc(l2_done, 1)
            pe.wait_ge(rn_ready, 1)
            for i in (8, 9):
                project_T(i, i % 4)
            for i in (10, 11):
                project_N(i, i % 4)
            pe.wait_ge(kb_ready, 2)
            pe.wait_ge(gam_arg, U)
            pe.wait_ge(exp_row_ready, 1)
            for m, src in enumerate((kbT, qkvT)):
                for u in range(U):
                    hd, t = u // TILES, u % TILES
                    last = mm(two(4 + 2 * m)[:, u * P:(u + 1) * P], qkvT[:, H + hd, t * P:(t + 1) * P],
                              src[:, hd, t * P:(t + 1) * P], start=True, stop=True)
                last.then_inc(kk_done, 1)
            pe.wait_ge(act_evac, 12)
            for m in range(2):
                for u in range(U):
                    hd, t = u // TILES, u % TILES
                    last = pe.transpose(two(2 * m)[:, u * P:(u + 1) * P], qkvT[:, (1 + m) * H + hd, t * P:(t + 1) * P],
                                        ident[:, :])
                last.then_inc(turn_done, 1)

            def gate_mix():
                pe.wait_ge(v_ready, TILES)
                pe.wait_ge(kd_ready, U)
                pe.wait_ge(kbe_ready, U)
                for t in range(TILES):
                    for g in range(G):
                        at = (g // 2) * SEQ + t * P
                        last = mm(two(0)[(g % 2) * GD:(g % 2 + 1) * GD, at:at + P], v_nat[:, t, g * GD:(g + 1) * GD],
                                  wsT[:, g, :], start=True, stop=True)
                last.then_inc(mix_done, 1)

            pe.wait_ge(lt_ready, 1)
            pe.wait_ge(attn_ready, 1)
            pe.wait_ge(vb_ready, U)
            for k in range(LEVELS):
                for hf in range(2):
                    if k:
                        pe.wait_ge(x_ready, 2 * k + hf - 1)
                    for m in range(4):
                        u = 4 * hf + m
                        last = mm(ps[:, 4 + hf, m * P:(m + 1) * P], gam[:, u, :], inv_x[:, u, :] if k else ident[:, :],
                                  start=True, stop=True)
                    last.then_inc(t_done, 1)
                for hf in range(2):
                    pe.wait_ge(t_ready, 2 * k + hf + 1)
                    if k:
                        pe.wait_ge(xt_ready, 2 * k + hf - 1)
                    if k < LEVELS - 1:
                        for m in range(4):
                            u = 4 * hf + m
                            last = mm(ps[:, 6 + hf, m * P:(m + 1) * P], inv_xt[:, u, :] if k else ident[:, :],
                                      inv_t[:, u, :], start=True, stop=True)
                        last.then_inc(x_done, 1)
                    for m in range(4):
                        u = 4 * hf + m
                        last = mm(ps[:, 2 + hf, m * P:(m + 1) * P], inv_t[:, u, :], inv_xt[:, u, :] if k else ident[:, :],
                                  start=True, stop=True)
                    last.then_inc(xt_done, 1)
                if k == 2:
                    gate_mix()
            pe.wait_ge(xt_ready, 2 * LEVELS)
            pe.wait_ge(ya_ready, 1)
            for u in range(U):
                last = mm(two(4)[:, u * P:(u + 1) * P], kbe[:, u, :], inv_xt[:, u, :], start=True, stop=True)
            last.then_inc(sol_done, 1)
            for u in range(U):
                last = mm(two(0)[:, u * P:(u + 1) * P], inv_xt[:, u, :], vb[:, u, :], start=True, stop=True)
            last.then_inc(sol_done, 1)
            pe.wait_ge(sol_w, 1)
            pe.wait_ge(qd_ready, 1)
            for c in range(NCH):
                t, p0 = c // 2, (c % 2) * CH
                rows, tok = slice(p0, p0 + CH), slice(c * CH, (c + 1) * CH)
                if c:
                    pe.wait_ge(st_ready, c)
                    for hd in range(H):
                        last = mm(ps[rows, 6, hd * P:(hd + 1) * P], w_solT[:, hd * TILES + t, rows], state[:, hd, :],
                                  start=True, stop=True)
                    last.then_inc(ws_done, 1)
                pe.wait_ge(vnew_ready, c + 1)
                if c < NCH - 1:
                    for hd in range(H):
                        last = mm(ps[:, 2, hd * P:(hd + 1) * P], kd[rows, hd * TILES + t, :],
                                  v_new[rows, t, hd * P:(hd + 1) * P], start=True, stop=True)
                    last.then_inc(st_done, 1)
                if c >= 2:
                    pe.wait_ge(o_sb, c - 1)
                for hd in range(H):
                    o = ps[:, (7, 3)[c % 2], hd * CH:(hd + 1) * CH]
                    if c:
                        mm(o, state[:, hd, :], qkvT[:, hd, tok], start=True, stop=False)
                    last = mm(o, v_new[rows, t, hd * P:(hd + 1) * P], attnT[rows, hd * TILES + t, rows],
                              start=(c == 0), stop=True)
                last.then_inc(o_done, 1)
            pe.wait_ge(osq_ready, 1)
            for b in range(2):
                last = mm(ps[:, b, :], ones[:, :], rn[:, 2 * b:2 * b + 2, :].rearrange("p a b -> p (a b)"), start=True, stop=True)
            last.then_inc(on_done, 1)
            pe.wait_ge(yl_ready, 2)
            for i in range(A_OUT, A_FFN):
                project_N(i, i % 4)

            def ffn(tiles, first, unit0, group0, x, n=None, between=None, parts=ALL_PARTS):
                nb, t_bank = tiles + 1, 7 if tiles == 2 else 3

                def up(g, half):
                    i = first + at_up(g, half)
                    pe.wait_ge(lo_done, count(n, PER, i + 1))
                    hi, lo = (w[i % SPLITS][:, :].rearrange("p (c n) -> p c n", c=HC) for w in (w_hi, w_lo))
                    for t in range(tiles):
                        u = tiles * g + t
                        if half == 0 and (u >= nb or n is not None):
                            pe.wait_ge(act_ready, count(n, FG, unit0 + max(u - nb + 1, 0)))
                        tok = slice(t * P, (t + 1) * P)
                        for c in range(HC):
                            cc = half * HC + c
                            last = product(pe, ps[:, 4 + u % nb, :], x[0][:, cc, tok], x[1][:, cc, tok], hi[:, c, :],
                                           lo[:, c, :], cc == 0, cc == DC - 1)
                    last.then_inc(piece_used, 1)

                def turn(g):
                    pe.wait_ge(act_ready, count(n, FG, unit0 + tiles * (g + 1)))
                    if n is not None and g == 0:
                        pe.wait_ge(back_ready, n + 1)
                    elif g:
                        pe.wait_ge(hTl_ready, count(n, FG, group0 + g))
                    for j in range(2):
                        for t in range(tiles):
                            at = (j * tiles + t) * P
                            last = pe.transpose(ps[:, t_bank, at:at + P], h_act[:, g % 2, t, j * P:(j + 1) * P], ident[:, :])
                    last.then_inc(hT_done, 1)

                def down(g):
                    i = first + at_down(g)
                    pe.wait_ge(lo_done, count(n, PER, i + 1))
                    pe.wait_ge(hTl_ready, count(n, FG, group0 + g + 1))
                    for j in range(2):
                        for t in range(tiles):
                            tok = slice(t * P, (t + 1) * P)
                            for hf in range(2):
                                cs = slice(j * D + hf * 512, j * D + (hf + 1) * 512)
                                last = product(pe, ps[:, 2 * t + hf, :], hT_hi[:, g % 2, j, tok], hT_lo[:, g % 2, j, tok],
                                               w_hi[i % SPLITS][:, cs], w_lo[i % SPLITS][:, cs],
                                               g == 0 and j == 0, g == FG - 1 and j == 1)
                    last.then_inc(piece_used, 1)

                for p in parts:
                    kind, g, half = ITEM[p]
                    if kind == "up":
                        up(g, half)
                        if half == 0 and g:
                            turn(g - 1)
                    else:
                        if g == FG - 1:
                            if between is not None:
                                between()
                            turn(g)
                        down(g)

            norm_turn(1)
            x_columns(1)
            ffn(TILES, A_FFN, 0, 0, (x_hi, x_lo))
            norm_turn(2)
            x_columns(2)
            for i in range(N_QK):
                if i >= 4:
                    pe.wait_ge(act_evac, 12 + i - 3)
                project_T(A_QKV + i, i % 4)
            pe.wait_ge(act_evac, 12 + N_QK)

            def scores(i):
                rows = slice((i % 2) * SB_D, (i % 2 + 1) * SB_D)
                if i >= 2:
                    pe.wait_ge(w_ready, i - 1)
                for b, (s, t) in enumerate(((0, 0), (1, 1), (0, 1))):
                    last = mm(ps[:, i % 2, b * P:(b + 1) * P], kT[rows, i // 2, s * P:(s + 1) * P],
                              qT[rows, i // 2, t * P:(t + 1) * P], start=True, stop=True)
                last.then_inc(z_done, 1)

            def sums_after(i):
                pe.wait_ge(spm_ready, i + 1)
                if i >= 3:
                    pe.wait_ge(la_ready, i - 2)
                o = ps[:, 3 + i % 3]
                mm(o[:, 0:2 * P], neg_after[:, :], sp_m[:, i % 2, 0:2 * P], start=True, stop=True)
                mm(o[:, 2 * P:NZ], neg_after[:, :], sp_m[:, i % 2, 2 * P:NZ], start=True, stop=False)
                mm(o[:, 2 * P:NZ], neg_ones[:, :], sp_m[:, i % 2, P:2 * P], start=False, stop=True).then_inc(after_done, 1)

            def head_o(i):
                pe.wait_ge(att_ready, i + 1)
                pe.wait_ge(act_evac, 12 + N_QK + i // (CW // SB_D) + 1)
                pr = i // 2
                if pr >= 2:
                    pe.wait_ge(oh_ready, pr - 1)
                o = ps[(i % 2) * SB_D:(i % 2 + 1) * SB_D, 6 + pr % 2]
                mm(o[:, 0:P], v_att[:, 0, i * SB_D:(i + 1) * SB_D], att[:, i % 2, 0:P], start=True, stop=True)
                mm(o[:, P:2 * P], v_att[:, 0, i * SB_D:(i + 1) * SB_D], att[:, i % 2, 2 * P:NZ], start=True, stop=False)
                mm(o[:, P:2 * P], v_att[:, 1, i * SB_D:(i + 1) * SB_D], att[:, i % 2, P:2 * P], start=False, stop=True)\
                    .then_inc(oh_done, 1)

            scores(0)
            scores(1)
            for i in range(SB_H + 2):
                if i + 2 < SB_H:
                    scores(i + 2)
                if i < N_QKV - N_QK:
                    if i:
                        pe.wait_ge(act_evac, 12 + N_QK + i)
                    project_N(A_QKV + N_QK + i, 2)
                if i < SB_H:
                    sums_after(i)
                if i >= 2:
                    head_o(i - 2)
            pe.wait_ge(oh_ready, SB_H // 2)
            for i in range(A_WO, A_MOE):
                project_N(i, (i - A_WO) % 4)
            norm_turn(3)
            x_columns(3)
            pe.wait_ge(wrl_ready, 1)
            narrow(ps[:, 6], wr_hi, wr_lo).then_inc(lgt_done, 1)
            pe.wait_ge(sel_ready, 1)
            o = ps[:, 7]
            mm(o[:, 0:NE], before[:, :], r2[:, 3, 0, :], start=True, stop=True)
            mm(o[:, NE:2 * NE], before[:, :], r2[:, 3, 1, :], start=True, stop=False)
            mm(o[:, NE:2 * NE], ones[:, :], r2[:, 3, 0, :], start=False, stop=True)
            mm(o[:, 2 * NE:3 * NE], ones[:, :], r2[:, 3, 0, :], start=True, stop=False)
            mm(o[:, 2 * NE:3 * NE], ones[:, :], r2[:, 3, 1, :], start=False, stop=True).then_inc(pos_done, 1)

            def gather(k):
                pe.wait_ge(prep_done, k * 4 + 4)
                if not isinstance(k, int) or k:
                    pe.wait_ge(xgl_ready, k * 2)
                for c in range(DC):
                    for t in range(TILES):
                        at = (c % 4) * SLOTS
                        last = mm(ps[:, 6 + c // 4, at:at + SLOTS], xn[:, t, c * P:(c + 1) * P], sel_p[:, t, :],
                                  start=(t == 0), stop=(t == TILES - 1))
                last.then_inc(gather_done, 1)

            def way_back(k):
                pe.wait_ge(prep_done, k * 4 + 4)
                pe.wait_ge(hTl_ready, k * FG + FG)
                for t in range(TILES):
                    last = pe.transpose(ps[0:SLOTS, 3, t * P:(t + 1) * P], sel_w[:, t, :], ident[:, :])
                last.then_inc(back_done, 1)

            def scatter(n):
                pe.wait_ge(back_ready, n + 1)
                pe.wait_ge(y_act, n + 1)
                pe.wait_ge(y_vec, n + 1)
                for m in range(4):
                    t, hf = m // 2, m % 2
                    if m == 3:
                        pe.wait_ge(scat_added, n * 4 + 1)
                    mm(ps[:, SCAT_BANKS[m], :], back[:, t, :], y_exp[:, hf * 512:(hf + 1) * 512], start=True, stop=True)\
                        .then_inc(scat_done, 1)

            def expert(n, parts, following=None):
                if parts[0] == 0:
                    pe.wait_ge(xgl_ready, n * 2 + 2)
                ffn(1, A_MOE, TILES * FG, FG, (x_hi, x_lo), n, following, parts)

            gather(0)
            expert(0, HEAD)
            way_back(0)
            with pe.Fori(0, NE - 1) as n:
                expert(n, REST, lambda: gather(n + 1))
                expert(n + 1, HEAD)
                scatter(n)
                way_back(n + 1)
            expert(NE - 1, REST)
            scatter(NE - 1)
            pe.wait_ge(items_ready, 1)
            n_more = pe.value_load(item_i[0:1, 0, 0:1], min_val=0, max_val=7)
            with pe.If(n_more > 0):
                with pe.Fori(0, n_more) as it:
                    gather(it + NE)
                    way_back(it + NE)
                    expert(it + NE, ALL_PARTS)
                    scatter(it + NE)

        @block.vector
        def _(vec):
            own = [0]

            def after(ins):
                own[0] += 1
                ins.then_inc(vec_own, 1)
                vec.wait_ge(vec_own, own[0])

            tt, ts, stt = vec.tensor_tensor, vec.tensor_scalar, vec.scalar_tensor_tensor
            vec.memset(eps_col, EPS)
            vec.memset(one_col, 1.0)
            after(vec.memset(qscale_col, -0.5 * math.log(DK)))

            def norm(k, last=False, between=None):
                vec.wait_ge(ld_gain[k % 2], 16 * (k // 2 + 1))
                for t in range(TILES):
                    vec.wait_ge(rinv_ready, TILES * k + t + 1)
                    stt(xn[:, t, :], h[:, t, :], stat[:, k, 4 + t:5 + t], gain[:, k % 2, :], ALU.mult, ALU.mult)\
                        .then_inc(out_ready if last else xn_ready, 1)
                if between is not None:
                    between()
                if not last:
                    for b in range(4):
                        vec.wait_ge(xh_ready, 4 * k + b + 1)
                        cs = slice(2 * b, 2 * b + 2)
                        tt(x_lo[:, cs, :], ps[:, b, :].rearrange("p (c n) -> p c n", c=2), x_hi[:, cs, :].bitcast(F32),
                           ALU.subtract).then_inc(xl_ready, 1)

            def split_lo(i, n=None):
                vec.wait_ge(hi_done, count(n, PER, i + 1))
                tt(w_lo[i % SPLITS][:, :], ring[slots[i]][:, :], w_hi[i % SPLITS][:, :].bitcast(F32),
                   ALU.subtract).then_inc(lo_done, 1)

            for t in range(TILES):
                vec.wait_ge(ld_x[t], 16)
            norm(0)
            vec.wait_ge(bah_ready, 1)
            tt(ba_lo[:, :, :], w_ba[:, :, :], ba_hi[:, :, :].bitcast(F32), ALU.subtract).then_inc(bal_ready, 1)
            for i in range(SPLITS):
                split_lo(i)
            vec.wait_ge(rows_done, 1)
            vec.tensor_copy(colt[:, 0:KCONV * CONV_C + 1], ps[:, 6, 0:KCONV * CONV_C + 1]).then_inc(colt_ready, 1)
            vec.wait_ge(ba_done, 1)
            vec.tensor_copy(ba[:, :, :], ps[:, 7, 0:2 * U].rearrange("p (t n) -> p t n", t=TILES)).then_inc(ba_sb, 1)
            vec.wait_ge(ba_sb, 1)
            vec.wait_ge(ld_small, 32)
            after(tt(small[:, 14], ba[:, :, H:2 * H], small[:, 0, 0, :].unsqueeze(1).to_broadcast([P, TILES, H]), ALU.add))
            stt(small[:, 4], small[:, 14], -1.0, small[:, 14], ALU.mult, ALU.max).then_inc(gb_vec, 1)
            vec.wait_ge(gb_act, 1)
            after(ts(small[:, 1], small[:, 1], 1.0, None, ALU.add))
            after(vec.reciprocal(small[:, 3], small[:, 1]))
            vec.wait_ge(gb_act, 3)
            after(stt(small[:, 15], small[:, 14], 0.0, small[:, 6], ALU.max, ALU.add))
            stt(small[:, 7], small[:, 15], -1.0, small[:, 2, 0, :].unsqueeze(1).to_broadcast([P, TILES, H]),
                ALU.mult, ALU.mult).then_inc(g_ready, 1)
            vec.wait_ge(wsT_done, 1)
            vec.tensor_copy(wsT[:, :, :].rearrange("p g n -> p (g n)"), two(4)).then_inc(wsT_ready, 1)

            conv_steps = [0]

            def conv(i):
                vec.wait_ge(act_evac, i + 1)
                for k in range(KCONV):
                    for c in (2 * i, 2 * i + 1):
                        w = colt[:, k * CONV_C + c:k * CONV_C + c + 1]
                        src = conv_in[:, c, k:k + SEQ]
                        if k == 0:
                            ins = ts(qkvT[:, c, :], src, w, None, ALU.mult)
                        else:
                            ins = stt(qkvT[:, c, :], src, w, qkvT[:, c, :], ALU.mult, ALU.add)
                        if k < KCONV - 1:
                            last = ins
                    if k < KCONV - 1:
                        after(last)
                ins.then_inc(conv_done, 1)

            vec.wait_ge(colt_ready, 1)
            for i in range(3):
                conv(i)
                split_lo(i + SPLITS)
            vec.wait_ge(gc_done, 1)
            after(vec.tensor_copy(small[:, 8:10].rearrange("p a t h -> p (a t h)"), ps[:, 6, 0:2 * U]))
            tt(small[:, 11], small[:, 9], small[:, 8], ALU.subtract).then_inc(gc_sb, 1)
            for i in range(3, 6):
                conv(i)
                split_lo(i + SPLITS)
            split_lo(9)
            vec.wait_ge(exp_row_ready, 1)
            for u in range(U):
                hd, t = u // TILES, u % TILES
                ts(gam[:, u, :], two(4)[:, u * P:(u + 1) * P], small[:, 8, t, hd:hd + 1], 0.0,
                   ALU.subtract, ALU.min).then_inc(gam_arg, 1)
            split_lo(10)
            vec.wait_ge(gcols_act, 1)
            tt(small[:, 13], small[:, 3], small[:, 10], ALU.mult).then_inc(kbe_scale, 1)
            vec.wait_ge(rn_ready, 2)
            after(tt(qkvT[:, H:2 * H, :], qkvT[:, H:2 * H, :], rn[:, H:2 * H, :], ALU.mult))
            vec.wait_ge(row_done, 2)
            tt(kbT[:, :, :].rearrange("p a b -> p (a b)"), qkvT[:, H:2 * H, :].rearrange("p a b -> p (a b)"), two(6),
               ALU.mult).then_inc(kb_ready, 1)
            tt(qkvT[:, 0:H, :], qkvT[:, 0:H, :], rn[:, 0:H, :], ALU.mult).then_inc(kb_ready, 1)
            split_lo(11)
            vec.wait_ge(gam_exp, 1)
            after(tt(gam[:, :, :], gam[:, :, :], tri_blk[:, :].unsqueeze(1).to_broadcast([P, U, P]), ALU.mult))
            vec.wait_ge(kk_done, 2)
            flat_g = gam[:, :, :].rearrange("p u n -> p (u n)")
            tt(attnT[:, :, :].rearrange("p u n -> p (u n)"), two(6), flat_g, ALU.mult).then_inc(attn_ready, 1)
            vec.wait_ge(attn_ready, 1)
            tt(flat_g, two(4), flat_g, ALU.mult).then_inc(lt_ready, 1)
            tt(qkvT[:, 0:H, :].rearrange("p a b -> p (a b)"), qkvT[:, 0:H, :].rearrange("p a b -> p (a b)"),
               exp_row[:, :, :, :].rearrange("p h t n -> p (h t n)"), ALU.mult).then_inc(qd_ready, 1)
            vec.wait_ge(turn_done, 2)
            for u in range(U):
                hd, t = u // TILES, u % TILES
                ts(vb[:, u, :], two(2)[:, u * P:(u + 1) * P], small[:, 3, t, hd:hd + 1], None, ALU.mult).then_inc(vb_ready, 1)
            for i in (12, 13, 14):
                split_lo(i)
            vec.wait_ge(act_evac, 12)
            for t in range(TILES):
                after(vec.bn_stats(bn[:, t, :], v_nat[:, t, :]))
            vec.bn_aggr(mv[:, 0, :], bn[:, 0, :])
            vec.bn_aggr(mv[:, 1, :], bn[:, 1, :]).then_inc(ln_var, 1)

            def layernorm():
                vec.wait_ge(ln_rstd, 1)
                vec.wait_ge(ld_lng, 32)
                for t in range(TILES):
                    after(ts(v_nat[:, t, :], v_nat[:, t, :], mv[:, t, 0:1], stat_ln[:, 1, t:t + 1], ALU.subtract, ALU.mult))
                    after(tt(v_nat[:, t, :], v_nat[:, t, :], ln_g, ALU.mult))
                    tt(v_nat[:, t, :], v_nat[:, t, :], ln_b, ALU.add).then_inc(v_ready, 1)

            def gate_out():
                vec.wait_ge(mix_done, 1)
                vec.wait_ge(ld_bias, 32)
                tmp = wsT[:, :, :].rearrange("p g n -> p (g n)")
                after(tt(tmp.rearrange("p (c t n) -> p c t n", c=G // 2, t=TILES),
                         two(0).rearrange("p (c t n) -> p c t n", c=G // 2, t=TILES),
                         sgu_bias[:, :, :].unsqueeze(2).to_broadcast([P, G // 2, TILES, P]), ALU.add))
                y = yT[:, 0:4, :].rearrange("p a b -> p (a b)")
                tt(y, tmp, y, ALU.mult).then_inc(ya_ready, 1)

            def units4(t):
                return t.unsqueeze(1).to_broadcast([P, 4, P])

            for k in range(LEVELS):
                for hf in range(2):
                    us = slice(4 * hf, 4 * hf + 4)
                    vec.wait_ge(t_done, 2 * k + hf + 1)
                    tt(inv_t[:, us, :], ps[:, 4 + hf, :].rearrange("p (u n) -> p u n", u=4), units4(level[:, k, :]),
                       ALU.mult).then_inc(t_ready, 1)
                for hf in range(2):
                    us = slice(4 * hf, 4 * hf + 4)
                    if k < LEVELS - 1:
                        vec.wait_ge(x_done, 2 * k + hf + 1)
                        tt(inv_x[:, us, :], inv_x[:, us, :] if k else units4(ident[:, :]),
                           ps[:, 6 + hf, :].rearrange("p (u n) -> p u n", u=4), ALU.subtract).then_inc(x_ready, 1)
                    vec.wait_ge(xt_done, 2 * k + hf + 1)
                    tt(inv_xt[:, us, :], inv_xt[:, us, :] if k else units4(ident[:, :]),
                       ps[:, 2 + hf, :].rearrange("p (u n) -> p u n", u=4), ALU.subtract).then_inc(xt_ready, 1)
                if k == 0:
                    layernorm()
                if k == 3:
                    gate_out()
            vec.wait_ge(sol_done, 2)
            vec.tensor_copy(u_sol.rearrange("p u n -> p (u n)"), two(0)).then_inc(sol_u, 1)
            vec.wait_ge(sol_u, 1)
            for c in range(NCH):
                t, p0 = c // 2, (c % 2) * CH
                rows = slice(p0, p0 + CH)
                u4 = u_sol.rearrange("p (h t) n -> p t h n", t=TILES)[rows, t]
                vn = v_new[rows, t, :].rearrange("p (h n) -> p h n", h=H)
                if c == 0:
                    vec.tensor_copy(vn, u4).then_inc(vnew_ready, 1)
                else:
                    vec.wait_ge(ws_done, c)
                    tt(vn, u4, ps[rows, 6, :].rearrange("p (h n) -> p h n", h=H), ALU.subtract).then_inc(vnew_ready, 1)
                if c < NCH - 1:
                    vec.wait_ge(st_done, c + 1)
                    if c == 0:
                        vec.tensor_copy(state[:, :, :].rearrange("p h n -> p (h n)"), ps[:, 2, :]).then_inc(st_ready, 1)
                    else:
                        vec.wait_ge(o_done, c + 1)
                        for hd in range(H):
                            ins = stt(state[:, hd, :], state[:, hd, :], exp_row[:, hd, t, p0 + CH - 1:p0 + CH],
                                      ps[:, 2, hd * P:(hd + 1) * P], ALU.mult, ALU.add)
                        ins.then_inc(st_ready, 1)
            vec.wait_ge(yh_ready, 1)
            tt(x_lo[:, 0:4, :], yT[:, 0:4, :], x_hi[:, 0:4, :].bitcast(F32), ALU.subtract).then_inc(yl_ready, 1)
            vec.wait_ge(on_ready, 1)
            fo = oT.rearrange("p a b -> p (a b)")
            after(stt(fo, fo, colt[:, KCONV * CONV_C:KCONV * CONV_C + 1], rn[:, H:2 * H, :].rearrange("p a b -> p (a b)"),
                      ALU.mult, ALU.mult))
            yb = yT[:, 4:8, :].rearrange("p a b -> p (a b)")
            tt(yb, fo, yb, ALU.mult).then_inc(yb_ready, 1)
            vec.wait_ge(yh_ready, 2)
            tt(x_lo[:, 4:8, :], yT[:, 4:8, :], x_hi[:, 4:8, :].bitcast(F32), ALU.subtract).then_inc(yl_ready, 1)

            def add_project(i, base, last_inc):
                used(vec, base + i)
                for t in range(TILES):
                    ins = tt(h[:, t, i * CW:(i + 1) * CW], h[:, t, i * CW:(i + 1) * CW],
                             ps[:, i % 4, t * CW:(t + 1) * CW], ALU.add)
                    if last_inc:
                        ins.then_inc(h_ready, 1)

            for i in range(N_OUT):
                add_project(i, A_OUT, i == N_OUT - 1)
                if i < 3:
                    split_lo(15 + i)
            norm(1)
            split_lo(18)

            def ffn(tiles, first, unit0, group0, ahead, n=None, parts=ALL_PARTS, extra={}):
                def multiply(g):
                    for t in range(tiles):
                        bank = 4 + (tiles * g + t) % (tiles + 1)
                        vec.wait_ge(silu_done, count(n, FG, unit0 + tiles * g + t + 1))
                        if t == 0 and g >= 2:
                            vec.wait_ge(hT_done, count(n, FG, group0 + g - 1))
                        tt(h_act[:, g % 2, t, :], silu_s[:, t, :], ps[:, bank, CW:2 * CW], ALU.mult).then_inc(act_ready, 1)

                def turned(g):
                    vec.wait_ge(hTh_ready, count(n, FG, group0 + g + 1))
                    tt(hT_lo[:, g % 2, :, 0:tiles * P], ps[:, 7 if tiles == 2 else 3, 0:2 * tiles * P].rearrange("p (j n) -> p j n", j=2),
                       hT_hi[:, g % 2, :, 0:tiles * P].bitcast(F32), ALU.subtract).then_inc(hTl_ready, 1)

                for p in parts:
                    kind, g, half = ITEM[p]
                    if kind == "up" and half == 1:
                        multiply(g)
                    if kind == "up" and half == 0 and g >= 1:
                        turned(g - 1)
                    if p in extra:
                        extra[p]()
                    if p + SPLITS < PER + ahead:
                        split_lo(first + p + SPLITS, n)
                    if p == PER - 2:
                        turned(FG - 1)

            ffn(TILES, A_FFN, 0, 0, SPLITS - 1)
            used(vec, A_QKV - 1)
            for m in range(4):
                t, hf = m // 2, m % 2
                cs = slice(hf * 512, (hf + 1) * 512)
                ins = tt(h[:, t, cs], h[:, t, cs], ps[:, m, :], ALU.add)
                if hf:
                    ins.then_inc(h_ready, 1)
            norm(2, between=lambda: split_lo(A_QKV + SPLITS - 1))
            for i in range(A_QKV + SPLITS, A_QKV + N_QK + SPLITS):
                split_lo(i)

            def softplus(i):
                vec.wait_ge(log_ready, i + 1)
                if i >= 2:
                    vec.wait_ge(after_done, i - 1)
                if i >= 2:
                    vec.wait_ge(att_exp, i - 1)
                stt(sp_m[:, i % 2], ps[:, i % 2, 0:NZ], 0.0, lg[:, i % 2], ALU.max, ALU.add).then_inc(sp_ready, 1)
                stt(w_log[:, i % 2], ps[:, i % 2, 0:NZ], 0.0, lg[:, i % 2], ALU.min, ALU.subtract).then_inc(w_ready, 1)

            def log_att(i):
                vec.wait_ge(after_done, i + 1)
                vec.wait_ge(w_ready, i + 1)
                tt(w_log[:, i % 2], w_log[:, i % 2], ps[:, 3 + i % 3, 0:NZ], ALU.add).then_inc(la_ready, 1)

            def head_out(pr):
                vec.wait_ge(oh_hi, pr + 1)
                tt(x_lo[:, pr, :], ps[:, 6 + pr % 2, 0:SEQ], x_hi[:, pr, :].bitcast(F32), ALU.subtract).then_inc(oh_ready, 1)

            for i in range(SB_H + 2):
                if i < SB_H:
                    softplus(i)
                if 1 <= i <= SB_H:
                    log_att(i - 1)
                if 1 <= i <= N_QKV - N_QK:
                    split_lo(A_QKV + N_QK + i - 1 + SPLITS)
                if i >= 5 and i % 2 == 1:
                    head_out((i - 5) // 2)
            head_out(SB_H // 2 - 1)
            vec.wait_ge(wrh_ready, 1)
            tt(wr_lo[:, :, :], w_router[:, :, :], wr_hi[:, :, :].bitcast(F32), ALU.subtract).then_inc(wrl_ready, 1)
            for i in range(N_OUT):
                add_project(i, A_WO, i == N_OUT - 1)
                if i < 3:
                    split_lo(A_WO + i + SPLITS)
            norm(3)
            split_lo(A_MOE + 2)

            vec.wait_ge(lgt_done, 1)
            after(vec.tensor_copy(logits[:, :, :].rearrange("p t e -> p (t e)"), ps[:, 6, 0:TILES * NE]))
            TE = TILES * NE
            lgf = logits[:, :, :]
            other = lgf.unsqueeze(2).to_broadcast([P, TILES, NE, NE])
            mine = lgf.rearrange("p t e -> p (t e)").unsqueeze(2).to_broadcast([P, TE, NE])

            def four(a):
                return a.rearrange("p (t e) f -> p t e f", t=TILES)

            mine4 = lgf.unsqueeze(3).to_broadcast([P, TILES, NE, NE])
            tt(four(rt[:, 0]), other, mine4, ALU.is_gt)
            after(tt(four(rt[:, 1]), other, mine4, ALU.is_equal))
            e_of = iota[:, 0:NE].unsqueeze(2).to_broadcast([P, NE, NE])
            f_of = iota[:, 0:NE].unsqueeze(1).to_broadcast([P, NE, NE])
            tt(rt[:, 2, 0:NE, :], f_of, e_of, ALU.is_lt)
            after(tt(rt[:, 2, NE:TE, :], f_of, e_of, ALU.is_lt))
            after(tt(rt[:, 1], rt[:, 1], rt[:, 2], ALU.mult))
            after(tt(rt[:, 0], rt[:, 0], rt[:, 1], ALU.add))
            after(vec.tensor_reduce(r2[:, 0].rearrange("p t e -> p (t e)"), rt[:, 0], AX.X, ALU.add))
            ts(r2[:, 1], r2[:, 0], 0.0, None, ALU.is_equal)
            after(ts(r2[:, 2], r2[:, 0], 1.0, None, ALU.is_equal))
            tt(r2[:, 3], r2[:, 1], r2[:, 2], ALU.add).then_inc(sel_ready, 1)
            tt(r2[:, 4], r2[:, 1], lgf, ALU.mult)
            after(tt(r2[:, 5], r2[:, 2], lgf, ALU.mult))
            after(tt(r2[:, 4], r2[:, 5], r2[:, 4], ALU.subtract))
            vec.tensor_reduce(r_small[:, 0], r2[:, 4], AX.X, ALU.add).then_inc(r_d, 1)
            vec.wait_ge(r_exp, 1)
            after(ts(r_small[:, 2], r_small[:, 1], 1.0, None, ALU.add))
            after(vec.reciprocal(r_small[:, 3], r_small[:, 2]))
            after(tt(r_small[:, 4], r_small[:, 3], r_small[:, 1], ALU.mult))
            for t in range(TILES):
                after(ts(r2[:, 6, t], r2[:, 1, t], r_small[:, 3, t:t + 1], None, ALU.mult))
                after(stt(r2[:, 7, t], r2[:, 2, t], r_small[:, 4, t:t + 1], r2[:, 6, t], ALU.mult, ALU.add))
            vec.wait_ge(sel_ready, 1)
            vec.wait_ge(pos_done, 1)
            place = ps[:, 7, 0:2 * NE].rearrange("p (t e) -> p t e", t=TILES)
            for b in range(NB):
                ks = slice(b * NE, (b + 1) * NE)
                ts(table[:, 0, :, ks], place, float(-SLOTS * b), None, ALU.add)
                vec.tensor_copy(table[:, 1, :, ks], r2[:, 3])
                after(vec.tensor_copy(table[:, 2, :, ks], r2[:, 7]))
            for b in range(1, NB):
                after(ts(li[0:1, 0, (b - 1) * NE:b * NE], ps[0:1, 7, 2 * NE:3 * NE], float(SLOTS * b), None, ALU.is_gt))
            after(vec.tensor_tensor_scan(li[0:1, 1, :], ones[0:1, 0:NK - NE], li[0:1, 0, :], 0.0, ALU.mult, ALU.add))
            after(tt(li[0:1, 2, :], li[0:1, 0, :], iota[0:1, NE:NK], ALU.mult))
            after(tt(li3[0:1], li[0:1, 1, :].unsqueeze(1).to_broadcast([1, 8, NK - NE]),
                     iota[0:1, 1:9].unsqueeze(2).to_broadcast([1, 8, NK - NE]), ALU.is_equal))
            after(tt(li3[0:1], li3[0:1], li[0:1, 2, :].unsqueeze(1).to_broadcast([1, 8, NK - NE]), ALU.mult))
            after(vec.tensor_reduce(item_f[0:1, 1, :], li3[0:1], AX.X, ALU.add))
            after(ts(item_f[0:1, 2, :], item_f[0:1, 1, :], -float(NE), 0.0, ALU.add, ALU.max))
            after(vec.tensor_copy(item_f[0:1, 0, :], li[0:1, 1, NK - NE - 1:NK - NE].to_broadcast([1, 8])))
            vec.tensor_copy(item_i[:, :, :], item_f).then_inc(items_ready, 1)

            def prep(n, k):
                vec.tensor_copy(col6[:, :, :, :], table[:, :, :, bass.ds(k, 1)]).then_inc(prep_col, 1)
                vec.wait_ge(prep_col, n + 1)
                if not isinstance(n, int) or n:
                    vec.wait_ge(back_done, n)
                for t in range(TILES):
                    ts(sel_p[:, t, :], iota[:, 0:SLOTS], col6[:, 0, t], col6[:, 1, t], ALU.is_equal, ALU.mult).then_inc(prep_done, 1)
                    ts(sel_w[:, t, :], iota[:, 0:SLOTS], col6[:, 0, t], col6[:, 2, t], ALU.is_equal, ALU.mult).then_inc(prep_done, 1)

            def evac_xg(k):
                for b in range(2):
                    vec.wait_ge(xgh_ready, k * 2 + (b + 1))
                    cs = slice(4 * b, 4 * b + 4)
                    tt(x_lo[:, cs, 0:SLOTS], ps[:, 6 + b, :].rearrange("p (c n) -> p c n", c=4), x_hi[:, cs, 0:SLOTS].bitcast(F32),
                       ALU.subtract).then_inc(xgl_ready, 1)

            def evac_back(n):
                vec.wait_ge(back_done, n + 1)
                vec.tensor_copy(back[:, :, :].rearrange("p t n -> p (t n)"), ps[0:SLOTS, 3, 0:SEQ]).then_inc(back_ready, 1)

            def evac_y(n):
                used(vec, A_MOE + PER - 1, n)
                vec.tensor_copy(y_exp[:, 0:512], ps[0:SLOTS, 0, :]).then_inc(y_vec, 1)

            def add_item(n, parts=range(4)):
                for m in parts:
                    t, hf = m // 2, m % 2
                    cs = slice(hf * 512, (hf + 1) * 512)
                    vec.wait_ge(scat_done, n * 4 + (m + 1))
                    tt(h[:, t, cs], h[:, t, cs], ps[:, SCAT_BANKS[m], :], ALU.add).then_inc(scat_added, 1)

            def expert(n, ahead, parts, add_last=None):
                def before_end():
                    if ahead:
                        evac_xg(n + 1)
                    evac_y(n)
                extra = {PER - 1: before_end}
                if add_last is not None:
                    extra[1] = add_last
                ffn(1, A_MOE, TILES * FG, FG, ahead, n, parts, extra)

            prep(0, 0)
            evac_xg(0)
            expert(0, SPLITS, HEAD)
            evac_back(0)
            with vec.Fori(0, NE - 1) as n:
                prep(n + 1, n + 1)
                expert(n, SPLITS, REST)
                expert(n + 1, SPLITS, HEAD, lambda: add_item(n, range(3)))
                add_item(n, range(3, 4))
                evac_back(n + 1)
            expert(NE - 1, 0, REST)
            add_item(NE - 1)
            vec.wait_ge(items_ready, 1)
            n_more = vec.value_load(item_i[0:1, 0, 0:1], min_val=0, max_val=7)
            with vec.If(n_more > 0):
                with vec.Fori(0, n_more) as it:
                    k = vec.value_load(item_i[0:1, 1, bass.ds(it, 1)], min_val=0, max_val=NK - 1)
                    prep(it + NE, k)
                    for p in range(SPLITS):
                        split_lo(A_MOE + p, it + NE)
                    evac_xg(it + NE)
                    evac_back(it + NE)
                    expert(it + NE, 0, ALL_PARTS)
                    add_item(it + NE)
            vec.wait_ge(items_ready, 1)
            vec.drain().then_inc(h_ready, TILES)
            norm(4, True)


_INS = ['x', 'e_norm1', 'e_w_in', 'e_sgu_ln_g', 'e_sgu_ln_b', 'e_sgu_w', 'e_sgu_b', 'e_conv_w', 'e_a_log',
        'e_dt_bias', 'e_o_norm', 'e_w_out', 'e_norm2', 'e_ffn_w1', 'e_ffn_w3', 'e_ffn_w2', 'o_norm1', 'o_w_qkv',
        'o_w_out', 'o_norm2', 'o_router', 'o_moe_w1', 'o_moe_w3', 'o_moe_w2', 'final_norm']
_OUTS = [((1, 256, 1024), 'float32')]


def kernel(**inputs):
    import numpy as _np
    import concourse.bacc as _bacc
    from concourse import mybir as _mybir
    from concourse.bass_utils import run_bass_kernel_spmd as _run

    nc = _bacc.Bacc("TRN2", target_bir_lowering=False, num_devices=1)
    arrays, args = {}, []
    for name in _INS:
        a = _np.ascontiguousarray(inputs[name])
        arrays[f"in_{name}_dram"] = a
        args.append(nc.dram_tensor(f"in_{name}_dram", a.shape, _mybir.dt.from_np(a.dtype), kind="ExternalInput").ap())
    for i, (shape, dtype) in enumerate(_OUTS):
        dt = _mybir.dt.from_np(_np.dtype(dtype))
        args.append(nc.dram_tensor(f"out_{i}_dram", shape, dt, kind="ExternalOutput").ap())
    trunk(nc, *args)
    r = _run(nc, [arrays], core_ids=[0])
    got = tuple(r.results[0][f"out_{i}_dram"] for i in range(len(_OUTS)))
    return got[0]
```

```python
import math
from contextlib import ExitStack

import concourse.bass as bass
from concourse import mybir

F32 = mybir.dt.float32
F32R = mybir.dt.float32r
I32 = mybir.dt.int32
ALU = mybir.AluOpType
ACT = mybir.ActivationFunctionType
AX = mybir.AxisListType

P = 128
EPS = 1e-6
EXP_LN = "natural_log_exp_and_others"


def trunk(nc, x, e_norm1, e_w_in, e_sgu_ln_g, e_sgu_ln_b, e_sgu_w, e_sgu_b, e_conv_w, e_a_log,
          e_dt_bias, e_o_norm, e_w_out, e_norm2, e_ffn_w1, e_ffn_w3, e_ffn_w2, o_norm1, o_w_qkv,
          o_w_out, o_norm2, o_router, o_moe_w1, o_moe_w3, o_moe_w2, final_norm, out):
    SEQ, D = x.shape[1], x.shape[2]
    TILES, DC = SEQ // P, D // P
    SGU_W = e_sgu_ln_g.shape[1]
    G = e_sgu_w.shape[1]
    GD = SGU_W // G
    H = e_a_log.shape[1]
    DK = e_o_norm.shape[1]
    KCONV = e_conv_w.shape[1]
    CONV_C = e_conv_w.shape[2] // P
    CH = 64
    NCH = SEQ // CH
    U = H * TILES
    SB_H, SB_D = 16, 64
    FF = e_ffn_w1.shape[2]
    FC = FF // P
    NE = o_router.shape[2]
    CW = 256
    SLOTS = P
    NB = SEQ // SLOTS
    NK = NB * NE
    assert TILES == 2 and DC == 8 and DK == P and U == 8 and FC == 22
    LEVELS = 6
    assert 2 ** LEVELS == CH
    QKV0, GATE0, BA0 = 2 * SGU_W, 2 * SGU_W + CONV_C * P, e_w_in.shape[2] - 2 * H

    R_EVEN, RING, SPLITS = 5, 11, 3
    N_IN, N_OUT, N_QKV = 12, D // CW, 3 * D // CW
    N_QK = 2 * D // CW
    FG = FF // CW
    PER = 3 * FG
    A_OUT, A_FFN = N_IN, N_IN + N_OUT
    A_QKV = A_FFN + PER
    A_WO = A_QKV + N_QKV
    A_MOE = A_WO + N_OUT
    assert PER % RING == 0 and PER % SPLITS == 0 and FG == 11
    HC = DC // 2

    def at_up(g, half):
        return (3 * g - 1 if g else 0) + half

    def at_down(g):
        return 3 * g + 4 if g < FG - 1 else PER - 1

    ITEM = {at_up(g, half): ("up", g, half) for g in range(FG) for half in range(2)}
    ITEM.update({at_down(g): ("down", g, 0) for g in range(FG)})
    assert sorted(ITEM) == list(range(PER))

    ALL_PARTS, HEAD, REST = range(PER), range(2), range(2, PER)
    SCAT_BANKS = (6, 7, 2, 6)
    OUT_BANKS, ATT_OUT_BANKS = (0, 1, 4, 5), (2, 3, 4, 5)

    def slot_of(i):
        return i % R_EVEN if i < A_FFN else (i - A_FFN + 1) % RING

    slots = [slot_of(i) for i in range(A_MOE + PER + SPLITS)]

    def before_it(i):
        same = [m for m in range(i) if slots[m] == slots[i]]
        return same[-1] if same else None

    def arrivals(i):
        return 32 * sum(slots[m] == slots[i] for m in range(i + 1))

    PER_SLOT = 32 * PER // RING

    w_in_cols = [QKV0 + CW * i for i in range(6)] + [GATE0, GATE0 + CW] + [SGU_W, SGU_W + CW] + [0, CW]

    def projection(i):
        if i < A_OUT:
            return e_w_in[0], w_in_cols[i]
        if i < A_FFN:
            return e_w_out[0], 0
        if i < A_WO:
            return o_w_qkv[0], CW * (i - A_QKV)
        return o_w_out[0], 0

    with ExitStack() as ctx:
        def sb(name, shape, dt=F32, stack=ctx):
            return stack.enter_context(nc.sbuf_tensor(name, shape, dt))

        def sem(name):
            return ctx.enter_context(nc.semaphore(name))

        PIECE = DC * CW
        ring = [sb(f"ring{i}", [P, PIECE]) for i in range(R_EVEN)]
        h = sb("h", [P, TILES, D])
        xn = sb("xn", [P, TILES, D])
        x_hi = sb("x_hi", [P, DC, SEQ], F32R)
        x_lo = sb("x_lo", [P, DC, SEQ], F32R)
        gain = sb("gain", [P, 2, D])
        ident = sb("ident", [P, P])
        ones = sb("ones", [P, P])
        neg_ones = sb("neg_ones", [P, P])
        tri_blk = sb("tri_blk", [P, P])
        blk_ones = sb("blk_ones", [P, P])
        before = sb("before", [P, P])
        neg_after = sb("neg_after", [P, P])
        level = sb("level", [P, LEVELS, P])
        iota = sb("iota", [P, P])
        colt = sb("colt", [P, KCONV * CONV_C + 1])
        stat = sb("stat", [P, 5, 6])
        small = sb("small", [P, 16, TILES, H])
        ba = sb("ba", [P, TILES, 2 * H])
        w_ba = sb("w_ba", [P, DC, 2 * H])
        ba_hi = sb("ba_hi", [P, DC, 2 * H], F32R)
        ba_lo = sb("ba_lo", [P, DC, 2 * H], F32R)
        w_hi = [sb(f"w_hi{i}", [P, PIECE], F32R) for i in range(SPLITS)]
        w_lo = [sb(f"w_lo{i}", [P, PIECE], F32R) for i in range(SPLITS)]
        const = sb("const", [P, 4])
        eps_col, one_col, qscale_col = const[:, 0:1], const[:, 1:2], const[:, 2:3]
        bn = sb("bn", [P, TILES, 6])
        mv = sb("mv", [P, TILES, 2])
        stat_ln = sb("stat_ln", [P, 2, TILES])
        r_small = sb("r_small", [P, 6, TILES])

        even = ExitStack()
        conv_in = sb("conv_in", [P, CONV_C, KCONV - 1 + SEQ], stack=even)
        qkvT = sb("qkvT", [P, CONV_C, SEQ], stack=even)
        yT = sb("yT", [P, DC, SEQ], stack=even)
        v_nat = sb("v_nat", [P, TILES, SGU_W], stack=even)
        wsT = sb("wsT", [P, G, P], stack=even)
        sgu_bias = sb("sgu_bias", [P, G // 2, P], stack=even)
        exp_row = sb("exp_row", [P, H, TILES, P], stack=even)
        kbT = sb("kbT", [P, H, SEQ], stack=even)
        gam = sb("gam", [P, U, P], stack=even)
        lower = sb("lower", [P, U, P], stack=even)
        kd = sb("kd", [P, U, P], stack=even)
        rn = sb("rn", [P, 2 * H, SEQ], stack=even)
        even.close()
        state = wsT[:, 0:H, :]
        ws_raw = gam
        rows_raw = kd[:, 0, :]
        inv = conv_in[:, :, :].rearrange("p a b -> p (a b)")[:, 0:3 * U * P].rearrange(
            "p (k u n) -> p k u n", k=3, u=U)
        inv_x, inv_xt, inv_t = inv[:, 0], inv[:, 1], inv[:, 2]
        vb = xn[:, 0, :].rearrange("p (u n) -> p u n", u=U)
        kbe = xn[:, 1, :].rearrange("p (u n) -> p u n", u=U)
        u_sol = rn[:, 0:H, :].rearrange("p h (t n) -> p (h t) n", t=TILES)
        w_solT = rn[:, H:2 * H, :].rearrange("p h (t n) -> p (h t) n", t=TILES)
        v_new = kbT[:, :, :].rearrange("p a b -> p (a b)").rearrange("p (t n) -> p t n", t=TILES)
        ba_T = exp_row[0:2 * H, 0, :, :].rearrange("p t n -> p (t n)")
        oT = qkvT[:, 2 * H:3 * H, :]
        ln_g, ln_b = gain[:, 1, 0:SGU_W], gain[:, 1, SGU_W:2 * SGU_W]

        ring += [sb(f"ring{i}", [P, PIECE]) for i in range(R_EVEN, RING)]
        w_router = sb("w_router", [P, DC, NE])
        wr_hi = sb("wr_hi", [P, DC, NE], F32R)
        wr_lo = sb("wr_lo", [P, DC, NE], F32R)
        odd = ExitStack()
        NZ = 384
        qT = sb("qT", [P, DC, SEQ], stack=odd)
        kT = sb("kT", [P, DC, SEQ], stack=odd)
        sp_m = sb("sp_m", [P, 2, NZ], stack=odd)
        att = sb("att", [P, 2, NZ], stack=odd)
        odd.close()
        lg = level[:, :, :].rearrange("p a b -> p (a b)").rearrange("p (a n) -> p a n", a=2)
        w_log = gain[:, 0, 0:2 * NZ].rearrange("p (a n) -> p a n", a=2)
        v_att = xn
        silu_s = sb("silu_s", [P, TILES, CW])
        h_act = sb("h_act", [P, 2, TILES, CW])
        hT_hi = sb("hT_hi", [P, 2, 2, SEQ], F32R)
        hT_lo = sb("hT_lo", [P, 2, 2, SEQ], F32R)
        sel_p = sb("sel_p", [P, TILES, SLOTS])
        sel_w = sb("sel_w", [P, TILES, SLOTS])
        back = sb("back", [SLOTS, TILES, P])
        y_exp = sb("y_exp", [SLOTS, D])
        logits_T = back[0:NE, :, :].rearrange("p t n -> p (t n)")
        logits = sb("logits", [P, TILES, NE])
        rt = y_exp[:, 0:3 * TILES * NE * NE].rearrange("p (k a b) -> p k a b", k=3, a=TILES * NE)
        r2 = sb("r2", [P, 8, TILES, NE])
        spent = r2[0:1, :, :, :].rearrange("p a t e -> p (a t e)")
        assert NK - NE == 8
        li = spent[:, 0:24].rearrange("p (a b) -> p a b", a=3)
        item_f = spent[:, 24:48].rearrange("p (a b) -> p a b", a=3)
        li3 = spent[:, 64:128].rearrange("p (a b) -> p a b", a=8)
        table = sb("table", [P, 3, TILES, NK])
        col6 = sb("col6", [P, 3, TILES, 1])
        counts = sb("counts", [1, NE])
        item_i = sb("item_i", [1, 3, 8], I32)

        ps = ctx.enter_context(nc.psum_tensor("ps", [P, 8, 512], F32))

        def two(b):
            return ps[:, b:b + 2, :].rearrange("p b n -> p (b n)")

        ld_ba, ld_small, ld_rows, ld_ws, ld_lng, ld_bias, ld_wr = (
            sem(n) for n in ("ld_ba", "ld_small", "ld_rows", "ld_ws", "ld_lng", "ld_bias", "ld_wr"))
        ld_x = [sem("ld_x0"), sem("ld_x1")]
        ld_gain = [sem("ld_gain0"), sem("ld_gain1")]
        ring_in = [sem(f"ring_in{i}") for i in range(RING)]
        hi_done, lo_done, piece_used = sem("hi_done"), sem("lo_done"), sem("piece_used")
        pool_own, act_own, vec_own = sem("pool_own"), sem("act_own"), sem("vec_own")
        consts_ready, pads_ready, ident_ready = sem("consts_ready"), sem("pads_ready"), sem("ident_ready")
        h_ready, rinv_ready, xn_ready, xnT_done = sem("h_ready"), sem("rinv_ready"), sem("xn_ready"), sem("xnT_done")
        xh_ready, xl_ready, yh_ready, yl_ready = sem("xh_ready"), sem("xl_ready"), sem("yh_ready"), sem("yl_ready")
        bah_ready, bal_ready, wrh_ready, wrl_ready = (
            sem(n) for n in ("bah_ready", "bal_ready", "wrh_ready", "wrl_ready"))
        act_evac, oh_hi = sem("act_evac"), sem("oh_hi")
        rows_done, colt_ready, ba_done = sem("rows_done"), sem("colt_ready"), sem("ba_done")
        wsT_done, wsT_ready = sem("wsT_done"), sem("wsT_ready")
        ba_sb, gb_act, gb_vec, g_ready = sem("ba_sb"), sem("gb_act"), sem("gb_vec"), sem("g_ready")
        conv_done, silu_even = sem("conv_done"), sem("silu_even")
        gc_done, gc_sb, row_done, exp_row_ready = sem("gc_done"), sem("gc_sb"), sem("row_done"), sem("exp_row_ready")
        gcols_act, kbe_scale = sem("gcols_act"), sem("kbe_scale")
        sq_ready, l2_done, rn_ready = sem("sq_ready"), sem("l2_done"), sem("rn_ready")
        kb_ready, gam_arg, gam_exp, kk_done, attn_ready, lt_ready = (
            sem(n) for n in ("kb_ready", "gam_arg", "gam_exp", "kk_done", "attn_ready", "lt_ready"))
        qd_ready, turn_done, vb_ready, kbe_ready, kd_ready = (
            sem(n) for n in ("qd_ready", "turn_done", "vb_ready", "kbe_ready", "kd_ready"))
        t_done, t_ready, x_done, x_ready, xt_done, xt_ready = (
            sem(n) for n in ("t_done", "t_ready", "x_done", "x_ready", "xt_done", "xt_ready"))
        sol_done, sol_u, sol_w = sem("sol_done"), sem("sol_u"), sem("sol_w")
        ws_done, vnew_ready, o_done, o_sb, st_done, st_ready = (
            sem(n) for n in ("ws_done", "vnew_ready", "o_done", "o_sb", "st_done", "st_ready"))
        tile_summed = sem("tile_summed")
        row_copied, gate_ready = sem("row_copied"), sem("gate_ready")
        osq_ready, on_done, on_ready, yb_ready = sem("osq_ready"), sem("on_done"), sem("on_ready"), sem("yb_ready")
        ln_var, ln_rstd, v_ready, mix_done, ya_ready = (
            sem(n) for n in ("ln_var", "ln_rstd", "v_ready", "mix_done", "ya_ready"))
        silu_done, act_ready, hT_done, hTh_ready, hTl_ready = (
            sem(n) for n in ("silu_done", "act_ready", "hT_done", "hTh_ready", "hTl_ready"))
        z_done, log_ready, sp_ready, w_ready, spm_ready = (
            sem(n) for n in ("z_done", "log_ready", "sp_ready", "w_ready", "spm_ready"))
        after_done, la_ready, att_exp, att_ready, oh_done, oh_ready = (
            sem(n) for n in ("after_done", "la_ready", "att_exp", "att_ready", "oh_done", "oh_ready"))
        baT_ready, lgT_ready, counts_read = sem("baT_ready"), sem("lgT_ready"), sem("counts_read")
        lgt_done, r_exp, r_d, sel_ready, pos_done, items_ready = (
            sem(n) for n in ("lgt_done", "r_exp", "r_d", "sel_ready", "pos_done", "items_ready"))
        prep_col, prep_done, gather_done, back_done, xgh_ready, xgl_ready, back_ready = (
            sem(n) for n in ("prep_col", "prep_done", "gather_done", "back_done", "xgh_ready", "xgl_ready", "back_ready"))
        y_act, y_vec, scat_done, scat_added = sem("y_act"), sem("y_vec"), sem("scat_done"), sem("scat_added")
        out_ready, out_sem = sem("out_ready"), sem("out_sem")

        block = ctx.enter_context(nc.Block())

        def used(eng, i, n=None):
            eng.wait_ge(piece_used, i + 1 if n is None else n * PER + (i + 1))

        def count(n, per, c):
            return c if n is None else n * per + c

        def product(pe, o, a_hi, a_lo, b_hi, b_lo, first, last):
            pe.matmul(o, a_hi, b_hi, start=first, stop=False)
            pe.matmul(o, a_hi, b_lo, start=False, stop=False)
            return pe.matmul(o, a_lo, b_hi, start=False, stop=last)

        @block.sync
        def _(sp):
            for t in range(TILES):
                sp.dma_start(h[:, t, :], x[0, t * P:(t + 1) * P, :]).then_inc(ld_x[t], 16)

            def load_projection(i):
                w, c0 = projection(i)
                if A_OUT <= i < A_FFN or i >= A_WO:
                    for m in range(2):
                        r0 = (2 * (i - (A_OUT if i < A_FFN else A_WO)) + m) * P
                        sp.dma_start(ring[slots[i]][:, m * D:(m + 1) * D], w[r0:r0 + P, :]).then_inc(ring_in[slots[i]], 16)
                    return
                dst = ring[slots[i]][:, :].rearrange("p (c n) -> p c n", c=DC)
                for m in range(2):
                    src = w[m * HC * P:(m + 1) * HC * P, c0:c0 + CW].rearrange("(c p) n -> p c n", p=P)
                    sp.dma_start(dst[:, m * HC:(m + 1) * HC, :], src).then_inc(ring_in[slots[i]], 16)

            def item_sources(p, w1, w3, w2):
                kind, g, half = ITEM[p]
                if kind == "up":
                    rows, cs = slice(half * HC * P, (half + 1) * HC * P), slice(g * CW, (g + 1) * CW)
                    return [(m, w, rows, cs) for m, w in enumerate((w1, w3))]
                return [(m, w2, slice((2 * g + m) * P, (2 * g + m + 1) * P), slice(0, D)) for m in range(2)]

            def destination(i, p, m):
                t = ring[slots[i]]
                if ITEM[p][0] == "up":
                    return t[:, :].rearrange("p (c w n) -> p c w n", c=HC, w=2)[:, :, m, :]
                return t[:, m * D:(m + 1) * D]

            for i in range(A_MOE):
                last = before_it(i)
                if last is not None:
                    sp.wait_ge(lo_done, last + 1)
                elif i >= A_FFN:
                    used(sp, A_FFN - 1)
                if A_FFN <= i < A_QKV:
                    for m, w, rows, cs in item_sources(i - A_FFN, e_ffn_w1, e_ffn_w3, e_ffn_w2):
                        src = w[0, rows, cs]
                        if ITEM[i - A_FFN][0] == "up":
                            src = src.rearrange("(c p) n -> p c n", p=P)
                        sp.dma_start(destination(i, i - A_FFN, m), src).then_inc(ring_in[slots[i]], 16)
                else:
                    load_projection(i)

            def load_item(n, e):
                for p in range(PER):
                    i = A_MOE + p
                    need = before_it(i) + 1 if isinstance(n, int) and n == 0 else sp.snap(n * PER + (A_MOE + p - RING + 1))
                    sp.wait_ge(lo_done, need)
                    for m, w, rows, cs in item_sources(p, o_moe_w1, o_moe_w3, o_moe_w2):
                        src = w[0][bass.ds(e, 1), rows, cs]
                        if ITEM[p][0] == "up":
                            src = src.rearrange("e (c p) n -> p (e c) n", p=P)
                        else:
                            src = src.rearrange("e p d -> p (e d)")
                        sp.dma_start(destination(i, p, m), src).then_inc(ring_in[slots[i]], 16)

            with sp.Fori(0, NE) as e:
                load_item(e, e)
            sp.wait_ge(items_ready, 1)
            n_more = sp.value_load(item_i[0:1, 0, 0:1], min_val=0, max_val=7)
            with sp.If(n_more > 0):
                with sp.Fori(0, n_more) as it:
                    e = sp.value_load(item_i[0:1, 2, bass.ds(it, 1)], min_val=0, max_val=NE - 1)
                    load_item(it + NE, e)
            for t in range(TILES):
                sp.wait_ge(out_ready, t + 1)
                sp.dma_start(out[0, t * P:(t + 1) * P, :], xn[:, t, :]).then_inc(out_sem, 16)
            sp.wait_ge(out_sem, 16 * TILES)

        @block.gpsimd
        def _(pool):
            own = [0]

            def after(ins):
                own[0] += 1
                ins.then_inc(pool_own, 1)
                pool.wait_ge(pool_own, own[0])

            def keep(t, pattern, base, cm, op=ALU.is_ge, fill=0.0):
                after(pool.affine_select(out=t, in_=t, pattern=pattern, compare_op=op, fill=fill, base=base,
                                         channel_multiplier=cm))

            def gain_load(k, g):
                if k >= 2:
                    pool.wait_ge(xn_ready, TILES * (k - 1))
                if k == 1:
                    pool.wait_ge(v_ready, TILES)
                pool.dma_start(gain[:, k % 2, :], g.partition_broadcast(P)).then_inc(ld_gain[k % 2], 16)

            gain_load(0, e_norm1[0])
            after(pool.memset(ident[:, :], 0.0))
            pool.affine_select(out=ident[:, :], in_=ident[:, :], pattern=[[-1, P]], compare_op=ALU.not_equal, fill=1.0,
                               base=0, channel_multiplier=1).then_inc(ident_ready, 1)
            pool.dma_start(w_ba[:, :, :], e_w_in[0][:, BA0:BA0 + 2 * H].rearrange("(c p) n -> p c n", p=P)).then_inc(ld_ba, 16)
            pool.dma_start(rows_raw[0:KCONV * CONV_C, :], e_conv_w[0].rearrange("k (c p) -> (k c) p", p=P)).then_inc(ld_rows, 16)
            pool.dma_start(rows_raw[KCONV * CONV_C:KCONV * CONV_C + 1, :], e_o_norm).then_inc(ld_rows, 16)
            pool.dma_start(small[:, 0, 0, :], e_dt_bias[0].partition_broadcast(P)).then_inc(ld_small, 16)
            pool.dma_start(small[:, 0, 1, :], e_a_log[0].partition_broadcast(P)).then_inc(ld_small, 16)
            pool.memset(conv_in[:, :, 0:KCONV - 1], 0.0).then_inc(pads_ready, 1)
            pool.memset(ones[:, :], 1.0)
            pool.memset(neg_ones[:, :], -1.0)
            after(pool.memset(before[:, :], 1.0))
            keep(before[:, :], [[1, P]], -1, -1)
            after(pool.memset(neg_after[:, :], -1.0))
            keep(neg_after[:, :], [[-1, P]], -1, 1)
            after(pool.memset(blk_ones[:, :], 1.0))
            halves = blk_ones[:, :].rearrange("p (a n) -> p a n", n=CH)
            keep(halves, [[-CH, P // CH], [0, CH]], 0, 1)
            keep(halves, [[CH, P // CH], [0, CH]], CH - 1, -1)
            after(pool.affine_select(out=tri_blk[:, :], in_=blk_ones[:, :], pattern=[[1, P]], compare_op=ALU.is_ge,
                                     fill=0.0, base=0, channel_multiplier=-1))
            after(pool.memset(level[:, :, :], 0.0))
            for k in range(LEVELS):
                b = 2 ** k
                v = level[:, k, :].rearrange("p (a n) -> p a n", n=2 * b)[:, :, 0:b]
                after(pool.memset(v, 1.0))
                keep(v, [[-2 * b, P // (2 * b)], [0, b]], -b, 1)
                keep(v, [[2 * b, P // (2 * b)], [0, b]], 2 * b - 1, -1)
            pool.iota(iota[:, :], [[1, P]], base=0, channel_multiplier=0,
                      allow_small_or_imprecise_dtypes=True).then_inc(pool_own, 1)
            own[0] += 1
            after(pool.memset(ws_raw[0:CH, :, CH:P], 0.0))
            pool.drain().then_inc(consts_ready, 1)
            w = e_sgu_w[0].rearrange("g t s -> t g s")
            pool.dma_start(ws_raw[0:CH, :, 0:CH], w[0:CH, :, 0:CH]).then_inc(ld_ws, 16)
            pool.dma_start(ws_raw[CH:P, :, :], w[CH:P]).then_inc(ld_ws, 16)
            pool.dma_start(ln_g, e_sgu_ln_g[0].partition_broadcast(P)).then_inc(ld_lng, 16)
            pool.dma_start(ln_b, e_sgu_ln_b[0].partition_broadcast(P)).then_inc(ld_lng, 16)
            for m in range(2):
                b = e_sgu_b[0].rearrange("(c m) t -> m c t", m=2)[m].partition_broadcast(CH)
                pool.dma_start(sgu_bias[m * CH:(m + 1) * CH, :, :], b).then_inc(ld_bias, 16)
            pool.wait_ge(ln_var, 1)
            after(pool.tensor_scalar(stat_ln[:, 0, :], mv[:, :, 1], EPS, None, ALU.add))
            pool.tensor_tensor(stat_ln[:, 1, :], stat_ln[:, 0, :], const[:, 3:4].to_broadcast([P, TILES]), ALU.pow)\
                .then_inc(ln_rstd, 1)
            gain_load(1, e_norm2[0])
            gain_load(2, o_norm1[0])
            gain_load(3, o_norm2[0])
            used(pool, A_FFN - 1)
            pool.dma_start(w_router[:, :, :], o_router[0].rearrange("(c p) e -> p c e", p=P)).then_inc(ld_wr, 16)
            mask2 = before[:, :].unsqueeze(1).to_broadcast([P, 2, P])

            def diag(t):
                return t[:, 0:2 * P].rearrange("p (a n) -> p a n", a=2)

            def mask_sp(i):
                pool.wait_ge(sp_ready, i + 1)
                pool.tensor_tensor(diag(sp_m[:, i % 2]), diag(sp_m[:, i % 2]), mask2, ALU.mult).then_inc(spm_ready, 1)

            def mask_att(i):
                pool.wait_ge(att_exp, i + 1)
                pool.tensor_tensor(diag(att[:, i % 2]), diag(att[:, i % 2]), mask2, ALU.mult).then_inc(att_ready, 1)

            for i in range(SB_H + 1):
                if i < SB_H:
                    mask_sp(i)
                if i >= 1:
                    mask_att(i - 1)
            pool.wait_ge(att_exp, SB_H)
            gain_load(4, final_norm)

        @block.scalar
        def _(act):
            own = [0]

            def after(ins):
                own[0] += 1
                ins.then_inc(act_own, 1)
                act.wait_ge(act_own, own[0])

            def norm(k, transposed=True, between=None):
                for t in range(TILES):
                    if k:
                        act.wait_ge(h_ready, TILES * (k - 1) + t + 1)
                    else:
                        act.wait_ge(ld_x[t], 16)
                    after(act.activation(xn[:, t, :], h[:, t, :], ACT.Square, accum_out=stat[:, k, t:t + 1]))
                    after(act.activation(stat[:, k, 2 + t:3 + t], stat[:, k, t:t + 1], ACT.Ln, scale=1.0 / D, bias=eps_col))
                    act.activation(stat[:, k, 4 + t:5 + t], stat[:, k, 2 + t:3 + t], ACT.Exp, scale=-0.5).then_inc(rinv_ready, 1)
                if between is not None:
                    between()
                if transposed:
                    for b in range(4):
                        act.wait_ge(xnT_done, 4 * k + b + 1)
                        act.activation(x_hi[:, 2 * b:2 * b + 2, :], ps[:, b, :].rearrange("p (c n) -> p c n", c=2),
                                       ACT.Copy).then_inc(xh_ready, 1)

            def split_hi(i, n=None):
                if n is None:
                    act.wait_ge(ring_in[slots[i]], arrivals(i))
                    if i >= SPLITS:
                        used(act, i - SPLITS)
                else:
                    act.wait_ge(ring_in[slots[i]], n * PER_SLOT + arrivals(i))
                    used(act, i - SPLITS, n)
                act.activation(w_hi[i % SPLITS][:, :], ring[slots[i]][:, :], ACT.Copy).then_inc(hi_done, 1)

            act.wait_ge(vec_own, 1)
            act.preload_act_table_set(EXP_LN)
            norm(0, between=lambda: split_hi(0))
            split_hi(1)
            act.wait_ge(ld_ba, 16)
            act.activation(ba_hi[:, :, :], w_ba[:, :, :], ACT.Copy).then_inc(bah_ready, 1)
            split_hi(2)
            act.wait_ge(ba_sb, 1)
            act.activation(small[:, 1], ba[:, :, 0:H], ACT.Exp, scale=-1.0).then_inc(gb_act, 1)
            act.wait_ge(ld_small, 32)
            act.activation(small[:, 2, 0, :], small[:, 0, 1, :], ACT.Exp).then_inc(gb_act, 1)
            act.wait_ge(gb_vec, 1)
            after(act.activation(small[:, 5], small[:, 4], ACT.Exp, scale=-1.0))
            act.activation(small[:, 6], small[:, 5], ACT.Ln, bias=one_col).then_inc(gb_act, 1)

            act.preload_act_table(ACT.Silu)
            def copy_conv(i):
                used(act, i)
                if i == 0:
                    act.wait_ge(pads_ready, 1)
                    act.wait_ge(colt_ready, 1)
                act.activation(conv_in[:, 2 * i:2 * i + 2, KCONV - 1:], ps[:, i % 4, :].rearrange("p (c n) -> p c n", c=2),
                               ACT.Copy)
                for m in range(2):
                    c = (KCONV - 1) * CONV_C + 2 * i + m
                    ins = act.activation(qkvT[:, 2 * i + m, :], ps[:, i % 4, m * SEQ:(m + 1) * SEQ], ACT.Copy,
                                         scale=colt[:, c:c + 1])
                ins.then_inc(act_evac, 1)

            def silu_conv(i):
                act.wait_ge(conv_done, i + 1)
                act.activation(qkvT[:, 2 * i:2 * i + 2, :], qkvT[:, 2 * i:2 * i + 2, :], ACT.Silu).then_inc(silu_even, 1)

            flat_row = exp_row[:, :, :, :].rearrange("p h t n -> p (h t n)")
            for i in range(6):
                copy_conv(i)
                split_hi(i + SPLITS)
                if i >= 1:
                    silu_conv(i - 1)
                if i == 3:
                    act.wait_ge(row_done, 1)
                    act.activation(flat_row, two(4), ACT.Copy).then_inc(row_copied, 1)
                if i == 4:
                    act.wait_ge(silu_even, 4)
                    act.activation(rn[:, :, :], qkvT[:, 0:2 * H, :], ACT.Square).then_inc(sq_ready, 1)
            silu_conv(5)

            act.preload_act_table_set(EXP_LN)
            flat = rn[:, :, :].rearrange("p a b -> p (a b)")
            half = H * SEQ
            act.wait_ge(l2_done, 1)
            after(act.activation(flat[:, half:], two(2), ACT.Ln, bias=eps_col))
            act.activation(flat[:, half:], flat[:, half:], ACT.Exp, scale=-0.5).then_inc(rn_ready, 1)
            act.wait_ge(gam_arg, U)
            act.activation(gam[:, :, :], gam[:, :, :], ACT.Exp).then_inc(gam_exp, 1)
            act.wait_ge(l2_done, 2)
            after(act.activation(flat[:, 0:half], two(0), ACT.Ln, bias=eps_col))
            act.activation(flat[:, 0:half], flat[:, 0:half], ACT.Exp, scale=-0.5, bias=qscale_col).then_inc(rn_ready, 1)

            def evac_gate(i):
                used(act, i)
                act.activation(yT[:, 4 + 2 * (i - 6):6 + 2 * (i - 6), :], ps[:, i - 2, :].rearrange("p (c n) -> p c n", c=2),
                               ACT.Copy).then_inc(act_evac, 1)
                split_hi(i + SPLITS)

            evac_gate(6)
            act.wait_ge(gc_sb, 1)
            act.activation(small[:, 10], small[:, 8], ACT.Exp).then_inc(gcols_act, 1)
            act.activation(small[:, 12], small[:, 11], ACT.Exp).then_inc(gcols_act, 1)
            act.activation(flat_row, flat_row, ACT.Exp).then_inc(exp_row_ready, 1)
            evac_gate(7)
            act.wait_ge(turn_done, 1)
            act.wait_ge(gcols_act, 2)
            for u in range(U):
                hd, t = u // TILES, u % TILES
                act.activation(kd[:, u, :], two(4)[:, u * P:(u + 1) * P], ACT.Copy,
                               scale=small[:, 12, t, hd:hd + 1]).then_inc(kd_ready, 1)
            act.wait_ge(kbe_scale, 1)
            for u in range(U):
                hd, t = u // TILES, u % TILES
                act.activation(kbe[:, u, :], two(4)[:, u * P:(u + 1) * P], ACT.Copy,
                               scale=small[:, 13, t, hd:hd + 1]).then_inc(kbe_ready, 1)
            act.preload_act_table(ACT.Gelu_apprx_tanh)
            for i in (8, 9):
                used(act, i)
                act.activation(v_nat[:, :, (i - 8) * CW:(i - 7) * CW], ps[:, 4 + i % 2, :].rearrange("p (t n) -> p t n", t=TILES),
                               ACT.Gelu_apprx_tanh).then_inc(act_evac, 1)
                split_hi(i + SPLITS)
            for i in (10, 11):
                used(act, i)
                act.activation(yT[:, 2 * (i - 10):2 + 2 * (i - 10), :], ps[:, 4 + i % 2, :].rearrange("p (c n) -> p c n", c=2),
                               ACT.Gelu_apprx_tanh).then_inc(act_evac, 1)
                split_hi(i + SPLITS)
            act.preload_act_table(ACT.Silu)
            act.wait_ge(act_evac, 8)
            act.activation(yT[:, 4:8, :], yT[:, 4:8, :], ACT.Silu).then_inc(gate_ready, 1)
            act.preload_act_table_set(EXP_LN)
            act.wait_ge(sol_done, 1)
            act.activation(w_solT.rearrange("p u n -> p (u n)"), two(0), ACT.Copy).then_inc(sol_w, 1)
            for c in range(NCH):
                if c == 1:
                    act.wait_ge(ya_ready, 1)
                    act.activation(x_hi[:, 0:4, :], yT[:, 0:4, :], ACT.Copy).then_inc(yh_ready, 1)
                act.wait_ge(o_done, c + 1)
                act.activation(oT[:, :, c * CH:(c + 1) * CH], ps[:, (7, 3)[c % 2], 0:H * CH].rearrange("p (h n) -> p h n", h=H),
                               ACT.Copy).then_inc(o_sb, 1)
            act.wait_ge(o_sb, NCH)
            act.activation(rn[:, 0:H, :], oT, ACT.Square).then_inc(osq_ready, 1)
            for b in range(2):
                hs = slice(H + 2 * b, H + 2 * b + 2)
                act.wait_ge(on_done, b + 1)
                after(act.activation(rn[:, hs, :].rearrange("p a b -> p (a b)"), ps[:, 2 + b, :], ACT.Ln, scale=1.0 / DK,
                                     bias=eps_col))
                act.activation(rn[:, hs, :], rn[:, hs, :], ACT.Exp, scale=-0.5).then_inc(on_ready, 1)
            for b in range(2):
                act.wait_ge(yb_ready, b + 1)
                act.activation(x_hi[:, 4 + 2 * b:6 + 2 * b, :], yT[:, 4 + 2 * b:6 + 2 * b, :], ACT.Copy).then_inc(yh_ready, 1)
            for i in (15, 16, 17):
                split_hi(i)
            norm(1, between=lambda: split_hi(18))

            def ffn(tiles, first, unit0, group0, ahead, n=None, parts=ALL_PARTS, extra={}):
                def silu(g):
                    used(act, first + at_up(g, 1), n)
                    for t in range(tiles):
                        bank = 4 + (tiles * g + t) % (tiles + 1)
                        if tiles * g + t >= 1 or n is not None:
                            act.wait_ge(act_ready, count(n, FG, unit0 + tiles * (g - 1) + t + 1))
                        act.activation(silu_s[:, t, :], ps[:, bank, 0:CW], ACT.Silu).then_inc(silu_done, 1)

                def turned(g):
                    act.wait_ge(hT_done, count(n, FG, group0 + g + 1))
                    if g >= 2:
                        used(act, first + at_down(g - 2), n)
                    act.activation(hT_hi[:, g % 2, :, 0:tiles * P], ps[:, 7 if tiles == 2 else 3, 0:2 * tiles * P].rearrange(
                        "p (j n) -> p j n", j=2), ACT.Copy).then_inc(hTh_ready, 1)

                for p in parts:
                    kind, g, half = ITEM[p]
                    if kind == "up" and half == 1:
                        silu(g)
                    if kind == "up" and half == 0 and g >= 1:
                        turned(g - 1)
                    if p == PER - 2:
                        turned(FG - 1)
                    if p in extra:
                        extra[p]()
                    if p + SPLITS < PER + ahead:
                        split_hi(first + p + SPLITS, n)

            act.preload_act_table(ACT.Silu)
            ffn(TILES, A_FFN, 0, 0, SPLITS - 1)

            act.preload_act_table_set(EXP_LN)
            norm(2, between=lambda: split_hi(A_QKV + SPLITS - 1))
            for i in range(N_QK):
                used(act, A_QKV + i)
                src = ps[:, i % 4, :].rearrange("p (c n) -> p c n", c=2)
                if i < 4:
                    ins = act.activation(qT[:, 2 * i:2 * i + 2, :], src, ACT.Copy, scale=float(SB_D) ** -0.5)
                else:
                    ins = act.activation(kT[:, 2 * i - 8:2 * i - 6, :], src, ACT.Copy)
                ins.then_inc(act_evac, 1)
                split_hi(A_QKV + i + SPLITS)
            def log_part(i):
                act.wait_ge(z_done, i + 1)
                if i >= 2:
                    act.wait_ge(w_ready, i - 1)
                after(act.activation(lg[:, i % 2], ps[:, i % 2, 0:NZ], ACT.Abs))
                after(act.activation(lg[:, i % 2], lg[:, i % 2], ACT.Exp, scale=-1.0))
                act.activation(lg[:, i % 2], lg[:, i % 2], ACT.Ln, bias=one_col).then_inc(log_ready, 1)

            def att_part(i):
                act.wait_ge(la_ready, i + 1)
                if i >= 2:
                    act.wait_ge(oh_done, i - 1)
                act.activation(att[:, i % 2], w_log[:, i % 2], ACT.Exp).then_inc(att_exp, 1)

            def evac_v(j):
                used(act, A_QKV + N_QK + j)
                act.activation(v_att[:, :, j * CW:(j + 1) * CW], ps[:, 2, :].rearrange("p (t n) -> p t n", t=TILES),
                               ACT.Copy).then_inc(act_evac, 1)
                split_hi(A_QKV + N_QK + j + SPLITS)

            def head_hi(pr):
                act.wait_ge(oh_done, 2 * pr + 2)
                if pr == 0:
                    used(act, A_WO - 1)
                act.activation(x_hi[:, pr, :], ps[:, 6 + pr % 2, 0:SEQ], ACT.Copy).then_inc(oh_hi, 1)

            for i in range(SB_H + 2):
                if i < SB_H:
                    log_part(i)
                if i >= 2:
                    att_part(i - 2)
                if 1 <= i <= N_QKV - N_QK:
                    evac_v(i - 1)
                if i >= 5 and i % 2 == 1:
                    head_hi((i - 5) // 2)
            head_hi(SB_H // 2 - 1)
            act.wait_ge(ld_wr, 16)
            act.activation(wr_hi[:, :, :], w_router[:, :, :], ACT.Copy).then_inc(wrh_ready, 1)
            for i in range(A_MOE - 1, A_MOE + 2):
                split_hi(i)
            norm(3)
            split_hi(A_MOE + 2)
            act.wait_ge(r_d, 1)
            act.activation(r_small[:, 1], r_small[:, 0], ACT.Exp).then_inc(r_exp, 1)
            act.preload_act_table(ACT.Silu)

            def evac_y(n):
                used(act, A_MOE + PER - 1, n)
                act.activation(y_exp[:, 512:D], ps[0:SLOTS, 1, :], ACT.Copy).then_inc(y_act, 1)

            def evac_xg(k):
                for b in range(2):
                    act.wait_ge(gather_done, k * 2 + (b + 1))
                    act.activation(x_hi[:, 4 * b:4 * b + 4, 0:SLOTS], ps[:, 6 + b, :].rearrange("p (c n) -> p c n", c=4),
                                   ACT.Copy).then_inc(xgh_ready, 1)

            def expert(n, ahead, parts):
                def before_end():
                    if ahead:
                        evac_xg(n + 1)
                    evac_y(n)
                ffn(1, A_MOE, TILES * FG, FG, ahead, n, parts, {PER - 1: before_end})

            evac_xg(0)
            expert(0, SPLITS, HEAD)
            with act.Fori(0, NE - 1) as n:
                expert(n, SPLITS, REST)
                expert(n + 1, SPLITS, HEAD)
            expert(NE - 1, 0, REST)
            act.wait_ge(items_ready, 1)
            n_more = act.value_load(item_i[0:1, 0, 0:1], min_val=0, max_val=7)
            with act.If(n_more > 0):
                with act.Fori(0, n_more) as it:
                    for p in range(SPLITS):
                        split_hi(A_MOE + p, it + NE)
                    evac_xg(it + NE)
                    expert(it + NE, 0, ALL_PARTS)
            act.preload_act_table_set(EXP_LN)
            norm(4, False)

        @block.tensor
        def _(pe):
            mm = pe.matmul

            def norm_turn(k):
                if k == 0:
                    pe.wait_ge(ident_ready, 1)
                for t in range(TILES):
                    pe.wait_ge(xn_ready, TILES * k + t + 1)
                    for b in range(4):
                        for c in (2 * b, 2 * b + 1):
                            at = (c % 2) * SEQ + t * P
                            last = pe.transpose(ps[:, b, at:at + P], xn[:, t, c * P:(c + 1) * P], ident[:, :])
                        if t == TILES - 1:
                            last.then_inc(xnT_done, 1)

            def x_part(k, c):
                if k is not None and c % 2 == 0:
                    pe.wait_ge(xl_ready, 4 * k + c // 2 + 1)

            def piece(i):
                pe.wait_ge(lo_done, i + 1)
                return [w[i % SPLITS][:, :].rearrange("p (c n) -> p c n", c=DC) for w in (w_hi, w_lo)]

            def project_T(i, bank, parts=range(2), fresh=None):
                hi, lo = piece(i)
                for m in parts:
                    ms = slice(m * P, (m + 1) * P)
                    for c in range(DC):
                        x_part(fresh, c)
                        last = product(pe, ps[:, bank, m * SEQ:(m + 1) * SEQ], hi[:, c, ms], lo[:, c, ms], x_hi[:, c, :],
                                       x_lo[:, c, :], c == 0, c == DC - 1)
                if m == 1:
                    last.then_inc(piece_used, 1)

            def project_N(i, bank, parts=range(TILES)):
                hi, lo = piece(i)
                for t in parts:
                    tok = slice(t * P, (t + 1) * P)
                    for c in range(DC):
                        last = product(pe, ps[:, bank, t * CW:(t + 1) * CW], x_hi[:, c, tok], x_lo[:, c, tok], hi[:, c, :],
                                       lo[:, c, :], c == 0, c == DC - 1)
                if t == TILES - 1:
                    last.then_inc(piece_used, 1)

            def narrow(bank, hi, lo, fresh=None):
                n = hi.shape[2]
                for c in range(DC):
                    x_part(fresh, c)
                    last = product(pe, ps[0:n, bank, 0:SEQ], hi[:, c, :], lo[:, c, :], x_hi[:, c, :], x_lo[:, c, :],
                                   c == 0, c == DC - 1)
                return last

            def narrow_turn(bank, zT):
                n = zT.shape[0]
                for t in range(TILES):
                    last = pe.transpose(ps[:, bank, t * n:(t + 1) * n], zT[:, t * P:(t + 1) * P], ident[0:n, 0:n])
                return last

            norm_turn(0)
            project_T(0, 0, fresh=0)
            n_rows = KCONV * CONV_C + 1
            pe.wait_ge(ld_rows, 32)
            pe.transpose(ps[:, 6, 0:n_rows], rows_raw[0:n_rows, :], ident[0:n_rows, 0:n_rows]).then_inc(rows_done, 1)
            pe.wait_ge(bal_ready, 1)
            narrow(7, ba_hi, ba_lo).then_inc(ba_done, 1)

            def decay_rows():
                pe.wait_ge(consts_ready, 1)
                pe.wait_ge(g_ready, 1)
                pe.wait_ge(wsT_ready, 1)
                g = small[:, 7].rearrange("p t h -> p (t h)")
                mm(ps[:, 6, 0:U], tri_blk[:, :], g, start=True, stop=True)
                mm(ps[:, 6, U:2 * U], blk_ones[:, :], g, start=True, stop=True).then_inc(gc_done, 1)
                for u in range(U):
                    last = mm(two(4)[:, u * P:(u + 1) * P], small[:, 7, u % TILES, u // TILES:u // TILES + 1].to_broadcast([P, P]),
                              tri_blk[:, :], start=True, stop=True)
                last.then_inc(row_done, 1)

            def beta_rows():
                pe.wait_ge(gc_sb, 1)
                for u in range(U):
                    last = mm(two(6)[:, u * P:(u + 1) * P], small[:, 3, u % TILES, u // TILES:u // TILES + 1].to_broadcast([P, P]),
                              ident[:, :], start=True, stop=True)
                last.then_inc(row_done, 1)

            for i in range(1, 6):
                if i >= 4:
                    pe.wait_ge(act_evac, i - 3)
                if i == 1:
                    project_T(1, 1, [0])
                    pe.wait_ge(baT_ready, 1)
                    narrow_turn(7, ba_T).then_inc(ba_done, 1)
                    project_T(1, 1, [1])
                else:
                    project_T(i, i % 4)
                if i == 1:
                    pe.wait_ge(ld_ws, 32)
                    for g in range(G):
                        last = pe.transpose(two(4)[:, g * P:(g + 1) * P], ws_raw[:, g, :], ident[:, :])
                    last.then_inc(wsT_done, 1)
                if i == 2:
                    decay_rows()
                if i == 4:
                    beta_rows()
            pe.wait_ge(sq_ready, 1)
            pe.wait_ge(act_evac, 6)
            for b in (2, 3, 0, 1):
                last = mm(ps[:, b, :], ones[:, :], rn[:, 2 * b:2 * b + 2, :].rearrange("p a b -> p (a b)"), start=True, stop=True)
                if b % 2:
                    last.then_inc(l2_done, 1)
            pe.wait_ge(row_copied, 1)
            for i in (6, 7):
                project_T(i, i - 2)
            pe.wait_ge(rn_ready, 2)
            for m, src in enumerate((kbT, qkvT)):
                pe.wait_ge(kb_ready, m + 1)
                for u in range(U):
                    hd, t = u // TILES, u % TILES
                    last = mm(two(2 * m)[:, u * P:(u + 1) * P], qkvT[:, H + hd, t * P:(t + 1) * P],
                              src[:, hd, t * P:(t + 1) * P], start=True, stop=True)
                last.then_inc(kk_done, 1)
            pe.wait_ge(act_evac, 8)
            pe.wait_ge(silu_even, 6)
            for m in range(2):
                for u in range(U):
                    hd, t = u // TILES, u % TILES
                    last = pe.transpose(two(4 + 2 * m)[:, u * P:(u + 1) * P], qkvT[:, (1 + m) * H + hd, t * P:(t + 1) * P],
                                        ident[:, :])
                last.then_inc(turn_done, 1)

            def gate_mix():
                pe.wait_ge(v_ready, TILES)
                pe.wait_ge(act_evac, 12)
                for t in range(TILES):
                    for g in range(G):
                        at = (g // 2) * SEQ + t * P
                        last = mm(two(4)[(g % 2) * GD:(g % 2 + 1) * GD, at:at + P], v_nat[:, t, g * GD:(g + 1) * GD],
                                  wsT[:, g, :], start=True, stop=True)
                last.then_inc(mix_done, 1)

            pe.wait_ge(lt_ready, 1)
            fillers = [[(8, 0)], [(8, 1)], [(9, 0), (9, 1)], [(10, 0), (10, 1)], [(11, 0)], [(11, 1)]]
            for k in range(LEVELS):
                for hf in range(2):
                    if k:
                        pe.wait_ge(x_ready, 2 * k + hf - 1)
                    for m in range(4):
                        u = 4 * hf + m
                        last = mm(ps[:, hf, m * P:(m + 1) * P], lower[:, u, :], inv_x[:, u, :] if k else ident[:, :],
                                  start=True, stop=True)
                    last.then_inc(t_done, 1)
                for i, half in fillers[k]:
                    if i == 8 and half == 0:
                        pe.wait_ge(kbe_ready, U)
                    if i >= 10 and half == 0:
                        pe.wait_ge(act_evac, i - 1)
                    (project_N if i < 10 else project_T)(i, 4 + i % 2, [half])
                if k == 0:
                    pe.wait_ge(attn_ready, 1)
                    pe.wait_ge(vb_ready, U)
                for hf in range(2):
                    pe.wait_ge(t_ready, 2 * k + hf + 1)
                    if k:
                        pe.wait_ge(xt_ready, 2 * k + hf - 1)
                    if 0 < k < LEVELS - 1:
                        for m in range(4):
                            u = 4 * hf + m
                            last = mm(ps[:, 6 + hf, m * P:(m + 1) * P], inv_xt[:, u, :],
                                      inv_t[:, u, :], start=True, stop=True)
                        last.then_inc(x_done, 1)
                    for m in range(4):
                        u = 4 * hf + m
                        last = mm(ps[:, 2 + hf, m * P:(m + 1) * P], inv_t[:, u, :], inv_xt[:, u, :] if k else ident[:, :],
                                  start=True, stop=True)
                    last.then_inc(xt_done, 1)
            gate_mix()
            pe.wait_ge(xt_ready, 2 * LEVELS)
            for u in range(U):
                last = mm(two(0)[:, u * P:(u + 1) * P], kbe[:, u, :], inv_xt[:, u, :], start=True, stop=True)
            last.then_inc(sol_done, 1)
            for u in range(U):
                last = mm(two(6)[:, u * P:(u + 1) * P], inv_xt[:, u, :], vb[:, u, :], start=True, stop=True)
            last.then_inc(sol_done, 1)
            pe.wait_ge(sol_w, 1)
            pe.wait_ge(qd_ready, 1)
            for c in range(NCH):
                t, p0 = c // 2, (c % 2) * CH
                rows, tok = slice(p0, p0 + CH), slice(c * CH, (c + 1) * CH)
                if c == 0:
                    pe.wait_ge(sol_u, 1)
                if c:
                    pe.wait_ge(st_ready, c)
                    for hd in range(H):
                        last = mm(ps[rows, 6, hd * P:(hd + 1) * P], w_solT[:, hd * TILES + t, rows], state[:, hd, :],
                                  start=True, stop=True)
                    last.then_inc(ws_done, 1)
                    if c >= 2:
                        pe.wait_ge(o_sb, c - 1)
                    for hd in range(H):
                        mm(ps[:, (7, 3)[c % 2], hd * CH:(hd + 1) * CH], state[:, hd, :], qkvT[:, hd, tok], start=(hd == 0),
                           stop=False)
                pe.wait_ge(vnew_ready, c + 1)
                if c < NCH - 1:
                    for hd in range(H):
                        last = mm(ps[:, 2, hd * P:(hd + 1) * P], kd[rows, hd * TILES + t, :],
                                  v_new[rows, t, hd * P:(hd + 1) * P], start=True, stop=True)
                    last.then_inc(st_done, 1)
                for hd in range(H):
                    o = ps[:, (7, 3)[c % 2], hd * CH:(hd + 1) * CH]
                    last = mm(o, v_new[rows, t, hd * P:(hd + 1) * P], gam[rows, hd * TILES + t, rows],
                              start=(c == 0 and hd == 0), stop=(hd == H - 1))
                last.then_inc(o_done, 1)

            def out_rows(first, banks, *chunks):
                for t in range(TILES):
                    tok = slice(t * P, (t + 1) * P)
                    for c in chunks:
                        i = first + c // 2
                        pe.wait_ge(lo_done, i + 1)
                        for hf in range(2):
                            cs = slice((c % 2) * D + hf * 512, (c % 2) * D + (hf + 1) * 512)
                            last = product(pe, ps[:, banks[2 * t + hf], :], x_hi[:, c, tok], x_lo[:, c, tok],
                                           w_hi[i % SPLITS][:, cs], w_lo[i % SPLITS][:, cs], c == 0, c == DC - 1)
                    if c == DC - 1 and t == 0:
                        last.then_inc(tile_summed, 1)
                if c % 2:
                    last.then_inc(piece_used, 1)

            pe.wait_ge(yl_ready, 1)
            out_rows(A_OUT, OUT_BANKS, 0)
            pe.wait_ge(osq_ready, 1)
            for b in range(2):
                mm(ps[:, 2 + b, :], ones[:, :], rn[:, 2 * b:2 * b + 2, :].rearrange("p a b -> p (a b)"), start=True, stop=True)\
                    .then_inc(on_done, 1)
            for c in range(1, 4):
                out_rows(A_OUT, OUT_BANKS, c)
            for c in (4, 6):
                pe.wait_ge(yl_ready, c // 2)
                out_rows(A_OUT, OUT_BANKS, c, c + 1)

            def ffn(tiles, first, unit0, group0, x, n=None, between=None, parts=ALL_PARTS, fresh=None):
                nb, t_bank = tiles + 1, 7 if tiles == 2 else 3

                def up(g, half):
                    i = first + at_up(g, half)
                    if n is not None and g == 0:
                        pe.wait_ge(xgl_ready, n * 2 + (half + 1))
                    pe.wait_ge(lo_done, count(n, PER, i + 1))
                    hi, lo = (w[i % SPLITS][:, :].rearrange("p (c n) -> p c n", c=HC) for w in (w_hi, w_lo))
                    for t in range(tiles):
                        u = tiles * g + t
                        if half == 0 and (u >= nb or n is not None):
                            pe.wait_ge(act_ready, count(n, FG, unit0 + max(u - nb + 1, 0)))
                        tok = slice(t * P, (t + 1) * P)
                        for c in range(HC):
                            cc = half * HC + c
                            x_part(fresh if g == 0 and t == 0 else None, cc)
                            last = product(pe, ps[:, 4 + u % nb, :], x[0][:, cc, tok], x[1][:, cc, tok], hi[:, c, :],
                                           lo[:, c, :], cc == 0, cc == DC - 1)
                    last.then_inc(piece_used, 1)

                def turn(g):
                    pe.wait_ge(act_ready, count(n, FG, unit0 + tiles * (g + 1)))
                    if n is not None and g == 0:
                        pe.wait_ge(back_ready, n + 1)
                    elif g:
                        pe.wait_ge(hTl_ready, count(n, FG, group0 + g))
                    for j in range(2):
                        for t in range(tiles):
                            at = (j * tiles + t) * P
                            last = pe.transpose(ps[:, t_bank, at:at + P], h_act[:, g % 2, t, j * P:(j + 1) * P], ident[:, :])
                    last.then_inc(hT_done, 1)

                def down(g):
                    i = first + at_down(g)
                    pe.wait_ge(lo_done, count(n, PER, i + 1))
                    pe.wait_ge(hTl_ready, count(n, FG, group0 + g + 1))
                    for t in range(tiles):
                        tok = slice(t * P, (t + 1) * P)
                        for j in range(2):
                            for hf in range(2):
                                cs = slice(j * D + hf * 512, j * D + (hf + 1) * 512)
                                last = product(pe, ps[:, 2 * t + hf, :], hT_hi[:, g % 2, j, tok], hT_lo[:, g % 2, j, tok],
                                               w_hi[i % SPLITS][:, cs], w_lo[i % SPLITS][:, cs],
                                               g == 0 and j == 0, g == FG - 1 and j == 1)
                        if g == FG - 1 and t == 0 and tiles > 1:
                            last.then_inc(tile_summed, 1)
                    last.then_inc(piece_used, 1)

                for p in parts:
                    kind, g, half = ITEM[p]
                    if kind == "up":
                        up(g, half)
                        if half == 0 and g:
                            turn(g - 1)
                    else:
                        if g == FG - 1:
                            turn(g)
                            if between is not None:
                                between()
                        down(g)

            norm_turn(1)
            ffn(TILES, A_FFN, 0, 0, (x_hi, x_lo), fresh=1)
            norm_turn(2)
            for i in range(N_QK):
                if i >= 4:
                    pe.wait_ge(act_evac, 12 + i - 3)
                project_T(A_QKV + i, i % 4, fresh=2 if i == 0 else None)
            pe.wait_ge(act_evac, 12 + N_QK)

            def scores(i):
                rows = slice((i % 2) * SB_D, (i % 2 + 1) * SB_D)
                if i >= 2:
                    pe.wait_ge(w_ready, i - 1)
                for b, (s, t) in enumerate(((0, 0), (1, 1), (0, 1))):
                    last = mm(ps[:, i % 2, b * P:(b + 1) * P], kT[rows, i // 2, s * P:(s + 1) * P],
                              qT[rows, i // 2, t * P:(t + 1) * P], start=True, stop=True)
                last.then_inc(z_done, 1)

            def sums_after(i):
                pe.wait_ge(spm_ready, i + 1)
                if i >= 3:
                    pe.wait_ge(la_ready, i - 2)
                o = ps[:, 3 + i % 3]
                mm(o[:, 0:2 * P], neg_after[:, :], sp_m[:, i % 2, 0:2 * P], start=True, stop=True)
                mm(o[:, 2 * P:NZ], neg_after[:, :], sp_m[:, i % 2, 2 * P:NZ], start=True, stop=False)
                mm(o[:, 2 * P:NZ], neg_ones[:, :], sp_m[:, i % 2, P:2 * P], start=False, stop=True).then_inc(after_done, 1)

            def head_o(i):
                pe.wait_ge(att_ready, i + 1)
                pe.wait_ge(act_evac, 12 + N_QK + i // (CW // SB_D) + 1)
                pr = i // 2
                if pr >= 2:
                    pe.wait_ge(oh_ready, pr - 1)
                o = ps[(i % 2) * SB_D:(i % 2 + 1) * SB_D, 6 + pr % 2]
                mm(o[:, 0:P], v_att[:, 0, i * SB_D:(i + 1) * SB_D], att[:, i % 2, 0:P], start=True, stop=True)
                mm(o[:, P:2 * P], v_att[:, 0, i * SB_D:(i + 1) * SB_D], att[:, i % 2, 2 * P:NZ], start=True, stop=False)
                mm(o[:, P:2 * P], v_att[:, 1, i * SB_D:(i + 1) * SB_D], att[:, i % 2, P:2 * P], start=False, stop=True)\
                    .then_inc(oh_done, 1)

            scores(0)
            scores(1)
            for i in range(SB_H + 2):
                if i < N_QKV - N_QK:
                    if i:
                        pe.wait_ge(act_evac, 12 + N_QK + i)
                    project_N(A_QKV + N_QK + i, 2)
                if i + 2 < SB_H:
                    scores(i + 2)
                if i < SB_H:
                    sums_after(i)
                if i == SB_H:
                    pe.wait_ge(la_ready, SB_H)
                if i >= SB_H:
                    c = i - SB_H
                    pe.wait_ge(oh_ready, c + 1)
                    out_rows(A_WO, ATT_OUT_BANKS, c)
                if i >= 2:
                    head_o(i - 2)
            for c in (2, 3, 4, 5):
                pe.wait_ge(oh_ready, c + 1)
                out_rows(A_WO, ATT_OUT_BANKS, c)
            pe.wait_ge(oh_ready, SB_H // 2)
            out_rows(A_WO, ATT_OUT_BANKS, 6, 7)
            norm_turn(3)
            pe.wait_ge(wrl_ready, 1)
            narrow(6, wr_hi, wr_lo, fresh=3).then_inc(lgt_done, 1)
            pe.wait_ge(lgT_ready, 1)
            narrow_turn(6, logits_T).then_inc(lgt_done, 1)
            pe.wait_ge(sel_ready, 1)
            o = ps[:, 7]
            mm(o[:, 0:NE], before[:, :], r2[:, 3, 0, :], start=True, stop=True)
            mm(o[:, NE:2 * NE], before[:, :], r2[:, 3, 1, :], start=True, stop=False)
            mm(o[:, NE:2 * NE], ones[:, :], r2[:, 3, 0, :], start=False, stop=True).then_inc(pos_done, 1)
            mm(ps[:, 5, 0:NE], ones[:, :], r2[:, 3, 0, :], start=True, stop=False)
            mm(ps[:, 5, 0:NE], ones[:, :], r2[:, 3, 1, :], start=False, stop=True).then_inc(pos_done, 1)

            def gather(k):
                pe.wait_ge(prep_done, k * 4 + 2)
                if not isinstance(k, int):
                    pe.wait_ge(xgl_ready, k * 2)
                for c in range(DC):
                    for t in range(TILES):
                        at = (c % 4) * SLOTS
                        last = mm(ps[:, 6 + c // 4, at:at + SLOTS], xn[:, t, c * P:(c + 1) * P], sel_p[:, t, :],
                                  start=(t == 0), stop=(t == TILES - 1))
                    if c % 4 == 3:
                        last.then_inc(gather_done, 1)

            def way_back(k):
                pe.wait_ge(prep_done, k * 4 + 4)
                pe.wait_ge(hTl_ready, k * FG + FG)
                for t in range(TILES):
                    last = pe.transpose(ps[0:SLOTS, 3, t * P:(t + 1) * P], sel_w[:, t, :], ident[:, :])
                last.then_inc(back_done, 1)

            def scatter(n):
                pe.wait_ge(back_ready, n + 1)
                pe.wait_ge(y_act, n + 1)
                pe.wait_ge(y_vec, n + 1)
                for m in range(4):
                    t, hf = m // 2, m % 2
                    if m == 3:
                        pe.wait_ge(scat_added, n * 4 + 1)
                    mm(ps[:, SCAT_BANKS[m], :], back[:, t, :], y_exp[:, hf * 512:(hf + 1) * 512], start=True, stop=True)\
                        .then_inc(scat_done, 1)

            def expert(n, parts, following=None):
                ffn(1, A_MOE, TILES * FG, FG, (x_hi, x_lo), n, following, parts)

            gather(0)
            pe.wait_ge(counts_read, 1)
            expert(0, HEAD)
            way_back(0)
            with pe.Fori(0, NE - 1) as n:
                expert(n, REST, lambda: gather(n + 1))
                expert(n + 1, HEAD)
                scatter(n)
                way_back(n + 1)
            expert(NE - 1, REST)
            scatter(NE - 1)
            pe.wait_ge(items_ready, 1)
            n_more = pe.value_load(item_i[0:1, 0, 0:1], min_val=0, max_val=7)
            with pe.If(n_more > 0):
                with pe.Fori(0, n_more) as it:
                    gather(it + NE)
                    way_back(it + NE)
                    expert(it + NE, ALL_PARTS)
                    scatter(it + NE)

        @block.vector
        def _(vec):
            own = [0]

            def after(ins):
                own[0] += 1
                ins.then_inc(vec_own, 1)
                vec.wait_ge(vec_own, own[0])

            tt, ts, stt = vec.tensor_tensor, vec.tensor_scalar, vec.scalar_tensor_tensor
            vec.memset(eps_col, EPS)
            vec.memset(one_col, 1.0)
            vec.memset(const[:, 3:4], -0.5)
            after(vec.memset(qscale_col, -0.5 * math.log(DK)))

            def norm(k, last=False, between=None):
                vec.wait_ge(ld_gain[k % 2], 16 * (k // 2 + 1))
                for t in range(TILES):
                    vec.wait_ge(rinv_ready, TILES * k + t + 1)
                    stt(xn[:, t, :], h[:, t, :], stat[:, k, 4 + t:5 + t], gain[:, k % 2, :], ALU.mult, ALU.mult)\
                        .then_inc(out_ready if last else xn_ready, 1)
                if between is not None:
                    between()
                if not last:
                    for b in range(4):
                        vec.wait_ge(xh_ready, 4 * k + b + 1)
                        cs = slice(2 * b, 2 * b + 2)
                        tt(x_lo[:, cs, :], ps[:, b, :].rearrange("p (c n) -> p c n", c=2), x_hi[:, cs, :].bitcast(F32),
                           ALU.subtract).then_inc(xl_ready, 1)

            def split_lo(i, n=None):
                vec.wait_ge(hi_done, count(n, PER, i + 1))
                tt(w_lo[i % SPLITS][:, :], ring[slots[i]][:, :], w_hi[i % SPLITS][:, :].bitcast(F32),
                   ALU.subtract).then_inc(lo_done, 1)

            def conv(i):
                vec.wait_ge(act_evac, i + 1)
                for k in range(KCONV - 1):
                    for c in (2 * i, 2 * i + 1):
                        w = colt[:, k * CONV_C + c:k * CONV_C + c + 1]
                        ins = stt(qkvT[:, c, :], conv_in[:, c, k:k + SEQ], w, qkvT[:, c, :], ALU.mult, ALU.add)
                    if k < KCONV - 2:
                        after(ins)
                ins.then_inc(conv_done, 1)

            for t in range(TILES):
                vec.wait_ge(ld_x[t], 16)
            norm(0, between=lambda: split_lo(0))
            split_lo(1)
            vec.wait_ge(bah_ready, 1)
            tt(ba_lo[:, :, :], w_ba[:, :, :], ba_hi[:, :, :].bitcast(F32), ALU.subtract).then_inc(bal_ready, 1)
            split_lo(2)
            vec.wait_ge(rows_done, 1)
            vec.tensor_copy(colt[:, 0:KCONV * CONV_C + 1], ps[:, 6, 0:KCONV * CONV_C + 1]).then_inc(colt_ready, 1)
            vec.wait_ge(ba_done, 1)
            vec.tensor_copy(ba_T, ps[0:2 * H, 7, 0:SEQ]).then_inc(baT_ready, 1)
            vec.wait_ge(ba_done, 2)
            vec.tensor_copy(ba[:, :, :], ps[:, 7, 0:2 * U].rearrange("p (t n) -> p t n", t=TILES)).then_inc(ba_sb, 1)
            vec.wait_ge(ba_sb, 1)
            vec.wait_ge(ld_small, 32)
            after(tt(small[:, 14], ba[:, :, H:2 * H], small[:, 0, 0, :].unsqueeze(1).to_broadcast([P, TILES, H]), ALU.add))
            stt(small[:, 4], small[:, 14], -1.0, small[:, 14], ALU.mult, ALU.max).then_inc(gb_vec, 1)
            vec.wait_ge(gb_act, 1)
            after(ts(small[:, 1], small[:, 1], 1.0, None, ALU.add))
            after(vec.reciprocal(small[:, 3], small[:, 1]))
            vec.wait_ge(gb_act, 3)
            after(stt(small[:, 15], small[:, 14], 0.0, small[:, 6], ALU.max, ALU.add))
            stt(small[:, 7], small[:, 15], -1.0, small[:, 2, 0, :].unsqueeze(1).to_broadcast([P, TILES, H]),
                ALU.mult, ALU.mult).then_inc(g_ready, 1)
            vec.wait_ge(wsT_done, 1)
            vec.tensor_copy(wsT[:, :, :].rearrange("p g n -> p (g n)"), two(4)).then_inc(wsT_ready, 1)


            for i in range(3):
                conv(i)
                split_lo(i + SPLITS)
            vec.wait_ge(gc_done, 1)
            after(vec.tensor_copy(small[:, 8:10].rearrange("p a t h -> p (a t h)"), ps[:, 6, 0:2 * U]))
            tt(small[:, 11], small[:, 9], small[:, 8], ALU.subtract).then_inc(gc_sb, 1)
            for i in range(3, 6):
                conv(i)
                split_lo(i + SPLITS)
                if i == 3:
                    vec.wait_ge(row_copied, 1)
                    for u in range(U):
                        hd, t = u // TILES, u % TILES
                        ts(gam[:, u, :], exp_row[:, hd, t, :], small[:, 8, t, hd:hd + 1], 0.0,
                           ALU.subtract, ALU.min).then_inc(gam_arg, 1)
            vec.wait_ge(rn_ready, 1)
            after(tt(qkvT[:, H:2 * H, :], qkvT[:, H:2 * H, :], rn[:, H:2 * H, :], ALU.mult))
            vec.wait_ge(row_done, 2)
            tt(kbT[:, :, :].rearrange("p a b -> p (a b)"), qkvT[:, H:2 * H, :].rearrange("p a b -> p (a b)"), two(6),
               ALU.mult).then_inc(kb_ready, 1)
            vec.wait_ge(gam_exp, 1)
            after(tt(gam[:, :, :], gam[:, :, :], tri_blk[:, :].unsqueeze(1).to_broadcast([P, U, P]), ALU.mult))
            vec.wait_ge(rn_ready, 2)
            tt(qkvT[:, 0:H, :], qkvT[:, 0:H, :], rn[:, 0:H, :], ALU.mult).then_inc(kb_ready, 1)
            split_lo(9)
            vec.wait_ge(gcols_act, 1)
            tt(small[:, 13], small[:, 3], small[:, 10], ALU.mult).then_inc(kbe_scale, 1)
            vec.wait_ge(kk_done, 1)
            flat_g = gam[:, :, :].rearrange("p u n -> p (u n)")
            tt(lower[:, :, :].rearrange("p u n -> p (u n)"), two(0), flat_g, ALU.mult).then_inc(lt_ready, 1)
            vec.wait_ge(lt_ready, 1)
            vec.wait_ge(kk_done, 2)
            tt(flat_g, two(2), flat_g, ALU.mult).then_inc(attn_ready, 1)
            vec.wait_ge(exp_row_ready, 1)
            tt(qkvT[:, 0:H, :].rearrange("p a b -> p (a b)"), qkvT[:, 0:H, :].rearrange("p a b -> p (a b)"),
               exp_row[:, :, :, :].rearrange("p h t n -> p (h t n)"), ALU.mult).then_inc(qd_ready, 1)
            vec.wait_ge(turn_done, 2)
            for u in range(U):
                hd, t = u // TILES, u % TILES
                ts(vb[:, u, :], two(6)[:, u * P:(u + 1) * P], small[:, 3, t, hd:hd + 1], None, ALU.mult).then_inc(vb_ready, 1)

            def ln_stats():
                vec.wait_ge(act_evac, 10)
                for t in range(TILES):
                    after(vec.bn_stats(bn[:, t, :], v_nat[:, t, :]))
                vec.bn_aggr(mv[:, 0, :], bn[:, 0, :])
                vec.bn_aggr(mv[:, 1, :], bn[:, 1, :]).then_inc(ln_var, 1)

            def layernorm():
                vec.wait_ge(ln_rstd, 1)
                vec.wait_ge(ld_lng, 32)
                for t in range(TILES):
                    after(ts(v_nat[:, t, :], v_nat[:, t, :], mv[:, t, 0:1], stat_ln[:, 1, t:t + 1], ALU.subtract, ALU.mult))
                    after(tt(v_nat[:, t, :], v_nat[:, t, :], ln_g, ALU.mult))
                    tt(v_nat[:, t, :], v_nat[:, t, :], ln_b, ALU.add).then_inc(v_ready, 1)

            def gate_out():
                vec.wait_ge(mix_done, 1)
                vec.wait_ge(ld_bias, 32)
                tmp = v_nat[:, :, :].rearrange("p t n -> p (t n)")
                after(tt(tmp.rearrange("p (c t n) -> p c t n", c=G // 2, t=TILES),
                         two(4).rearrange("p (c t n) -> p c t n", c=G // 2, t=TILES),
                         sgu_bias[:, :, :].unsqueeze(2).to_broadcast([P, G // 2, TILES, P]), ALU.add))
                y = yT[:, 0:4, :].rearrange("p a b -> p (a b)")
                tt(y, tmp, y, ALU.mult).then_inc(ya_ready, 1)

            def units4(t):
                return t.unsqueeze(1).to_broadcast([P, 4, P])

            for k in range(LEVELS):
                for hf in range(2):
                    us = slice(4 * hf, 4 * hf + 4)
                    vec.wait_ge(t_done, 2 * k + hf + 1)
                    tt(inv_t[:, us, :], ps[:, hf, :].rearrange("p (u n) -> p u n", u=4), units4(level[:, k, :]),
                       ALU.mult).then_inc(t_ready, 1)
                for hf in range(2):
                    us = slice(4 * hf, 4 * hf + 4)
                    if k == 0:
                        vec.wait_ge(t_ready, hf + 1)
                        tt(inv_x[:, us, :], units4(ident[:, :]), inv_t[:, us, :], ALU.subtract).then_inc(x_ready, 1)
                    elif k < LEVELS - 1:
                        vec.wait_ge(x_done, 2 * (k - 1) + hf + 1)
                        tt(inv_x[:, us, :], inv_x[:, us, :], ps[:, 6 + hf, :].rearrange("p (u n) -> p u n", u=4),
                           ALU.subtract).then_inc(x_ready, 1)
                    vec.wait_ge(xt_done, 2 * k + hf + 1)
                    tt(inv_xt[:, us, :], inv_xt[:, us, :] if k else units4(ident[:, :]),
                       ps[:, 2 + hf, :].rearrange("p (u n) -> p u n", u=4), ALU.subtract).then_inc(xt_ready, 1)
                if k == 0:
                    split_lo(10)
                if k == 2:
                    split_lo(11)
                if k == 3:
                    ln_stats()
                if k == 4:
                    layernorm()
            split_lo(12)
            split_lo(13)
            vec.wait_ge(sol_done, 2)
            for c in range(NCH):
                t, p0 = c // 2, (c % 2) * CH
                rows = slice(p0, p0 + CH)
                u4 = u_sol.rearrange("p (h t) n -> p t h n", t=TILES)[rows, t]
                vn = v_new[rows, t, :].rearrange("p (h n) -> p h n", h=H)
                if c == 0:
                    vec.tensor_copy(vn, two(6).rearrange("p (h t n) -> p t h n", t=TILES, h=H)[rows, t]).then_inc(vnew_ready, 1)
                    vec.tensor_copy(u_sol.rearrange("p u n -> p (u n)"), two(6)).then_inc(sol_u, 1)
                    vec.wait_ge(sol_u, 1)
                else:
                    vec.wait_ge(ws_done, c)
                    tt(vn, u4, ps[rows, 6, :].rearrange("p (h n) -> p h n", h=H), ALU.subtract).then_inc(vnew_ready, 1)
                if c < NCH - 1:
                    vec.wait_ge(st_done, c + 1)
                    if c == 0:
                        vec.tensor_copy(state[:, :, :].rearrange("p h n -> p (h n)"), ps[:, 2, :]).then_inc(st_ready, 1)
                    else:
                        vec.wait_ge(o_done, c + 1)
                        for hd in range(H):
                            ins = stt(state[:, hd, :], state[:, hd, :], exp_row[:, hd, t, p0 + CH - 1:p0 + CH],
                                      ps[:, 2, hd * P:(hd + 1) * P], ALU.mult, ALU.add)
                        ins.then_inc(st_ready, 1)
                if c == 0:
                    gate_out()
                if c == 1:
                    vec.wait_ge(yh_ready, 1)
                    tt(x_lo[:, 0:4, :], yT[:, 0:4, :], x_hi[:, 0:4, :].bitcast(F32), ALU.subtract).then_inc(yl_ready, 1)
                if c == 2:
                    split_lo(14)
            vec.wait_ge(gate_ready, 1)
            for b in range(2):
                hs = slice(2 * b, 2 * b + 2)
                vec.wait_ge(on_ready, b + 1)
                after(stt(oT[:, hs, :], oT[:, hs, :], colt[:, KCONV * CONV_C:KCONV * CONV_C + 1],
                          rn[:, H + 2 * b:H + 2 * b + 2, :], ALU.mult, ALU.mult))
                y = yT[:, 4 + 2 * b:6 + 2 * b, :]
                tt(y, oT[:, hs, :], y, ALU.mult).then_inc(yb_ready, 1)
            for b in range(2):
                vec.wait_ge(yh_ready, b + 2)
                ys = slice(4 + 2 * b, 6 + 2 * b)
                tt(x_lo[:, ys, :], yT[:, ys, :], x_hi[:, ys, :].bitcast(F32), ALU.subtract).then_inc(yl_ready, 1)

            def add_banks(k, banks, last_piece):
                for m in range(4):
                    t, hf = m // 2, m % 2
                    if m == 0:
                        vec.wait_ge(tile_summed, k + 1)
                    if m == 2:
                        used(vec, last_piece)
                    cs = slice(hf * 512, (hf + 1) * 512)
                    ins = tt(h[:, t, cs], h[:, t, cs], ps[:, banks[m], :], ALU.add)
                    if hf:
                        ins.then_inc(h_ready, 1)

            for i in (15, 16, 17):
                split_lo(i)
            add_banks(0, OUT_BANKS, A_FFN - 1)
            norm(1)
            split_lo(18)

            def ffn(tiles, first, unit0, group0, ahead, n=None, parts=ALL_PARTS, extra={}):
                def multiply(g):
                    for t in range(tiles):
                        bank = 4 + (tiles * g + t) % (tiles + 1)
                        vec.wait_ge(silu_done, count(n, FG, unit0 + tiles * g + t + 1))
                        if t == 0 and g >= 2:
                            vec.wait_ge(hT_done, count(n, FG, group0 + g - 1))
                        tt(h_act[:, g % 2, t, :], silu_s[:, t, :], ps[:, bank, CW:2 * CW], ALU.mult).then_inc(act_ready, 1)

                def turned(g):
                    vec.wait_ge(hTh_ready, count(n, FG, group0 + g + 1))
                    turned_h = ps[:, 7 if tiles == 2 else 3, 0:2 * tiles * P].rearrange("p (j n) -> p j n", j=2)
                    tt(hT_lo[:, g % 2, :, 0:tiles * P], turned_h,
                       hT_hi[:, g % 2, :, 0:tiles * P].bitcast(F32), ALU.subtract).then_inc(hTl_ready, 1)

                for p in parts:
                    kind, g, half = ITEM[p]
                    if kind == "up" and half == 1:
                        multiply(g)
                    if kind == "up" and half == 0 and g >= 1:
                        turned(g - 1)
                    if p == PER - 2:
                        turned(FG - 1)
                    if p in extra:
                        extra[p]()
                    if p + SPLITS < PER + ahead:
                        split_lo(first + p + SPLITS, n)

            ffn(TILES, A_FFN, 0, 0, SPLITS - 1)
            add_banks(1, range(4), A_QKV - 1)
            norm(2)
            for i in range(A_QKV + SPLITS - 1, A_QKV + N_QK + SPLITS):
                split_lo(i)

            def softplus(i):
                vec.wait_ge(log_ready, i + 1)
                if i >= 2:
                    vec.wait_ge(after_done, i - 1)
                if i >= 2:
                    vec.wait_ge(att_exp, i - 1)
                stt(sp_m[:, i % 2], ps[:, i % 2, 0:NZ], 0.0, lg[:, i % 2], ALU.max, ALU.add).then_inc(sp_ready, 1)
                stt(w_log[:, i % 2], ps[:, i % 2, 0:NZ], 0.0, lg[:, i % 2], ALU.min, ALU.subtract).then_inc(w_ready, 1)

            def log_att(i):
                vec.wait_ge(after_done, i + 1)
                vec.wait_ge(w_ready, i + 1)
                tt(w_log[:, i % 2], w_log[:, i % 2], ps[:, 3 + i % 3, 0:NZ], ALU.add).then_inc(la_ready, 1)

            def head_out(pr):
                vec.wait_ge(oh_hi, pr + 1)
                tt(x_lo[:, pr, :], ps[:, 6 + pr % 2, 0:SEQ], x_hi[:, pr, :].bitcast(F32), ALU.subtract).then_inc(oh_ready, 1)

            for i in range(SB_H + 2):
                if i < SB_H:
                    softplus(i)
                if 1 <= i <= SB_H:
                    log_att(i - 1)
                if 1 <= i <= N_QKV - N_QK:
                    split_lo(A_QKV + N_QK + i - 1 + SPLITS)
                if i >= 5 and i % 2 == 1:
                    head_out((i - 5) // 2)
            head_out(SB_H // 2 - 1)
            vec.wait_ge(wrh_ready, 1)
            tt(wr_lo[:, :, :], w_router[:, :, :], wr_hi[:, :, :].bitcast(F32), ALU.subtract).then_inc(wrl_ready, 1)
            for i in range(A_MOE - 1, A_MOE + 2):
                split_lo(i)
            add_banks(2, ATT_OUT_BANKS, A_MOE - 1)
            norm(3)

            vec.wait_ge(lgt_done, 1)
            vec.tensor_copy(logits_T, ps[0:NE, 6, 0:SEQ]).then_inc(lgT_ready, 1)
            vec.wait_ge(lgt_done, 2)
            after(vec.tensor_copy(logits[:, :, :].rearrange("p t e -> p (t e)"), ps[:, 6, 0:TILES * NE]))
            TE = TILES * NE
            lgf = logits[:, :, :]
            other = lgf.unsqueeze(2).to_broadcast([P, TILES, NE, NE])
            mine = lgf.rearrange("p t e -> p (t e)").unsqueeze(2).to_broadcast([P, TE, NE])

            def four(a):
                return a.rearrange("p (t e) f -> p t e f", t=TILES)

            mine4 = lgf.unsqueeze(3).to_broadcast([P, TILES, NE, NE])
            tt(four(rt[:, 0]), other, mine4, ALU.is_gt)
            after(tt(four(rt[:, 1]), other, mine4, ALU.is_equal))
            e_of = iota[:, 0:NE].unsqueeze(2).to_broadcast([P, NE, NE])
            f_of = iota[:, 0:NE].unsqueeze(1).to_broadcast([P, NE, NE])
            tt(rt[:, 2, 0:NE, :], f_of, e_of, ALU.is_lt)
            after(tt(rt[:, 2, NE:TE, :], f_of, e_of, ALU.is_lt))
            after(tt(rt[:, 1], rt[:, 1], rt[:, 2], ALU.mult))
            after(tt(rt[:, 0], rt[:, 0], rt[:, 1], ALU.add))
            after(vec.tensor_reduce(r2[:, 0].rearrange("p t e -> p (t e)"), rt[:, 0], AX.X, ALU.add))
            ts(r2[:, 1], r2[:, 0], 0.0, None, ALU.is_equal)
            after(ts(r2[:, 2], r2[:, 0], 1.0, None, ALU.is_equal))
            tt(r2[:, 3], r2[:, 1], r2[:, 2], ALU.add).then_inc(sel_ready, 1)
            tt(r2[:, 4], r2[:, 1], lgf, ALU.mult)
            after(tt(r2[:, 5], r2[:, 2], lgf, ALU.mult))
            after(tt(r2[:, 4], r2[:, 5], r2[:, 4], ALU.subtract))
            vec.tensor_reduce(r_small[:, 0], r2[:, 4], AX.X, ALU.add).then_inc(r_d, 1)
            vec.wait_ge(sel_ready, 1)
            vec.wait_ge(pos_done, 1)
            place = ps[:, 7, 0:2 * NE].rearrange("p (t e) -> p t e", t=TILES)
            for b in range(NB):
                ks = slice(b * NE, (b + 1) * NE)
                ts(table[:, 0, :, ks], place, float(-SLOTS * b), None, ALU.add)
                last = vec.tensor_copy(table[:, 1, :, ks], r2[:, 3])
            after(last)
            vec.tensor_copy(col6[:, 0:2], table[:, 0:2, :, 0:1]).then_inc(prep_col, 1)
            vec.wait_ge(prep_col, 1)

            def places():
                for t in range(TILES):
                    ts(sel_p[:, t, :], iota[:, 0:SLOTS], col6[:, 0, t], col6[:, 1, t], ALU.is_equal, ALU.mult)\
                        .then_inc(prep_done, 1)

            def places_gated():
                for t in range(TILES):
                    ts(sel_w[:, t, :], iota[:, 0:SLOTS], col6[:, 0, t], col6[:, 2, t], ALU.is_equal, ALU.mult)\
                        .then_inc(prep_done, 1)

            places()
            vec.wait_ge(pos_done, 2)
            vec.tensor_copy(counts[0:1, :], ps[0:1, 5, 0:NE]).then_inc(counts_read, 1)
            vec.wait_ge(r_exp, 1)
            after(ts(r_small[:, 2], r_small[:, 1], 1.0, None, ALU.add))
            after(vec.reciprocal(r_small[:, 3], r_small[:, 2]))
            after(tt(r_small[:, 4], r_small[:, 3], r_small[:, 1], ALU.mult))
            for t in range(TILES):
                after(ts(r2[:, 6, t], r2[:, 1, t], r_small[:, 3, t:t + 1], None, ALU.mult))
                after(stt(r2[:, 7, t], r2[:, 2, t], r_small[:, 4, t:t + 1], r2[:, 6, t], ALU.mult, ALU.add))
            for b in range(NB):
                last = vec.tensor_copy(table[:, 2, :, b * NE:(b + 1) * NE], r2[:, 7])
            after(last)
            after(vec.tensor_copy(col6[:, 2:3], table[:, 2:3, :, 0:1]))
            places_gated()
            split_lo(A_MOE + 2)

            def list_items():
                for b in range(1, NB):
                    after(ts(li[0:1, 0, (b - 1) * NE:b * NE], counts[0:1, :], float(SLOTS * b), None, ALU.is_gt))
                after(vec.tensor_tensor_scan(li[0:1, 1, :], ones[0:1, 0:NK - NE], li[0:1, 0, :], 0.0, ALU.mult, ALU.add))
                after(tt(li[0:1, 2, :], li[0:1, 0, :], iota[0:1, NE:NK], ALU.mult))
                after(tt(li3[0:1], li[0:1, 1, :].unsqueeze(1).to_broadcast([1, 8, NK - NE]),
                         iota[0:1, 1:9].unsqueeze(2).to_broadcast([1, 8, NK - NE]), ALU.is_equal))
                after(tt(li3[0:1], li3[0:1], li[0:1, 2, :].unsqueeze(1).to_broadcast([1, 8, NK - NE]), ALU.mult))
                after(vec.tensor_reduce(item_f[0:1, 1, :], li3[0:1], AX.X, ALU.add))
                after(ts(item_f[0:1, 2, :], item_f[0:1, 1, :], -float(NE), 0.0, ALU.add, ALU.max))
                after(vec.tensor_copy(item_f[0:1, 0, :], li[0:1, 1, NK - NE - 1:NK - NE].to_broadcast([1, 8])))
                vec.tensor_copy(item_i[:, :, :], item_f).then_inc(items_ready, 1)

            def prep(n, k):
                vec.tensor_copy(col6[:, :, :, :], table[:, :, :, bass.ds(k, 1)]).then_inc(prep_col, 1)
                vec.wait_ge(prep_col, n + 1)
                vec.wait_ge(back_done, n)
                places()
                places_gated()

            def evac_xg(k):
                for b in range(2):
                    vec.wait_ge(xgh_ready, k * 2 + (b + 1))
                    cs = slice(4 * b, 4 * b + 4)
                    tt(x_lo[:, cs, 0:SLOTS], ps[:, 6 + b, :].rearrange("p (c n) -> p c n", c=4), x_hi[:, cs, 0:SLOTS].bitcast(F32),
                       ALU.subtract).then_inc(xgl_ready, 1)

            def evac_back(n):
                vec.wait_ge(back_done, n + 1)
                vec.tensor_copy(back[:, :, :].rearrange("p t n -> p (t n)"), ps[0:SLOTS, 3, 0:SEQ]).then_inc(back_ready, 1)

            def evac_y(n):
                used(vec, A_MOE + PER - 1, n)
                vec.tensor_copy(y_exp[:, 0:512], ps[0:SLOTS, 0, :]).then_inc(y_vec, 1)

            def add_item(n, parts=range(4)):
                for m in parts:
                    t, hf = m // 2, m % 2
                    cs = slice(hf * 512, (hf + 1) * 512)
                    vec.wait_ge(scat_done, n * 4 + (m + 1))
                    tt(h[:, t, cs], h[:, t, cs], ps[:, SCAT_BANKS[m], :], ALU.add).then_inc(scat_added, 1)

            def expert(n, ahead, parts, add_last=None):
                def before_end():
                    if ahead:
                        evac_xg(n + 1)
                    evac_y(n)
                extra = {PER - 1: before_end}
                if add_last is not None:
                    extra[1] = add_last
                ffn(1, A_MOE, TILES * FG, FG, ahead, n, parts, extra)

            evac_xg(0)
            expert(0, SPLITS, HEAD, lambda: evac_back(0))
            with vec.Fori(0, NE - 1) as n:
                prep(n + 1, n + 1)
                expert(n, SPLITS, REST)

                def last_item():
                    add_item(n)
                    evac_back(n + 1)
                expert(n + 1, SPLITS, HEAD, last_item)
            list_items()
            expert(NE - 1, 0, REST)
            add_item(NE - 1)
            vec.wait_ge(items_ready, 1)
            n_more = vec.value_load(item_i[0:1, 0, 0:1], min_val=0, max_val=7)
            with vec.If(n_more > 0):
                with vec.Fori(0, n_more) as it:
                    k = vec.value_load(item_i[0:1, 1, bass.ds(it, 1)], min_val=0, max_val=NK - 1)
                    prep(it + NE, k)
                    for p in range(SPLITS):
                        split_lo(A_MOE + p, it + NE)
                    evac_xg(it + NE)
                    evac_back(it + NE)
                    expert(it + NE, 0, ALL_PARTS)
                    add_item(it + NE)
            vec.wait_ge(items_ready, 1)
            vec.drain().then_inc(h_ready, TILES)
            norm(4, True)


_INS = ['x', 'e_norm1', 'e_w_in', 'e_sgu_ln_g', 'e_sgu_ln_b', 'e_sgu_w', 'e_sgu_b', 'e_conv_w', 'e_a_log',
        'e_dt_bias', 'e_o_norm', 'e_w_out', 'e_norm2', 'e_ffn_w1', 'e_ffn_w3', 'e_ffn_w2', 'o_norm1', 'o_w_qkv',
        'o_w_out', 'o_norm2', 'o_router', 'o_moe_w1', 'o_moe_w3', 'o_moe_w2', 'final_norm']
_OUTS = [((1, 256, 1024), 'float32')]


def kernel(**inputs):
    import numpy as _np
    import concourse.bacc as _bacc
    from concourse import mybir as _mybir
    from concourse.bass_utils import run_bass_kernel_spmd as _run

    nc = _bacc.Bacc("TRN2", target_bir_lowering=False, num_devices=1)
    arrays, args = {}, []
    for name in _INS:
        a = _np.ascontiguousarray(inputs[name])
        arrays[f"in_{name}_dram"] = a
        args.append(nc.dram_tensor(f"in_{name}_dram", a.shape, _mybir.dt.from_np(a.dtype), kind="ExternalInput").ap())
    for i, (shape, dtype) in enumerate(_OUTS):
        dt = _mybir.dt.from_np(_np.dtype(dtype))
        args.append(nc.dram_tensor(f"out_{i}_dram", shape, dt, kind="ExternalOutput").ap())
    trunk(nc, *args)
    r = _run(nc, [arrays], core_ids=[0])
    got = tuple(r.results[0][f"out_{i}_dram"] for i in range(len(_OUTS)))
    return got[0]
```
